# Optimizing a Trainium2 kernel written in Bass

```python
import jax, jax.numpy as jnp
from jax import lax
import numpy as np

D_MODEL = 1024
BATCH = 1
SEQ = 256
DEPTH = 2

CHUNK = 64
D_MIX = D_MODEL
D_SSM = D_MIX // 2
SSM_HEAD_DIM = 64
N_SSM_HEADS = D_SSM // SSM_HEAD_DIM
SSM_GROUPS = 2
D_STATE = 128
CONV_WIDTH = 4
CONV_DIM = D_SSM + 2 * SSM_GROUPS * D_STATE
D_ATT = D_MIX - D_SSM
ATT_HEAD_DIM = 64
N_ATT_HEADS = D_ATT // ATT_HEAD_DIM
N_KV_HEADS = 2
WINDOW = 128
WINDOW_CHUNKS = WINDOW // CHUNK
ROPE_THETA = 10000.0
D_FF = 2816
FFN_RES_WEIGHT = 0.5
N_MOD = 9
EPS = 1e-6
D_IN_PROJ = D_SSM + CONV_DIM + N_SSM_HEADS + D_ATT + 2 * N_KV_HEADS * ATT_HEAD_DIM
IN_SPLITS = [int(v) for v in np.cumsum([D_SSM, CONV_DIM, N_SSM_HEADS, D_ATT, N_KV_HEADS * ATT_HEAD_DIM])]

kernel_name = "hymba_ssd_swa_sink_macaron_adaln"

def rms_norm(x, g):
    xf = x.astype(jnp.float32)
    y = xf * lax.rsqrt(jnp.mean(xf * xf, axis=-1, keepdims=True) + EPS)
    return (y * g.astype(jnp.float32)).astype(x.dtype)

def modulate(x, g, shift, scale):
    return rms_norm(x, g) * (1 + scale[:, None, :]) + shift[:, None, :]

def swiglu(h, w_gate, w_up, w_down):
    return (jax.nn.silu(h @ w_gate) * (h @ w_up)) @ w_down

def rope(x, pos):
    half = x.shape[-1] // 2
    inv_freq = ROPE_THETA ** (-jnp.arange(half, dtype=jnp.float32) / half)
    ang = pos.astype(jnp.float32)[:, None] * inv_freq[None, :]
    cos = jnp.cos(ang)[None, :, None, :]
    sin = jnp.sin(ang)[None, :, None, :]
    xf = x.astype(jnp.float32)
    x1, x2 = xf[..., :half], xf[..., half:]
    return jnp.concatenate([x1 * cos - x2 * sin, x2 * cos + x1 * sin], axis=-1).astype(x.dtype)

def causal_dwconv(x, w, b):
    C = x.shape[-1]
    out = lax.conv_general_dilated(
        x, w[:, None, :].astype(x.dtype), window_strides=(1,), padding=[(CONV_WIDTH - 1, 0)],
        dimension_numbers=("NWC", "WIO", "NWC"), feature_group_count=C)
    return out + b

def segsum(x):
    Q = x.shape[-1]
    strict = jnp.tril(jnp.ones((Q, Q), dtype=bool), -1)
    lower = jnp.tril(jnp.ones((Q, Q), dtype=bool), 0)
    xr = jnp.where(strict, x[..., :, None], 0.0)
    cs = jnp.cumsum(xr, axis=-2)
    return jnp.where(lower, cs, -jnp.inf)

def ssd_chunked(xs, dt, a, bm, cm):
    Bsz, L, H, P = xs.shape
    N = bm.shape[-1]
    nC = L // CHUNK
    xc = (xs * dt[..., None]).reshape(Bsz, nC, CHUNK, H, P)
    bc = bm.reshape(Bsz, nC, CHUNK, H, N)
    cc = cm.reshape(Bsz, nC, CHUNK, H, N)
    adt = (dt * a).reshape(Bsz, nC, CHUNK, H).transpose(0, 3, 1, 2)
    a_cs = jnp.cumsum(adt, axis=-1)
    lmat = jnp.exp(segsum(adt))
    y_diag = jnp.einsum("bclhn,bcshn,bhcls,bcshp->bclhp", cc, bc, lmat, xc)
    decay_states = jnp.exp(a_cs[..., -1:] - a_cs)
    states = jnp.einsum("bclhn,bhcl,bclhp->bchpn", bc, decay_states, xc)
    chunk_decay = jnp.exp(a_cs[..., -1])

    def step(h, inp):
        s, d = inp
        return d[..., None, None] * h + s, h

    h0 = jnp.zeros((Bsz, H, P, N), jnp.float32)
    _, prev = lax.scan(step, h0, (states.transpose(1, 0, 2, 3, 4), chunk_decay.transpose(2, 0, 1)))
    prev = prev.transpose(1, 0, 2, 3, 4)
    y_off = jnp.einsum("bclhn,bchpn,bhcl->bclhp", cc, prev, jnp.exp(a_cs))
    return (y_diag + y_off).reshape(Bsz, L, H, P)

def shift_chunks(t, s):
    if s == 0:
        return t
    nC = t.shape[1]
    pad = [(0, 0), (s, 0)] + [(0, 0)] * (t.ndim - 2)
    return jnp.pad(t, pad)[:, :nC]

def swa_sink_attention(q, k, v, sinks, pos):
    Bsz, L = q.shape[:2]
    nC = L // CHUNK
    R = N_ATT_HEADS // N_KV_HEADS
    q = rope(q.reshape(Bsz, L, N_ATT_HEADS, ATT_HEAD_DIM), pos)
    k = rope(k.reshape(Bsz, L, N_KV_HEADS, ATT_HEAD_DIM), pos)
    v = v.reshape(Bsz, L, N_KV_HEADS, ATT_HEAD_DIM)
    qb = q.reshape(Bsz, nC, CHUNK, N_KV_HEADS, R, ATT_HEAD_DIM)
    kb = k.reshape(Bsz, nC, CHUNK, N_KV_HEADS, ATT_HEAD_DIM)
    vb = v.reshape(Bsz, nC, CHUNK, N_KV_HEADS, ATT_HEAD_DIM)
    shifts = list(range(WINDOW_CHUNKS - 1, -1, -1))
    kw = jnp.concatenate([shift_chunks(kb, s) for s in shifts], axis=2)
    vw = jnp.concatenate([shift_chunks(vb, s) for s in shifts], axis=2)
    key_shift = jnp.asarray(np.repeat(np.array(shifts, dtype=np.int32), CHUNK))
    valid = jnp.arange(nC)[:, None] >= key_shift[None, :]
    scores = jnp.einsum("bcqgrd,bckgd->bgrcqk", qb, kw).astype(jnp.float32) * (ATT_HEAD_DIM ** -0.5)
    scores = jnp.where(valid[:, None, :], scores, -jnp.inf)
    sink = sinks.astype(jnp.float32).reshape(N_KV_HEADS, R)[None, :, :, None, None, None]
    logits = jnp.concatenate([scores, jnp.broadcast_to(sink, scores.shape[:-1] + (1,))], axis=-1)
    p = jax.nn.softmax(logits, axis=-1)[..., :-1].astype(v.dtype)
    o = jnp.einsum("bgrcqk,bckgd->bcqgrd", p, vw)
    return o.reshape(Bsz, L, D_ATT)

def hybrid_mixer(h, w_in, conv_w, conv_b, dt_bias, a_log, d_skip, ssd_norm, sinks, w_out, pos):
    Bsz, L, _ = h.shape
    proj = h @ w_in
    z, xbc, dt_raw, q, k, v = jnp.split(proj, IN_SPLITS, axis=-1)
    xbc = jax.nn.silu(causal_dwconv(xbc, conv_w, conv_b))
    xs, bm, cm = jnp.split(xbc, [D_SSM, D_SSM + SSM_GROUPS * D_STATE], axis=-1)
    xs = xs.reshape(Bsz, L, N_SSM_HEADS, SSM_HEAD_DIM).astype(jnp.float32)
    rep = N_SSM_HEADS // SSM_GROUPS
    bm = jnp.repeat(bm.reshape(Bsz, L, SSM_GROUPS, D_STATE).astype(jnp.float32), rep, axis=2)
    cm = jnp.repeat(cm.reshape(Bsz, L, SSM_GROUPS, D_STATE).astype(jnp.float32), rep, axis=2)
    dt = jax.nn.softplus(dt_raw.astype(jnp.float32) + dt_bias.astype(jnp.float32))
    a = -jnp.exp(a_log.astype(jnp.float32))
    y = ssd_chunked(xs, dt, a, bm, cm) + d_skip.astype(jnp.float32)[:, None] * xs
    y = y.reshape(Bsz, L, D_SSM).astype(h.dtype)
    yg = (y * jax.nn.silu(z)).reshape(Bsz, L, SSM_GROUPS, D_SSM // SSM_GROUPS)
    y_ssd = rms_norm(yg, ssd_norm.reshape(SSM_GROUPS, D_SSM // SSM_GROUPS)).reshape(Bsz, L, D_SSM)
    y_att = swa_sink_attention(q, k, v, sinks, pos)
    return jnp.concatenate([y_ssd, y_att], axis=-1) @ w_out

def setup_inputs(seed: int = 0) -> dict:
    key = jax.random.key(seed)
    ks = jax.random.split(key, 24)
    f32 = jnp.float32

    def nrm(k, shape, scale):
        return jax.random.normal(k, shape, f32) * scale

    def gain(k, shape):
        return 1.0 + 0.1 * jax.random.normal(k, shape, f32)

    dt0 = jnp.exp(jax.random.uniform(ks[13], (DEPTH, N_SSM_HEADS), f32, np.log(1e-3), np.log(1e-1)))
    dt_bias = dt0 + jnp.log(-jnp.expm1(-dt0))
    a_log = jnp.log(jax.random.uniform(ks[14], (DEPTH, N_SSM_HEADS), f32, 1.0, 16.0))
    return {
        "x": nrm(ks[0], (BATCH, SEQ, D_MODEL), 1.0),
        "c": nrm(ks[1], (BATCH, D_MODEL), 1.0),
        "ada_w": nrm(ks[2], (DEPTH, D_MODEL, N_MOD * D_MODEL), D_MODEL ** -0.5),
        "ada_b": nrm(ks[3], (DEPTH, N_MOD * D_MODEL), 0.01),
        "ffn1_norm_pre": gain(ks[4], (DEPTH, D_MODEL)),
        "ffn1_w_gate": nrm(ks[5], (DEPTH, D_MODEL, D_FF), D_MODEL ** -0.5),
        "ffn1_w_up": nrm(ks[6], (DEPTH, D_MODEL, D_FF), D_MODEL ** -0.5),
        "ffn1_w_down": nrm(ks[7], (DEPTH, D_FF, D_MODEL), D_FF ** -0.5),
        "ffn1_norm_post": gain(ks[8], (DEPTH, D_MODEL)),
        "mix_norm_pre": gain(ks[9], (DEPTH, D_MODEL)),
        "w_in": nrm(ks[10], (DEPTH, D_MODEL, D_IN_PROJ), D_MODEL ** -0.5),
        "conv_w": nrm(ks[11], (DEPTH, CONV_WIDTH, CONV_DIM), CONV_WIDTH ** -0.5),
        "conv_b": nrm(ks[12], (DEPTH, CONV_DIM), 0.01),
        "dt_bias": dt_bias,
        "a_log": a_log,
        "d_skip": gain(ks[15], (DEPTH, N_SSM_HEADS)),
        "ssd_norm": gain(ks[16], (DEPTH, D_SSM)),
        "attn_sinks": nrm(ks[17], (DEPTH, N_ATT_HEADS), 0.5),
        "w_out": nrm(ks[18], (DEPTH, D_MIX, D_MODEL), D_MIX ** -0.5),
        "mix_norm_post": gain(ks[19], (DEPTH, D_MODEL)),
        "ffn2_norm_pre": gain(ks[20], (DEPTH, D_MODEL)),
        "ffn2_w_gate": nrm(ks[21], (DEPTH, D_MODEL, D_FF), D_MODEL ** -0.5),
        "ffn2_w_up": nrm(ks[22], (DEPTH, D_MODEL, D_FF), D_MODEL ** -0.5),
        "ffn2_w_down": nrm(ks[23], (DEPTH, D_FF, D_MODEL), D_FF ** -0.5),
        "ffn2_norm_post": gain(jax.random.fold_in(key, 99), (DEPTH, D_MODEL)),
    }

def reference(x, c, ada_w, ada_b, ffn1_norm_pre, ffn1_w_gate, ffn1_w_up, ffn1_w_down, ffn1_norm_post,
              mix_norm_pre, w_in, conv_w, conv_b, dt_bias, a_log, d_skip, ssd_norm, attn_sinks, w_out,
              mix_norm_post, ffn2_norm_pre, ffn2_w_gate, ffn2_w_up, ffn2_w_down, ffn2_norm_post):
    pos = jnp.arange(x.shape[1], dtype=jnp.int32)
    c_act = jax.nn.silu(c)
    for i in range(DEPTH):
        mod = c_act @ ada_w[i] + ada_b[i]
        sh1, sc1, g1, sh2, sc2, g2, sh3, sc3, g3 = jnp.split(mod, N_MOD, axis=-1)
        h = modulate(x, ffn1_norm_pre[i], sh1, sc1)
        y = swiglu(h, ffn1_w_gate[i], ffn1_w_up[i], ffn1_w_down[i])
        x = x + FFN_RES_WEIGHT * g1[:, None, :] * rms_norm(y, ffn1_norm_post[i])
        h = modulate(x, mix_norm_pre[i], sh2, sc2)
        y = hybrid_mixer(h, w_in[i], conv_w[i], conv_b[i], dt_bias[i], a_log[i], d_skip[i], ssd_norm[i],
                         attn_sinks[i], w_out[i], pos)
        x = x + g2[:, None, :] * rms_norm(y, mix_norm_post[i])
        h = modulate(x, ffn2_norm_pre[i], sh3, sc3)
        y = swiglu(h, ffn2_w_gate[i], ffn2_w_up[i], ffn2_w_down[i])
        x = x + FFN_RES_WEIGHT * g3[:, None, :] * rms_norm(y, ffn2_norm_post[i])
    return x


_drawn_inputs = setup_inputs


def setup_inputs(seed=0):
    import zlib

    import numpy as np

    out = dict(_drawn_inputs(seed))
    spreads = {}
    factors = {'ada_b': 2.678, 'conv_b': 8.0, 'd_skip': 4.274, 'attn_sinks': 8.0}
    for name, (base, spread) in spreads.items():
        noise = np.random.default_rng([zlib.crc32(name.encode()), seed]).standard_normal(out[name].shape)
        drawn = base * np.exp(spread * noise) if base else spread * noise
        out[name] = __import__('jax').numpy.asarray(drawn.astype(out[name].dtype))
    for name, factor in factors.items():
        out[name] = (out[name] * factor).astype(out[name].dtype)
    return out
```

```python
from contextlib import ExitStack

import numpy as np

import concourse.bass as bass
from concourse import mybir

ALU = mybir.AluOpType
ACT = mybir.ActivationFunctionType
AX_X = mybir.AxisListType.X
F32 = mybir.dt.float32
F32R = mybir.dt.float32r

P = 128
DEPTH, T, D, FF = 2, 256, 1024, 2816
CHUNK, HEAD, STATE = 64, 64, 128
SSM_H, GROUPS, D_SSM = 8, 2, 512
ATT_H, KV_H = 8, 2
CONV_W, CONV_DIM = 4, 1024
D_IN = D_SSM + CONV_DIM + SSM_H + ATT_H * HEAD + 2 * KV_H * HEAD
EPS = 1e-6
ROPE_THETA = 10000.0
TB = T // P
KC = D // P
FB = 256
FSTEPS = FF // FB
SITES = 3
ATT_SCALE = HEAD ** -0.5

COL_Z, COL_XBC = 0, D_SSM
COL_DT = COL_XBC + CONV_DIM
COL_Q = COL_DT + SSM_H
COL_KV = COL_Q + ATT_H * HEAD

PIECE = 2048
RING, STAGES = 6, 3
FFN_PIECES = 3 * FSTEPS
MIX_PIECES, MIX_PLACES = 13, 18
PLACES = 2 * FFN_PIECES + MIX_PLACES
PIECES = 2 * FFN_PIECES + MIX_PIECES
Q_MIX = FFN_PIECES
Q_FFN2 = FFN_PIECES + MIX_PLACES
assert PLACES % RING == 0 and RING % STAGES == 0 and DEPTH == 2


def is_piece(q):
    return not Q_MIX + MIX_PIECES <= q % PLACES < Q_FFN2


def number(q):
    return q if q < Q_MIX + MIX_PIECES else q - (MIX_PLACES - MIX_PIECES)


def before(q, ring):
    p = q - ring
    while not is_piece(p):
        p -= ring
    return number(p) if p >= 0 else number(p + PLACES) - PIECES


def uses(q):
    return sum(is_piece(p) for p in range(q % RING, q + 1, RING))


USES = [uses(PLACES - RING + s) for s in range(RING)]

ADA_W = 256
ADA_PIECES = 9 * D // ADA_W
ADA_RING = 2
ADA_AHEAD = 10
ADA_LOOP1, ADA_EPI, ADA_PRO = 20, 4, 2
assert ADA_AHEAD + ADA_LOOP1 + ADA_EPI + ADA_PRO == ADA_PIECES and ADA_PIECES % ADA_RING == 0

ROW_ADA = 0
ROW_PRE = [72, 80, 88]
ROW_POST = [96, 104, 112]
ROW_SSDN = 120
ROWS_A = 124
ROW_CONVB, ROW_CONVW = 0, 8
ROWS_B = 8 + 8 * CONV_W
PCOLS = ROWS_A + ROWS_B

C_IDENT, C_AFTER, C_UPTO, C_FIRST, C_SECOND, C_ONES, C_COS, C_SIN = 0, 128, 256, 384, 512, 640, 768, 896
C_WIDTH = 1024
SHIFT, SCALE, GATE = 0, 1, 2


def constants():
    c = np.zeros((P, C_WIDTH), np.float32)
    k, l = np.arange(P)[:, None], np.arange(P)[None, :]
    same = k // CHUNK == l // CHUNK
    c[:, C_IDENT:C_IDENT + P] = k == l
    c[:, C_AFTER:C_AFTER + P] = same & (k > l)
    c[:, C_UPTO:C_UPTO + P] = same & (k <= l)
    c[:, C_FIRST:C_FIRST + P] = k < CHUNK
    c[:, C_SECOND:C_SECOND + P] = k >= CHUNK
    c[:, C_ONES:C_ONES + P] = 1.0
    half = HEAD // 2
    inv_freq = np.float32(ROPE_THETA) ** (-np.arange(half, dtype=np.float32) / np.float32(half))
    ang = np.arange(T, dtype=np.float32)[:, None] * inv_freq[None, :]
    cos, sin = np.cos(ang).astype(np.float32), np.sin(ang).astype(np.float32)
    for t in range(TB):
        rows = slice(t * P, (t + 1) * P)
        c[:, C_COS + t * HEAD:C_COS + (t + 1) * HEAD] = np.concatenate([cos[rows], cos[rows]], 1)
        c[:, C_SIN + t * HEAD:C_SIN + (t + 1) * HEAD] = np.concatenate([-sin[rows], sin[rows]], 1)
    return c


VEC_STEPS = 7 + 3 * 2 * TB + 3 * 8 + 5 * 4 + 2 + 4 * TB


class Steps:

    def __init__(self, sem, per_layer):
        self.sem, self.per_layer = sem, per_layer

    def begin(self, l):
        self.l, self.n = l, 0

    def link(self, eng, ins):
        self.mark(ins)
        self.settle(eng)

    def mark(self, ins):
        ins.then_inc(self.sem, 1)
        self.n += 1

    def settle(self, eng):
        eng.wait_ge(self.sem, self.l * self.per_layer + self.n)

    def end(self):
        assert self.n == self.per_layer, (self.n, self.per_layer)


def trunk(nc, a, out):
    ctx = ExitStack()
    with ctx:
        def sb(name, shape, dt=F32):
            return ctx.enter_context(nc.sbuf_tensor(name, shape, dt))

        def sem(name):
            return ctx.enter_context(nc.semaphore(name))

        raw = sb("raw", [P, RING, PIECE])
        w_hi = sb("w_hi", [P, STAGES, PIECE], F32R)
        w_lo = sb("w_lo", [P, STAGES, PIECE], F32R)
        ada_raw = sb("ada_raw", [P, ADA_RING, KC, ADA_W])
        ada_acc = sb("ada_acc", [P, ADA_RING, ADA_W])
        x_sb = sb("x_sb", [P, TB, D])
        h_hi = sb("h_hi", [P, KC, T], F32R)
        h_lo = sb("h_lo", [P, KC, T], F32R)
        nrm = sb("nrm", [P, TB, KC, P])
        gate_rows = sb("gate_rows", [P, D])
        const = sb("const", [P, C_WIDTH])
        prow_a = sb("prow_a", [ROWS_A, DEPTH, P])
        prow_b = sb("prow_b", [ROWS_B, DEPTH, P])
        c_row = sb("c_row", [KC, P])
        pcol = sb("pcol", [P, DEPTH, PCOLS])
        c_col = sb("c_col", [P, KC])
        small = sb("small", [P, DEPTH, 4, 8])
        cur = sb("cur", [P, PCOLS])
        cur_small = sb("cur_small", [P, 4, 8])
        cur_sink = sb("cur_sink", [P, 4])
        mod = sb("mod", [P, 2 * ADA_PIECES])
        a_col = sb("a_col", [P, KC])
        g_col = sb("g_col", [P, KC])
        sq_sum = sb("sq_sum", [P, 2, TB])
        pow_in = sb("pow_in", [P, 2, TB])
        rstd = sb("rstd", [P, 2, TB])
        minus_half = sb("minus_half", [P, 4])
        zeros_r = sb("zeros_r", [P, 512], F32R)
        ffn_buf = sb("ffn_buf", [P, 1024])
        silu_sb = ffn_buf[:, 0:TB * FB].rearrange("p (t n) -> p t n", t=TB)
        prod = ffn_buf[:, TB * FB:2 * TB * FB].rearrange("p (t n) -> p t n", t=TB)
        hid_hi = sb("hid_hi", [P, 2, T], F32R)
        hid_lo = sb("hid_lo", [P, 2, T], F32R)
        w_dt = sb("w_dt", [P, KC, SSM_H])
        soft = sb("soft", [P, 8, TB * SSM_H])
        dt_sb = sb("dt_sb", [P, TB, SSM_H])
        adt = sb("adt", [P, TB, SSM_H])
        exp_a = sb("exp_a", [P, SSM_H])
        decays = sb("decays", [P, TB, 4, SSM_H])
        rope_buf = sb("rope_buf", [P, 2 * SSM_H * P])
        rope_t = rope_buf[:, 0:1024].rearrange("p (a h d) -> p a h d", a=2, d=HEAD)
        q_rot = rope_buf[:, 1024:2048].rearrange("p (t h d) -> p t h d", t=TB, d=HEAD)
        decay_l = rope_buf[:, :].rearrange("p (t h s) -> p t h s", t=TB, s=P)
        k_rot = sb("k_rot", [P, TB, KV_H, 2, HEAD])
        v_sb = sb("v_sb", [P, TB + 1, KV_H * HEAD])
        k_t = sb("k_t", [P, KV_H, 2, T])
        conv = sb("conv", [P, 8, T])
        tanh_b = sb("tanh_b", [P, 512])
        tanh_sb = tanh_b[:, :].rearrange("p (b n) -> p b n", b=2)
        b_nat = tanh_b[:, :].rearrange("p (t n) -> p t n", t=TB)
        probs = ffn_buf[:, :].rearrange("p (b i k) -> p b i k", b=2, i=4)
        z_tanh = ffn_buf[:, 0:512]
        gram = ffn_buf[:, 512:1024].rearrange("p (b l) -> p b l", b=4)
        z_silu = sb("z_silu", [P, TB, 512])
        xs_nat = sb("xs_nat", [P, TB, D_SSM])
        xs_dt = sb("xs_dt", [P, TB, D_SSM])
        probs_t = xs_dt[:, :, :].rearrange("p b (i q) -> p b i q", i=4)
        xs_dec = sb("xs_dec", [P, TB, D_SSM])
        q_t = xs_dec[:, :, :].rearrange("p b (i q) -> p (b i) q", i=2)
        state = sb("state", [P, 3, D_SSM])
        att = sb("att", [P, 4, T])
        sm = sb("sm", [P, 4, 6, 4])
        gsq = sb("gsq", [P, TB, GROUPS])
        gpow = sb("gpow", [P, TB, GROUPS])
        grstd = sb("grstd", [P, TB, GROUPS])

        bank = ctx.enter_context(nc.psum_tensor("bank", [P, 8, 512], F32))

        ident = const[:, C_IDENT:C_IDENT + P]
        after = const[:, C_AFTER:C_AFTER + P]
        upto = const[:, C_UPTO:C_UPTO + P]
        ones = const[:, C_ONES:C_ONES + P]

        def pair(b):
            return bank[:, b:b + 2, :].rearrange("p a n -> p (a n)")

        x_landed = sem("x_landed")
        const_landed = sem("const_landed")
        rows_landed = sem("rows_landed")
        small_landed = sem("small_landed")
        params_turned = sem("params_turned")
        pcol_ready = sem("pcol_ready")
        c_ready = sem("c_ready")
        half_ready = sem("half_ready")
        zeros_ready = sem("zeros_ready")
        kt_zeroed = sem("kt_zeroed")
        out_landed = sem("out_landed")
        raw_landed = [sem(f"raw_landed{s}") for s in range(RING)]
        hi_ready = sem("hi_ready")
        lo_ready = sem("lo_ready")
        stage_used = sem("stage_used")
        ada_landed = [sem(f"ada_landed{s}") for s in range(ADA_RING)]
        ada_step = sem("ada_step")
        ada_summed = sem("ada_summed")
        mod_ready = sem("mod_ready")
        cur_ready = sem("cur_ready")
        x_ready = sem("x_ready")
        x_squared = sem("x_squared")
        y_squared = sem("y_squared")
        pow_arg = sem("pow_arg")
        x_rstd = sem("x_rstd")
        y_rstd = sem("y_rstd")
        xn_ready = sem("xn_ready")
        xn_turned = sem("xn_turned")
        a_ready = sem("a_ready")
        h_full = sem("h_full")
        h_hi_ready = sem("h_hi_ready")
        h_lo_ready = sem("h_lo_ready")
        gcol_ready = sem("gcol_ready")
        diag_ready = sem("diag_ready")
        gate_spread = sem("gate_spread")
        gate_ready = sem("gate_ready")
        y_done = sem("y_done")
        y_scaled = sem("y_scaled")
        gu_done = sem("gu_done")
        silu_done = sem("silu_done")
        prod_done = sem("prod_done")
        hid_turned = sem("hid_turned")
        hid_hi_ready = sem("hid_hi_ready")
        hid_lo_ready = sem("hid_lo_ready")
        vec_step = sem("vec_step")
        dtw_landed = sem("dtw_landed")
        dt_mm = sem("dt_mm")
        dt_x = sem("dt_x")
        dt_abs = sem("dt_abs")
        dt_exp = sem("dt_exp")
        dt_one = sem("dt_one")
        dt_ln = sem("dt_ln")
        exp_a_ready = sem("exp_a_ready")
        adt_ready = sem("adt_ready")
        decay_sums = sem("decay_sums")
        decays_ready = sem("decays_ready")
        q_mm = sem("q_mm")
        kv_mm = sem("kv_mm")
        q_roped = sem("q_roped")
        k_roped = sem("k_roped")
        v_ready = sem("v_ready")
        q_turned = sem("q_turned")
        k_turned = sem("k_turned")
        q_t_ready = sem("q_t_ready")
        k_t_ready = sem("k_t_ready")
        xbc_mm = sem("xbc_mm")
        conv_ready = sem("conv_ready")
        conv_tanh = sem("conv_tanh")
        tanh_plus = sem("tanh_plus")
        xbc_ready = sem("xbc_ready")
        z_mm = sem("z_mm")
        z_tanhed = sem("z_tanhed")
        z_ready = sem("z_ready")
        scores = sem("scores")
        row_max = sem("row_max")
        exps = sem("exps")
        sink_exp = sem("sink_exp")
        probs_ready = sem("probs_ready")
        probs_turned = sem("probs_turned")
        probs_t_ready = sem("probs_t_ready")
        att_mm = sem("att_mm")
        att_ready = sem("att_ready")
        att_hi = sem("att_hi")
        att_lo = sem("att_lo")
        seg_in_ready = sem("seg_in_ready")
        seg_mm = sem("seg_mm")
        seg_exp = sem("seg_exp")
        xs_turned = sem("xs_turned")
        xs_ready = sem("xs_ready")
        xs_dt_ready = sem("xs_dt_ready")
        xs_dec_ready = sem("xs_dec_ready")
        b_turned = sem("b_turned")
        b_ready = sem("b_ready")
        gram_mm = sem("gram_mm")
        gram_ready = sem("gram_ready")
        mix_ready = sem("mix_ready")
        state_mm = sem("state_mm")
        state_ready = sem("state_ready")
        diag_mm = sem("diag_mm")
        off_mm = sem("off_mm")
        gated = sem("gated")
        g_squared = sem("g_squared")
        g_pow = sem("g_pow")
        g_rstd = sem("g_rstd")
        ssd_ready = sem("ssd_ready")
        ssd_turned = sem("ssd_turned")
        ssd_full = sem("ssd_full")
        ssd_hi = sem("ssd_hi")
        ssd_lo = sem("ssd_lo")

        block = ctx.enter_context(nc.Block())

        def at(l, per_layer, k):
            return l * per_layer + k

        def piece_done(l, q, i=None):
            return at(l, PIECES, STAGES + number(q) + 1) + (0 if i is None else i * RING)

        def wait_apart(eng, signal, value):
            value = value if isinstance(value, int) else eng.to_reg(value)
            eng.wait_ge(kt_zeroed, 1)
            eng.wait_ge(signal, value)

        def wait_block(eng, signal, l, t, q):
            if t == 0:
                eng.wait_ge(signal, at(l, 1, 1))
            else:
                eng.wait_ge(stage_used, piece_done(l, q))

        FFNS = [("ffn1", 0, 0), ("ffn2", 1, Q_FFN2)]
        LAST_PIECE = [Q_MIX - 1, Q_MIX + MIX_PIECES - 1, PLACES - 1]
        ODD, EVEN = slice(64, 128), slice(0, 64)
        WINDOWS = [[(0, 64)], [(0, 128)], [(128, 64), (64, 64)], [(128, 128)]]
        KEYS = [sum(n for _, n in w) for w in WINDOWS]
        V_OF = [0, 0, 2, 1]

        @block.sync
        def _(sp):
            def load(l, q, i, parts):
                n = before(q, RING) if i is None else number(q) - RING
                wait_apart(sp, lo_ready, at(l, PIECES, RING + n + 1) + (0 if i is None else i * RING))
                for dst, src in parts:
                    sp.dma_start(dst, src).then_inc(raw_landed[q % RING], 16)

            def slot(q, pattern, **sizes):
                return raw[:, q % RING, :].rearrange(pattern, **sizes)

            def load_gu(f, l, q, j, half, i=None):
                dst = slot(q, "p (g k n) -> p g k n", g=2, k=4)
                load(l, q, i, [(dst[:, g], a[f + w].rearrange("l (k p) n -> l p k n", p=P)
                                [l, :, 4 * half:4 * half + 4, bass.ds(j * FB, FB)])
                               for g, w in enumerate(("_w_gate", "_w_up"))])

            def load_down(f, l, q, j, i=None):
                dst = slot(q, "p (c n) -> p c n", c=2)
                src = a[f + "_w_down"].rearrange("l (j p) n -> l p j n", p=P)
                load(l, q, i, [(dst[:, c], src[l, :, bass.ds(j * 2 + c, 1), :].rearrange("p j n -> p (j n)"))
                               for c in range(2)])

            def load_ada(pos, slot_no, layer, r):
                wait_apart(sp, ada_step, (pos + 1) * KC)
                sp.dma_start(ada_raw[:, slot_no],
                             a["ada_w"].rearrange("l (k p) n -> l p k n", p=P)
                             [layer, :, :, bass.ds(r * ADA_W, ADA_W)]).then_inc(ada_landed[slot_no], 16)

            sp.dma_start(c_row[:, :], a["c"].rearrange("b (k p) -> (b k) p", p=P)).then_inc(rows_landed, 16)
            sp.dma_start(const[:, :], a["const"]).then_inc(const_landed, 16)
            for l in range(DEPTH):
                def rows(name, tile, r0):
                    src = a[name][l]
                    src = src.rearrange("w (k p) -> (w k) p", p=P) if name == "conv_w" else \
                        src.rearrange("(k p) -> k p", p=P)
                    sp.dma_start(tile[r0:r0 + src.shape[0], l, :], src).then_inc(rows_landed, 16)
                rows("ada_b", prow_a, ROW_ADA)
                for s, name in enumerate(("ffn1", "mix", "ffn2")):
                    rows(name + "_norm_pre", prow_a, ROW_PRE[s])
                    rows(name + "_norm_post", prow_a, ROW_POST[s])
                rows("ssd_norm", prow_a, ROW_SSDN)
                rows("conv_b", prow_b, ROW_CONVB)
                rows("conv_w", prow_b, ROW_CONVW)
            for r in range(ADA_RING):
                load_ada(r, r % ADA_RING, 0, r)
            for t in range(TB):
                sp.dma_start(x_sb[:, t, :], a["x"][0, t * P:(t + 1) * P, :]).then_inc(x_landed, 16)
            for n, name in enumerate(("dt_bias", "a_log", "d_skip", "attn_sinks")):
                for l in range(DEPTH):
                    sp.dma_start(small[:, l, n, :], a[name][l:l + 1, :].broadcast_to([P, 8])).then_inc(small_landed, 16)
            for r in range(ADA_RING, ADA_AHEAD):
                load_ada(r, r % ADA_RING, 0, r)

            with sp.Fori(0, DEPTH) as l:
                ada0 = l * ADA_PIECES + ADA_AHEAD
                for f, ff, q0 in FFNS:
                    load_gu(f, l, q0, 0, 0)
                    load_gu(f, l, q0 + 1, 0, 1)
                    if ff:
                        for u in range(ADA_PRO):
                            load_ada(ada0 + (ADA_LOOP1 + ADA_EPI + u), u, l, ADA_AHEAD + ADA_LOOP1 + ADA_EPI + u)
                    with sp.Fori(0, 5) as i:
                        for u in range(2):
                            q, j = q0 + 2 + 3 * u, i * 2 + (1 + u)
                            load_gu(f, l, q, j, 0, i)
                            load_gu(f, l, q + 1, j, 1, i)
                            if ff == 0:
                                load_ada(i * 4 + (ada0 + 2 * u), 0, l, i * 4 + (ADA_AHEAD + 2 * u))
                            load_down(f, l, q + 2, i * 2 + u, i)
                            if ff == 0:
                                load_ada(i * 4 + (ada0 + (2 * u + 1)), 1, l, i * 4 + (ADA_AHEAD + 2 * u + 1))
                            else:
                                load_ada(i * 2 + (ada0 + (26 + u)), u, 1 - l, i * 2 + u)
                    load_down(f, l, q0 + 32, FSTEPS - 1)
                    if ff == 0:
                        w_in = a["w_in"].rearrange("l (k p) n -> l p k n", p=P)
                        w_out = a["w_out"].rearrange("l (k p) n -> l p k n", p=P)
                        sp.wait_ge(dt_mm, at(l, 1, 1))
                        sp.dma_start(w_dt[:, :, :], w_in[l, :, :, COL_DT:COL_DT + SSM_H]).then_inc(dtw_landed, 16)

                        def load_wide(m, col, kh):
                            dst = slot(Q_MIX + m, "p (k n) -> p k n", k=4)
                            load(l, Q_MIX + m, None, [(dst[:, 2 * e:2 * e + 2],
                                 w_in[l, :, 4 * kh + 2 * e:4 * kh + 2 * e + 2, col:col + 512]) for e in range(2)])

                        def load_tall(m, col):
                            dst = slot(Q_MIX + m, "p (k n) -> p k n", k=8)
                            load(l, Q_MIX + m, None, [(dst[:, 4 * e:4 * e + 4],
                                 w_in[l, :, 4 * e:4 * e + 4, col:col + 256]) for e in range(2)])

                        load_wide(0, COL_Q, 0)
                        load_wide(1, COL_Q, 1)
                        for u in range(ADA_EPI):
                            load_ada(ada0 + (ADA_LOOP1 + u), u % ADA_RING, l, ADA_AHEAD + ADA_LOOP1 + u)
                        load_tall(2, COL_KV)
                        for m in range(4):
                            load_tall(3 + m, COL_XBC + 256 * m)
                        load_wide(7, COL_Z, 0)
                        load_wide(8, COL_Z, 1)
                        for n, k2 in enumerate((2, 3, 0, 1)):
                            dst = slot(Q_MIX + 9 + n, "p (c n) -> p c n", c=2)
                            load(l, Q_MIX + 9 + n, None, [(dst[:, c], w_out[l, :, 2 * k2 + c, :]) for c in range(2)])
            sp.wait_ge(x_ready, TB + DEPTH * SITES * TB)
            for t in range(TB):
                sp.dma_start(out[0, t * P:(t + 1) * P, :], x_sb[:, t, :]).then_inc(out_landed, 16)
            sp.wait_ge(out_landed, 16 * TB)

        @block.gpsimd
        def _(pool):
            pool.memset(minus_half[:, :], -0.5).then_inc(half_ready, 1)
            pool.memset(k_t[:, :, :, :], 0.0).then_inc(kt_zeroed, 1)
            pool.wait_ge(half_ready, 1)
            args = Steps(pow_arg, 4 * SITES)

            def power(l, which, t, squared, signal, k):
                wait_apart(pool, squared, at(l, SITES * TB, k))
                args.link(pool, pool.tensor_scalar(pow_in[:, which, t:t + 1], sq_sum[:, which, t:t + 1],
                                                   1.0 / D, EPS, ALU.mult, ALU.add))
                pool.tensor_tensor(rstd[:, which, t:t + 1], pow_in[:, which, t:t + 1], minus_half[:, 0:1],
                                   ALU.pow).then_inc(signal, 1)

            def pre(l, site):
                for t in range(TB):
                    power(l, 1, t, x_squared, x_rstd, site * TB + t + 1)

            def post(l, site):
                for t in range(TB):
                    power(l, 0, t, y_squared, y_rstd, site * TB + t + 1)

            with pool.Fori(0, DEPTH) as l:
                args.begin(l)
                pre(l, 0)
                post(l, 0)
                pre(l, 1)
                for ct in range(8):
                    wait_apart(pool, conv_tanh, at(l, 8, ct + 1))
                    pool.tensor_scalar(tanh_sb[:, ct % 2, :], tanh_sb[:, ct % 2, :], 1.0, None, ALU.add)\
                        .then_inc(tanh_plus, 1)
                    pool.wait_ge(tanh_plus, at(l, 8, ct + 1))
                    pool.tensor_tensor(conv[:, ct, :], tanh_sb[:, ct % 2, :], conv[:, ct, :], ALU.mult)\
                        .then_inc(xbc_ready, 1)
                for t in range(TB):
                    wait_apart(pool, g_squared, at(l, TB * GROUPS, GROUPS * (t + 1)))
                    pool.tensor_scalar(gpow[:, t, :], gsq[:, t, :], 1.0 / (D_SSM // GROUPS), EPS,
                                       ALU.mult, ALU.add).then_inc(g_pow, 1)
                    pool.wait_ge(g_pow, at(l, TB, t + 1))
                    pool.tensor_tensor(grstd[:, t, :], gpow[:, t, :], minus_half[:, 0:GROUPS],
                                       ALU.pow).then_inc(g_rstd, 1)
                post(l, 1)
                pre(l, 2)
                post(l, 2)
                args.end()

        @block.scalar
        def _(act):
            def hi(l, q, i=None):
                n = before(q, STAGES) if i is None else number(q) - STAGES
                act.wait_ge(raw_landed[q % RING], (l * USES[q % RING] + (uses(q) if i is None else i + uses(q))) * 32)
                act.wait_ge(stage_used, at(l, PIECES, STAGES + n + 1) + (0 if i is None else i * RING))
                nc.scalar.activation(w_hi[:, q % STAGES], raw[:, q % RING], ACT.Copy).then_inc(hi_ready, 1)

            def squares(l, site, which, t):
                if which:
                    act.wait_ge(x_ready, at(l, SITES * TB, site * TB + t + 1))
                    src, signal = x_sb[:, t, :], x_squared
                else:
                    if t == 0:
                        act.wait_ge(y_done, at(l, SITES, site + 1))
                    else:
                        act.wait_ge(stage_used, piece_done(l, LAST_PIECE[site]))
                    src, signal = pair(2 + 2 * t), y_squared
                nc.scalar.activation(nrm[:, t, :, :].rearrange("p k c -> p (k c)"), src, ACT.Square,
                                     accum_out=sq_sum[:, which, t:t + 1]).then_inc(signal, 1)

            def h_high(l, site, t, e):
                act.wait_ge(h_full, at(l, 16 * SITES, 16 * site + 4 * (2 * t + e + 1)))
                nc.scalar.activation(h_hi[:, 4 * e:4 * e + 4, t * P:(t + 1) * P],
                                     nrm[:, t, 4 * e:4 * e + 4, :], ACT.Copy).then_inc(h_hi_ready, 1)

            def gate(l, site, b):
                act.wait_ge(gate_spread, at(l, SITES, site + 1))
                nc.scalar.activation(gate_rows[:, :], pair(b), ACT.Copy).then_inc(gate_ready, 1)

            def silu(l, ff, j, t):
                act.wait_ge(gu_done, at(l, 4 * FSTEPS, 2 * FSTEPS * ff + t + 1) + j * 2)
                nc.scalar.activation(silu_sb[:, t], bank[:, t, 0:FB], ACT.Silu).then_inc(silu_done, 1)

            def hid(l, ff, j):
                act.wait_ge(hid_turned, at(l, 2 * FSTEPS, FSTEPS * ff + 1) + j)
                nc.scalar.activation(hid_hi[:, :, :], bank[:, 6, :].rearrange("p (c t) -> p c t", c=2),
                                     ACT.Copy).then_inc(hid_hi_ready, 1)

            def mixer(l):
                def dt_part():
                    act.wait_ge(cur_ready, at(l, 5, 5))
                    nc.scalar.activation(exp_a[:, :], cur_small[:, 1, :], ACT.Exp).then_inc(exp_a_ready, 1)
                    act.wait_ge(dt_abs, at(l, 1, 1))
                    nc.scalar.activation(soft[:, 3, :], soft[:, 2, :], ACT.Exp, scale=-1.0).then_inc(dt_exp, 1)
                    act.wait_ge(dt_one, at(l, 1, 1))
                    nc.scalar.activation(soft[:, 5, :], soft[:, 4, :], ACT.Ln).then_inc(dt_ln, 1)

                def decay_part():
                    act.wait_ge(decay_sums, at(l, 1, 1))
                    nc.scalar.activation(decays[:, :, :, :], bank[:, 1, 0:64].rearrange(
                        "p (t a h) -> p t a h", t=TB, a=4), ACT.Exp).then_inc(decays_ready, 1)

                def tanh(ct):
                    act.wait_ge(conv_ready, at(l, 8, ct + 1))
                    if ct >= 2:
                        act.wait_ge(xbc_ready, at(l, 8, ct - 1))
                    nc.scalar.activation(tanh_sb[:, ct % 2, :], conv[:, ct, :], ACT.Tanh).then_inc(conv_tanh, 1)

                def exp_scores(c):
                    act.wait_ge(row_max, at(l, 4, c + 1))
                    for i in range(4):
                        nc.scalar.activation(probs[:, c % 2, i, 0:KEYS[c]], bank[:, 4 + c % 2, i * P:i * P + KEYS[c]],
                                             ACT.Exp, bias=sm[:, c, 2, i:i + 1], scale=ATT_SCALE,
                                             accum_out=sm[:, c, 3, i:i + 1]).then_inc(exps, 1)
                    nc.scalar.activation(sm[:, c, 4, :], sm[:, c, 1, :], ACT.Exp).then_inc(sink_exp, 1)

                def probs_part(c):
                    act.wait_ge(probs_turned, at(l, 4, c + 1))
                    nc.scalar.activation(probs_t[0:KEYS[c], c % 2, :, :], bank[0:KEYS[c], 6 + c % 2, :].rearrange(
                        "p (i q) -> p i q", i=4), ACT.Copy).then_inc(probs_t_ready, 1)

                def att_part(c):
                    act.wait_ge(att_mm, at(l, 4, c + 1))
                    nc.scalar.activation(att[:, :, 64 * c:64 * c + 64], bank[:, 4 + c % 2, 0:256].rearrange(
                        "p (i q) -> p i q", i=4), ACT.Copy).then_inc(att_ready, 1)

                M = Q_MIX
                hi(l, M + 2)
                dt_part()
                decay_part()
                for t in range(TB):
                    wait_block(act, kv_mm, l, t, Q_MIX + 2)
                    nc.scalar.activation(v_sb[:, t, :], bank[:, 6 + t, 128:256], ACT.Copy).then_inc(v_ready, 1)
                for t, half in ((1, EVEN), (0, ODD)):
                    act.wait_ge(v_ready, at(l, TB + 2, TB))
                    nc.scalar.activation(v_sb[half, 2, :], v_sb[half, t, :], ACT.Copy).then_inc(v_ready, 1)
                hi(l, M + 3)
                hi(l, M + 4)
                for t in range(TB):
                    act.wait_ge(q_turned, at(l, TB, t + 1))
                    nc.scalar.activation(q_t[:, :, t * P:(t + 1) * P], bank[:, 4 + t, :].rearrange(
                        "p (i q) -> p i q", i=4), ACT.Copy).then_inc(q_t_ready, 1)
                act.wait_ge(k_turned, at(l, 1, 1))
                for e, half in enumerate((EVEN, ODD)):
                    nc.scalar.activation(k_t[half, :, e, :], bank[half, 6, :].rearrange("p (g q) -> p g q", g=2),
                                         ACT.Copy).then_inc(k_t_ready, 1)
                tanh(0)
                tanh(1)
                hi(l, M + 5)
                exp_scores(0)
                exp_scores(1)
                tanh(2)
                tanh(3)
                hi(l, M + 6)
                probs_part(0)
                probs_part(1)
                att_part(0)
                att_part(1)
                tanh(4)
                tanh(5)
                hi(l, M + 7)
                exp_scores(2)
                exp_scores(3)
                tanh(6)
                tanh(7)
                hi(l, M + 8)
                probs_part(2)
                probs_part(3)
                att_part(2)
                att_part(3)
                hi(l, M + 9)
                hi(l, M + 10)
                for t in range(TB):
                    wait_block(act, z_mm, l, t, Q_MIX + 8)
                    if t:
                        act.wait_ge(z_ready, at(l, TB, t))
                    nc.scalar.activation(z_tanh, bank[:, t, :], ACT.Tanh, scale=0.5).then_inc(z_tanhed, 1)
                    for hh in range(2):
                        act.wait_ge(seg_mm, at(l, 2 * TB, 2 * t + hh + 1))
                        nc.scalar.activation(decay_l[:, t, 4 * hh:4 * hh + 4, :], bank[:, 6 + hh, :].rearrange(
                            "p (h s) -> p h s", h=4), ACT.Exp).then_inc(seg_exp, 1)
                for t in range(TB):
                    act.wait_ge(xs_turned, at(l, TB, t + 1))
                    nc.scalar.activation(xs_nat[:, t, :], bank[:, 2 + t, :], ACT.Copy).then_inc(xs_ready, 1)
                act.wait_ge(b_turned, at(l, 1, 1))
                nc.scalar.activation(b_nat[:, :, :], bank[:, 4, :].rearrange("p (t n) -> p t n", t=TB),
                                     ACT.Copy).then_inc(b_ready, 1)
                nc.scalar.activation(h_hi[:, 4:8, :], att[:, :, :], ACT.Copy).then_inc(att_hi, 1)
                hi(l, M + 11)
                for t in range(TB):
                    act.wait_ge(gated, at(l, TB, t + 1))
                    for g in range(GROUPS):
                        nc.scalar.activation(nrm[:, t, 4 + 2 * g:6 + 2 * g, :].rearrange("p k c -> p (k c)"),
                                             xs_dec[:, t, 256 * g:256 * g + 256], ACT.Square,
                                             accum_out=gsq[:, t, g:g + 1]).then_inc(g_squared, 1)
                hi(l, M + 12)
                for t in range(TB):
                    act.wait_ge(ssd_full, at(l, 4 * TB, 4 * t + 4))
                    nc.scalar.activation(h_hi[:, 0:4, t * P:(t + 1) * P], nrm[:, t, 0:4, :], ACT.Copy)\
                       .then_inc(ssd_hi, 1)

            act.wait_ge(kt_zeroed, 1)
            nc.scalar.activation(zeros_r[:, :], k_t[:, :, :, :].rearrange("p g e q -> p (g e q)")[:, 0:512],
                                 ACT.Copy).then_inc(zeros_ready, 1)
            act.wait_ge(params_turned, 1)
            nc.scalar.activation(c_col[:, :], bank[:, 0, 0:KC], ACT.Silu).then_inc(c_ready, 1)

            with act.Fori(0, DEPTH) as l:
                for f, ff, q0 in FFNS:
                    site = 2 * ff
                    squares(l, site, 1, 0)
                    squares(l, site, 1, 1)
                    hi(l, q0)
                    for t in range(TB):
                        for e in range(2):
                            h_high(l, site, t, e)
                    hi(l, q0 + 1)
                    with act.Fori(0, 5) as i:
                        for u in range(2):
                            q, j = q0 + 2 + 3 * u, i * 2 + u
                            hi(l, q, i)
                            silu(l, ff, j, 0)
                            silu(l, ff, j, 1)
                            hi(l, q + 1, i)
                            hid(l, ff, j)
                            hi(l, q + 2, i)
                    hi(l, q0 + 32)
                    silu(l, ff, FSTEPS - 1, 0)
                    silu(l, ff, FSTEPS - 1, 1)
                    hid(l, ff, FSTEPS - 1)
                    gate(l, site, 0)
                    if ff == 0:
                        hi(l, Q_MIX)
                        hi(l, Q_MIX + 1)
                    squares(l, site, 0, 0)
                    squares(l, site, 0, 1)
                    if ff == 0:
                        squares(l, 1, 1, 0)
                        squares(l, 1, 1, 1)
                        for t in range(TB):
                            for e in range(2):
                                h_high(l, 1, t, e)
                        mixer(l)
                        gate(l, 1, 6)
                        squares(l, 1, 0, 0)
                        squares(l, 1, 0, 1)

        @block.vector
        def _(dve):
            V = nc.vector
            steps = Steps(vec_step, VEC_STEPS)

            def lo(l, q, i=None):
                n = number(q) + 1
                dve.wait_ge(hi_ready, at(l, PIECES, n) + (0 if i is None else i * RING))
                V.tensor_tensor(w_lo[:, q % STAGES], raw[:, q % RING], w_hi[:, q % STAGES], ALU.subtract)\
                 .then_inc(lo_ready, 1)

            def ada_reduce(pos, s, use):
                dve.wait_ge(ada_landed[s], use * 16)
                V.tensor_scalar(ada_acc[:, s, :], ada_raw[:, s, 0, :], c_col[:, 0:1], None, ALU.mult)\
                 .then_inc(ada_step, 1)
                for k in range(1, KC):
                    dve.wait_ge(ada_step, (pos + ADA_RING) * KC + k)
                    V.scalar_tensor_tensor(out=ada_acc[:, s, :], in0=ada_raw[:, s, k, :], scalar=c_col[:, k:k + 1],
                                           in1=ada_acc[:, s, :], op0=ALU.mult, op1=ALU.add).then_inc(ada_step, 1)

            def ada_store(pos, layer, r):
                wait_apart(dve, ada_summed, pos + 1)
                bias = pcol[:, layer, bass.ds(r * 2 + ROW_ADA, 2)]
                V.tensor_tensor(mod[:, bass.ds(r * 2, 2)], bank[:, 7, 0:2], bias, ALU.add).then_inc(mod_ready, 1)

            def scale_col(l, site, mods):
                dve.wait_ge(mod_ready, mods)
                c0 = KC * (3 * site + SCALE)
                V.scalar_tensor_tensor(out=a_col[:, :], in0=mod[:, c0:c0 + KC], scalar=1.0,
                                       in1=cur[:, ROW_PRE[site]:ROW_PRE[site] + KC], op0=ALU.add, op1=ALU.mult)\
                 .then_inc(a_ready, 1)

            def gate_diag(l, site, mods, weight):
                dve.wait_ge(mod_ready, mods)
                c0 = KC * (3 * site + GATE)
                V.scalar_tensor_tensor(out=g_col[:, :], in0=mod[:, c0:c0 + KC], scalar=weight,
                                       in1=cur[:, ROW_POST[site]:ROW_POST[site] + KC], op0=ALU.mult, op1=ALU.mult)\
                 .then_inc(gcol_ready, 1)
                dve.wait_ge(gcol_ready, at(l, SITES, site + 1))
                V.tensor_tensor(nrm[:, 0, :, :], ident.unsqueeze(1).broadcast_to([P, KC, P]),
                                g_col[:, :].unsqueeze(2).broadcast_to([P, KC, P]), ALU.mult).then_inc(diag_ready, 1)

            def post(l, site):
                dve.wait_ge(gate_ready, at(l, SITES, site + 1))
                for t in range(TB):
                    k = at(l, SITES * TB, site * TB + t + 1)
                    dve.wait_ge(y_rstd, k)
                    scaled = nrm[:, t, :, :].rearrange("p k c -> p (k c)")
                    V.scalar_tensor_tensor(out=scaled, in0=pair(2 + 2 * t), scalar=rstd[:, 0, t:t + 1],
                                           in1=gate_rows[:, :], op0=ALU.mult, op1=ALU.mult).then_inc(y_scaled, 1)
                    dve.wait_ge(y_scaled, k)
                    V.tensor_tensor(x_sb[:, t, :], x_sb[:, t, :], scaled, ALU.add).then_inc(x_ready, 1)

            def normalise(l, site):
                for t in range(TB):
                    dve.wait_ge(x_rstd, at(l, SITES * TB, site * TB + t + 1))
                    V.tensor_scalar(nrm[:, t, :, :].rearrange("p k c -> p (k c)"), x_sb[:, t, :],
                                    rstd[:, 1, t:t + 1], None, ALU.mult).then_inc(xn_ready, 1)

            def h_whole(l, site, t):
                if t == 0:
                    dve.wait_ge(a_ready, at(l, SITES, site + 1))
                for e in range(2):
                    dve.wait_ge(xn_turned, at(l, 4 * SITES, 4 * site + 2 * t + e + 1))
                    for k in range(4 * e, 4 * e + 4):
                        c0 = KC * (3 * site + SHIFT) + k
                        V.tensor_scalar(nrm[:, t, k, :], bank[:, 2 * t + e, (k % 4) * P:(k % 4 + 1) * P],
                                        a_col[:, k:k + 1], mod[:, c0:c0 + 1], ALU.mult, ALU.add).then_inc(h_full, 1)

            def h_low(l, site, t):
                for e in range(2):
                    dve.wait_ge(h_hi_ready, at(l, 4 * SITES, 4 * site + 2 * t + e + 1))
                    part = h_hi[:, 4 * e:4 * e + 4, t * P:(t + 1) * P]
                    V.tensor_tensor(h_lo[:, 4 * e:4 * e + 4, t * P:(t + 1) * P], nrm[:, t, 4 * e:4 * e + 4, :],
                                    part, ALU.subtract).then_inc(h_lo_ready, 1)

            def product(l, ff, j):
                for t in range(TB):
                    dve.wait_ge(silu_done, at(l, 4 * FSTEPS, 2 * FSTEPS * ff + t + 1) + j * 2)
                    V.tensor_tensor(prod[:, t], silu_sb[:, t], bank[:, t, FB:2 * FB], ALU.mult).then_inc(prod_done, 1)

            def hid_low(l, ff, j):
                dve.wait_ge(hid_hi_ready, at(l, 2 * FSTEPS, FSTEPS * ff + 1) + j)
                V.tensor_tensor(hid_lo[:, :, :], bank[:, 6, :].rearrange("p (c t) -> p c t", c=2), hid_hi[:, :, :],
                                ALU.subtract).then_inc(hid_lo_ready, 1)

            def take_columns(l):
                V.tensor_copy(cur[:, :], pcol[:, bass.ds(l, 1), :].rearrange("p a n -> p (a n)")).then_inc(cur_ready, 1)
                V.tensor_copy(cur_small[:, :, :], small[:, bass.ds(l, 1), :, :].rearrange("p a b n -> p (a b) n"))\
                 .then_inc(cur_ready, 1)
                dve.wait_ge(cur_ready, at(l, 5, 2))
                sinks = cur_small[:, 3, :].rearrange("p (i e) -> p e i", e=2)
                for e, half in enumerate((EVEN, ODD)):
                    V.tensor_copy(cur_sink[half, :], sinks[half, e, :]).then_inc(cur_ready, 1)
                cb = cur[:, ROWS_A:PCOLS]
                V.tensor_scalar(cb, cb, 0.5, None, ALU.mult).then_inc(cur_ready, 1)
                dve.wait_ge(cur_ready, at(l, 5, 5))

            def mixer(l):
                steps.begin(l)

                def link(ins):
                    steps.link(dve, ins)

                def dt_part():
                    bias = cur_small[:, 0, :].unsqueeze(1).broadcast_to([P, TB, SSM_H])
                    v, mx, ab, ex, one, ln, t6, t7 = (soft[:, n, :] for n in range(8))
                    dve.wait_ge(dt_mm, at(l, 1, 2))
                    V.tensor_tensor(v.rearrange("p (t h) -> p t h", t=TB),
                                    bank[:, 0, 0:TB * SSM_H].rearrange("p (t h) -> p t h", t=TB), bias, ALU.add)\
                     .then_inc(dt_x, 1)
                    dve.wait_ge(dt_x, at(l, 1, 1))
                    V.scalar_tensor_tensor(out=ab, in0=v, scalar=-1.0, in1=v, op0=ALU.mult, op1=ALU.max)\
                     .then_inc(dt_abs, 1)
                    link(V.tensor_scalar(mx, v, 0.0, None, ALU.max))
                    dve.wait_ge(dt_exp, at(l, 1, 1))
                    V.tensor_scalar(one, ex, 1.0, None, ALU.add).then_inc(dt_one, 1)
                    dve.wait_ge(dt_one, at(l, 1, 1))
                    link(V.tensor_scalar(t6, one, -1.0, None, ALU.add))
                    link(V.tensor_tensor(t6, ex, t6, ALU.subtract))
                    link(V.reciprocal(t7, one))
                    link(V.tensor_tensor(t6, t6, t7, ALU.mult))
                    link(V.tensor_tensor(t6, t6, mx, ALU.add))
                    dve.wait_ge(dt_ln, at(l, 1, 1))
                    link(V.tensor_tensor(dt_sb[:, :, :].rearrange("p t h -> p (t h)"), ln, t6, ALU.add))
                    dve.wait_ge(exp_a_ready, at(l, 1, 1))
                    V.scalar_tensor_tensor(out=adt[:, :, :], in0=dt_sb[:, :, :], scalar=-1.0,
                                           in1=exp_a[:, :].unsqueeze(1).broadcast_to([P, TB, SSM_H]),
                                           op0=ALU.mult, op1=ALU.mult).then_inc(adt_ready, 1)

                def rope(src, t, heads, outs, signal):
                    v = src.rearrange("p (h d) -> p h d", d=HEAD)
                    cos = const[:, C_COS + t * HEAD:C_COS + (t + 1) * HEAD].unsqueeze(1)
                    sin = const[:, C_SIN + t * HEAD:C_SIN + (t + 1) * HEAD].unsqueeze(1)
                    c_part, s_part = rope_t[:, 0, 0:heads, :], rope_t[:, 1, 0:heads, :]
                    steps.mark(V.tensor_tensor(c_part, v, cos.broadcast_to([P, heads, HEAD]), ALU.mult))
                    for lo_, hi_ in ((0, 32), (32, 0)):
                        steps.mark(V.tensor_tensor(s_part[:, :, lo_:lo_ + 32], v[:, :, hi_:hi_ + 32],
                                                   sin[:, :, lo_:lo_ + 32].broadcast_to([P, heads, 32]), ALU.mult))
                    steps.settle(dve)
                    for dst in outs:
                        ins = V.tensor_tensor(dst, c_part, s_part, ALU.add)
                        ins.then_inc(signal, 1)
                    return ins

                def conv_part(ct):
                    src = bank[:, ct % 4, 0:T]
                    w = [cur[:, ROWS_A + ROW_CONVW + 8 * tap + ct:ROWS_A + ROW_CONVW + 8 * tap + ct + 1]
                         for tap in range(CONV_W)]
                    b = cur[:, ROWS_A + ROW_CONVB + ct:ROWS_A + ROW_CONVB + ct + 1]
                    if ct % 2 == 0:
                        dve.wait_ge(xbc_mm, at(l, 4, ct // 2 + 1))
                    else:
                        dve.wait_ge(stage_used, piece_done(l, Q_MIX + 3 + ct // 2))
                    link(V.tensor_scalar(conv[:, ct, :], src, w[CONV_W - 1], b, ALU.mult, ALU.add))
                    for back in range(1, CONV_W):
                        ins = V.scalar_tensor_tensor(out=conv[:, ct, back:T], in0=src[:, 0:T - back],
                                                     scalar=w[CONV_W - 1 - back], in1=conv[:, ct, back:T],
                                                     op0=ALU.mult, op1=ALU.add)
                        if back < CONV_W - 1:
                            link(ins)
                        else:
                            ins.then_inc(conv_ready, 1)

                def soft_max(c):
                    dve.wait_ge(scores, at(l, 4, c + 1))
                    link(V.tensor_reduce(sm[:, c, 0, :], bank[:, 4 + c % 2, :].rearrange("p (i k) -> p i k", i=4)
                                         [:, :, 0:KEYS[c]], AX_X, ALU.max))
                    link(V.scalar_tensor_tensor(out=sm[:, c, 0, :], in0=sm[:, c, 0, :], scalar=ATT_SCALE,
                                                in1=cur_sink[:, :], op0=ALU.mult, op1=ALU.max))
                    link(V.tensor_tensor(sm[:, c, 1, :], cur_sink[:, :], sm[:, c, 0, :], ALU.subtract))
                    V.tensor_scalar(sm[:, c, 2, :], sm[:, c, 0, :], -1.0, None, ALU.mult).then_inc(row_max, 1)

                def soft_divide(c):
                    dve.wait_ge(exps, at(l, 16, 4 * c + 4))
                    dve.wait_ge(sink_exp, at(l, 4, c + 1))
                    link(V.tensor_tensor(sm[:, c, 5, :], sm[:, c, 3, :], sm[:, c, 4, :], ALU.add))
                    link(V.reciprocal(sm[:, c, 5, :], sm[:, c, 5, :]))
                    p = probs[:, c % 2, :, 0:KEYS[c]]
                    V.tensor_tensor(p, p, sm[:, c, 5, :].unsqueeze(2).broadcast_to([P, 4, KEYS[c]]), ALU.mult)\
                     .then_inc(probs_ready, 1)

                def by_head(col):
                    return col.unsqueeze(2).broadcast_to([col.shape[0], SSM_H, HEAD])

                def heads_of(ap):
                    return ap.rearrange("p (h d) -> p h d", d=HEAD)

                M = Q_MIX
                lo(l, M + 2)
                dt_part()
                for t in range(TB):
                    wait_block(dve, q_mm, l, t, Q_MIX + 1)
                    if t:
                        dve.wait_ge(q_roped, at(l, TB, t))
                    rope(bank[:, 4 + t, :], t, ATT_H, [q_rot[:, t]], q_roped)
                for t in range(TB):
                    dve.wait_ge(v_ready, at(l, TB + 2, t + 1))
                    if t == 0:
                        dve.wait_ge(q_roped, at(l, TB, TB))
                    else:
                        dve.wait_ge(k_roped, at(l, 2 * TB, 2 * t))
                    rope(bank[:, 6 + t, 0:128], t, KV_H, [k_rot[:, t, :, n, :] for n in range(2)], k_roped)
                lo(l, M + 3)
                lo(l, M + 4)
                conv_part(0)
                conv_part(1)
                lo(l, M + 5)
                soft_max(0)
                soft_max(1)
                conv_part(2)
                conv_part(3)
                lo(l, M + 6)
                soft_divide(0)
                soft_divide(1)
                conv_part(4)
                conv_part(5)
                lo(l, M + 7)
                soft_max(2)
                soft_max(3)
                conv_part(6)
                conv_part(7)
                lo(l, M + 8)
                soft_divide(2)
                soft_divide(3)
                for t in range(TB):
                    V.tensor_tensor(nrm[:, t, :, :], upto.unsqueeze(1).broadcast_to([P, SSM_H, P]),
                                    adt[:, t, :].unsqueeze(2).broadcast_to([P, SSM_H, P]), ALU.mult)\
                     .then_inc(seg_in_ready, 1)
                lo(l, M + 9)
                lo(l, M + 10)
                for t in range(TB):
                    dve.wait_ge(z_tanhed, at(l, TB, t + 1))
                    V.scalar_tensor_tensor(out=z_silu[:, t, :], in0=z_tanh, scalar=1.0, in1=bank[:, t, :],
                                           op0=ALU.add, op1=ALU.mult).then_inc(z_ready, 1)
                for t in range(TB):
                    dve.wait_ge(xs_ready, at(l, TB, t + 1))
                    V.tensor_tensor(heads_of(xs_dt[:, t, :]), heads_of(xs_nat[:, t, :]), by_head(dt_sb[:, t, :]),
                                    ALU.mult).then_inc(xs_dt_ready, 1)
                    dve.wait_ge(xs_dt_ready, at(l, TB, t + 1))
                    V.tensor_tensor(heads_of(xs_dec[:, t, :]), heads_of(xs_dt[:, t, :]), by_head(decays[:, t, 0, :]),
                                    ALU.mult).then_inc(xs_dec_ready, 1)
                dve.wait_ge(gram_mm, at(l, 1, 1))
                V.tensor_tensor(gram[:, :, :], bank[:, 5, :].rearrange("p (b l) -> p b l", b=4),
                                upto.unsqueeze(1).broadcast_to([P, 4, P]), ALU.mult).then_inc(gram_ready, 1)
                dve.wait_ge(gram_ready, at(l, 1, 1))
                for t in range(TB):
                    dve.wait_ge(seg_exp, at(l, 2 * TB, 2 * t + 2))
                    for g in range(GROUPS):
                        m = decay_l[:, t, 4 * g:4 * g + 4, :]
                        V.tensor_tensor(m, m, gram[:, 2 * t + g, :].unsqueeze(1).broadcast_to([P, 4, P]), ALU.mult)\
                         .then_inc(mix_ready, 1)
                dve.wait_ge(state_mm, at(l, 3, 1))
                V.tensor_copy(state[:, 0, :], bank[:, 2, :]).then_inc(state_ready, 1)
                for c in (1, 2):
                    dve.wait_ge(state_ready, at(l, 3, c))
                    link(V.tensor_tensor(heads_of(state[:, c, :]), heads_of(state[:, c - 1, :]),
                                         by_head(decays[:, c // 2, 2 + c % 2, :]), ALU.mult))
                    dve.wait_ge(state_mm, at(l, 3, c + 1))
                    V.tensor_tensor(state[:, c, :], state[:, c, :], bank[:, 2 + c, :], ALU.add)\
                     .then_inc(state_ready, 1)
                dve.wait_ge(att_hi, at(l, 1, 1))
                V.tensor_tensor(h_lo[:, 4:8, :], att[:, :, :], h_hi[:, 4:8, :], ALU.subtract).then_inc(att_lo, 1)
                lo(l, M + 11)
                for t in range(TB):
                    y = xs_dec[:, t, :]
                    tmp = nrm[:, t, 0:4, :].rearrange("p k c -> p (k c)")
                    r = ODD if t == 0 else slice(0, P)
                    link(V.tensor_tensor(heads_of(y), heads_of(xs_nat[:, t, :]), by_head(cur_small[:, 2, :]), ALU.mult))
                    dve.wait_ge(diag_mm, at(l, TB, t + 1))
                    link(V.tensor_tensor(y, y, bank[:, t, :], ALU.add))
                    dve.wait_ge(off_mm, at(l, TB, t + 1))
                    link(V.tensor_tensor(heads_of(tmp[r]), heads_of(bank[r, 6 + t, :]), by_head(decays[r, t, 1, :]),
                                         ALU.mult))
                    link(V.tensor_tensor(y[r], y[r], tmp[r], ALU.add))
                    V.scalar_tensor_tensor(out=y, in0=y, scalar=0.5, in1=z_silu[:, t, :], op0=ALU.mult,
                                           op1=ALU.mult).then_inc(gated, 1)
                for t in range(TB):
                    dve.wait_ge(g_rstd, at(l, TB, t + 1))
                    for g in range(GROUPS):
                        y = xs_dec[:, t, 256 * g:256 * g + 256]
                        V.tensor_scalar(y, y, grstd[:, t, g:g + 1], None, ALU.mult).then_inc(ssd_ready, 1)
                lo(l, M + 12)
                for t in range(TB):
                    dve.wait_ge(ssd_turned, at(l, TB, t + 1))
                    for k in range(4):
                        V.tensor_scalar(nrm[:, t, k, :], bank[:, t, k * P:(k + 1) * P],
                                        cur[:, ROW_SSDN + k:ROW_SSDN + k + 1], None, ALU.mult).then_inc(ssd_full, 1)
                for t in range(TB):
                    dve.wait_ge(ssd_hi, at(l, TB, t + 1))
                    V.tensor_tensor(h_lo[:, 0:4, t * P:(t + 1) * P], nrm[:, t, 0:4, :],
                                    h_hi[:, 0:4, t * P:(t + 1) * P], ALU.subtract).then_inc(ssd_lo, 1)
                steps.end()

            dve.sem_inc(lo_ready, RING)
            dve.sem_inc(ada_step, KC * ADA_RING)
            dve.wait_ge(params_turned, 2)
            V.tensor_copy(pcol[:, :, 0:ROWS_A], bank[:, 1, 0:DEPTH * ROWS_A].rearrange("p (l n) -> p l n", l=DEPTH))\
             .then_inc(pcol_ready, 1)
            V.tensor_copy(pcol[:, :, ROWS_A:PCOLS], bank[:, 2, 0:DEPTH * ROWS_B].rearrange("p (l n) -> p l n", l=DEPTH))\
             .then_inc(pcol_ready, 1)
            dve.wait_ge(pcol_ready, 2)
            dve.wait_ge(const_landed, 16)
            dve.wait_ge(c_ready, 1)
            for r in range(ADA_AHEAD):
                ada_reduce(r, r % ADA_RING, r // ADA_RING + 1)
                if r:
                    ada_store(r - 1, 0, r - 1)
            ada_store(ADA_AHEAD - 1, 0, ADA_AHEAD - 1)
            dve.wait_ge(x_landed, 16 * TB)
            dve.wait_ge(small_landed, 16 * 4 * DEPTH)
            dve.sem_inc(x_ready, TB)

            with dve.Fori(0, DEPTH) as l:
                ada0 = l * ADA_PIECES + ADA_AHEAD
                use0 = l * (ADA_PIECES // 2) + ADA_AHEAD // 2
                take_columns(l)
                for f, ff, q0 in FFNS:
                    site = 2 * ff
                    scale_col(l, site, ada0 if ff == 0 else ada0 + (ADA_LOOP1 + ADA_EPI))
                    normalise(l, site)
                    h_whole(l, site, 0)
                    h_low(l, site, 0)
                    lo(l, q0)
                    h_whole(l, site, 1)
                    h_low(l, site, 1)
                    lo(l, q0 + 1)
                    if ff:
                        for u in range(ADA_PRO):
                            p = ADA_LOOP1 + ADA_EPI + u
                            ada_reduce(ada0 + p, u, use0 + (p // 2 + 1))
                            ada_store(ada0 + p, l, ADA_AHEAD + p)
                    with dve.Fori(0, 5) as i:
                        for u in range(2):
                            q, j = q0 + 2 + 3 * u, i * 2 + u
                            lo(l, q, i)
                            product(l, ff, j)
                            if ff == 0:
                                p, r, use = i * 4 + (ada0 + 2 * u), i * 4 + (ADA_AHEAD + 2 * u), i * 2 + (use0 + u + 1)
                                if u:
                                    ada_store(p - 1, l, r - 1)
                                lo(l, q + 1, i)
                                ada_reduce(p, 0, use)
                                hid_low(l, ff, j)
                                lo(l, q + 2, i)
                                ada_reduce(p + 1, 1, use)
                                ada_store(p, l, r)
                                if u:
                                    ada_store(p + 1, l, r + 1)
                            else:
                                p, r, use = i * 2 + (ada0 + (26 + u)), i * 2 + u, i + (use0 + 14)
                                lo(l, q + 1, i)
                                ada_reduce(p, u, use)
                                hid_low(l, ff, j)
                                lo(l, q + 2, i)
                                ada_store(p, 1 - l, r)
                    gate_diag(l, site, ada0 + (ADA_LOOP1 if ff == 0 else 26), 0.5)
                    lo(l, q0 + 32)
                    product(l, ff, FSTEPS - 1)
                    hid_low(l, ff, FSTEPS - 1)
                    if ff == 0:
                        lo(l, Q_MIX)
                        lo(l, Q_MIX + 1)
                    post(l, site)
                    if ff == 0:
                        scale_col(l, 1, ada0 + ADA_LOOP1)
                        normalise(l, 1)
                        for t in range(TB):
                            h_whole(l, 1, t)
                            h_low(l, 1, t)
                        for u in range(ADA_EPI):
                            p = ADA_LOOP1 + u
                            ada_reduce(ada0 + p, u % 2, use0 + (p // 2 + 1))
                            ada_store(ada0 + p, l, ADA_AHEAD + p)
                        mixer(l)
                        gate_diag(l, 1, ada0 + (ADA_LOOP1 + ADA_EPI), 1.0)
                        post(l, 1)

        @block.tensor
        def _(pe):
            MM = nc.tensor.matmul

            def split(dst, xs, ys, start=False, stop=False):
                first = MM(dst, xs[0], ys[0], start=start, stop=False)
                MM(dst, xs[0], ys[1], start=False, stop=False)
                return first, MM(dst, xs[1], ys[0], start=False, stop=stop)

            def weights(l, q, i=None):
                pe.wait_ge(lo_ready, at(l, PIECES, RING + number(q) + 1) + (0 if i is None else i * RING))

            def stage(q, pattern, **sizes):
                return [w[:, q % STAGES, :].rearrange(pattern, **sizes) for w in (w_hi, w_lo)]

            def h_cols(k, t):
                return h_hi[:, k, t * P:(t + 1) * P], h_lo[:, k, t * P:(t + 1) * P]

            def hid_cols(c, t):
                return hid_hi[:, c, t * P:(t + 1) * P], hid_lo[:, c, t * P:(t + 1) * P]

            def h_parts(l, site, t, e):
                pe.wait_ge(h_lo_ready, at(l, 4 * SITES, 4 * site + 2 * t + e + 1))

            def gu_piece(l, ff, q, half, j=None, i=None):
                weights(l, q, i)
                wh, wl = stage(q, "p (g k n) -> p g k n", g=2, k=4)
                for t in range(TB):
                    if i is None:
                        h_parts(l, 2 * ff, t, half)
                    elif half == 0:
                        pe.wait_ge(prod_done, at(l, 4 * FSTEPS, 2 * FSTEPS * ff + t - 1) + j * 2)
                    for k in range(4):
                        _, mm = split(bank[:, t, :], h_cols(4 * half + k, t), (wh[:, :, k, :], wl[:, :, k, :]),
                                      start=(half == 0 and k == 0), stop=(half == 1 and k == 3))
                    if half == 1:
                        mm.then_inc(gu_done, 1)
                if half == 0:
                    mm.then_inc(stage_used, 1)

            def turn_products(l, ff, j):
                for t in range(TB):
                    pe.wait_ge(prod_done, at(l, 4 * FSTEPS, 2 * FSTEPS * ff + t + 1) + j * 2)
                    for c in range(2):
                        o = c * T + t * P
                        mm = nc.tensor.transpose(bank[:, 6, o:o + P], prod[:, t, c * P:(c + 1) * P], ident)
                mm.then_inc(hid_turned, 1)

            def rows_piece(q, cols, start=False, stop=False, frees=False, done=None):
                wh, wl = stage(q, "p (c n) -> p c n", c=2)
                for t in range(TB):
                    for half in range(2):
                        n = slice(512 * half, 512 * half + 512)
                        for c in range(2):
                            first, mm = split(bank[:, 2 + 2 * t + half, :], cols(c, t), (wh[:, c, n], wl[:, c, n]),
                                              start=(start and c == 0), stop=(stop and c == 1))
                            if frees and (t, half, c) == (0, 0, 0):
                                first.then_inc(stage_used, 1)
                    if done is not None and t == 0:
                        mm.then_inc(done, 1)
                mm.then_inc(stage_used, 1)

            def open_y():
                for b in range(2, 6):
                    mm = MM(bank[:, b, :], zeros_r[:, 0:P], zeros_r[:, :], start=True, stop=False)
                    if b == 2:
                        mm.then_inc(stage_used, 1)

            def sum_columns(s):
                for e in range(2):
                    mm = MM(bank[:, 7, e:e + 1], ada_acc[:, s, e * P:(e + 1) * P], ones[:, 0:1], start=True, stop=True)
                mm.then_inc(ada_summed, 1)

            def ada(pos, s):
                pe.wait_ge(ada_step, (pos + (ADA_RING + 1)) * KC)
                pe.wait_ge(mod_ready, pos)
                sum_columns(s)

            def turn_rows(l, site):
                for t in range(TB):
                    pe.wait_ge(xn_ready, at(l, SITES * TB, site * TB + t + 1))
                    for e in range(2):
                        for k in range(4):
                            mm = nc.tensor.transpose(bank[:, 2 * t + e, k * P:(k + 1) * P], nrm[:, t, 4 * e + k, :],
                                                     ident)
                        mm.then_inc(xn_turned, 1)

            def spread_gate(l, site, b):
                pe.wait_ge(diag_ready, at(l, SITES, site + 1))
                for e in range(2):
                    mm = MM(bank[:, b + e, :], ones, nrm[:, 0, 4 * e:4 * e + 4, :], start=True, stop=True)
                mm.then_inc(gate_spread, 1)

            def mixer(l):
                M = Q_MIX

                def wide(m, kh, b, signal):
                    weights(l, M + m)
                    wh, wl = stage(M + m, "p (k n) -> p k n", k=4)
                    for t in range(TB):
                        for k in range(4):
                            _, mm = split(bank[:, b + t, :], h_cols(4 * kh + k, t), (wh[:, k, :], wl[:, k, :]),
                                          start=(kh == 0 and k == 0), stop=(kh == 1 and k == 3))
                        if kh == 1 and t == 0:
                            mm.then_inc(signal, 1)
                    mm.then_inc(stage_used, 1)

                def xbc(m):
                    weights(l, M + 3 + m)
                    wh, wl = stage(M + 3 + m, "p (k n) -> p k n", k=KC)
                    for e in range(2):
                        for k in range(KC):
                            cols = slice(e * P, (e + 1) * P)
                            _, mm = split(bank[:, (2 * m + e) % 4, 0:T], (wh[:, k, cols], wl[:, k, cols]),
                                          (h_hi[:, k, :], h_lo[:, k, :]), start=(k == 0), stop=(k == KC - 1))
                        mm.then_inc(stage_used if e else xbc_mm, 1)

                def score(c):
                    for i in range(4):
                        for e in range(2):
                            o = i * P
                            for k0, n in WINDOWS[c]:
                                mm = MM(bank[64 * e:64 * e + 64, 4 + c % 2, o:o + n], q_t[:, i, 64 * c:64 * c + 64],
                                        k_t[:, i // 2, e, k0:k0 + n], start=True, stop=True)
                                o += n
                    mm.then_inc(scores, 1)

                def turn_probs(c):
                    wait_apart(pe, probs_ready, at(l, 4, c + 1))
                    for i in range(4):
                        mm = nc.tensor.transpose(bank[0:KEYS[c], 6 + c % 2, i * P:(i + 1) * P],
                                                 probs[:, c % 2, i, 0:KEYS[c]], ident)
                    mm.then_inc(probs_turned, 1)

                def attend(c):
                    wait_apart(pe, probs_t_ready, at(l, 4, c + 1))
                    n = KEYS[c]
                    for i in range(4):
                        for e in range(2):
                            mm = MM(bank[64 * e:64 * e + 64, 4 + c % 2, 64 * i:64 * i + 64],
                                    v_sb[0:n, V_OF[c], 64 * (i // 2):64 * (i // 2) + 64],
                                    probs_t[0:n, c % 2, i, 64 * e:64 * e + 64], start=True, stop=True)
                    mm.then_inc(att_mm, 1)

                pe.wait_ge(dtw_landed, at(l, 1, 1) * 16)
                for t in range(TB):
                    for e in range(2):
                        h_parts(l, 1, t, e)
                for t in range(TB):
                    for k in range(KC):
                        mm = MM(bank[:, 0, t * SSM_H:(t + 1) * SSM_H], nrm[:, t, k, :], w_dt[:, k, :],
                                start=(k == 0), stop=(k == KC - 1))
                mm.then_inc(dt_mm, 1)
                wide(0, 0, 4, None)
                wide(1, 1, 4, q_mm)
                for u in range(ADA_EPI):
                    ada(l * ADA_PIECES + (ADA_AHEAD + ADA_LOOP1 + u), u % ADA_RING)
                weights(l, M + 2)
                pe.wait_ge(mod_ready, l * ADA_PIECES + (ADA_AHEAD + ADA_LOOP1 + ADA_EPI))
                wh, wl = stage(M + 2, "p (k n) -> p k n", k=KC)
                for t in range(TB):
                    for k in range(KC):
                        _, mm = split(bank[:, 6 + t, 0:256], h_cols(k, t), (wh[:, k, :], wl[:, k, :]),
                                      start=(k == 0), stop=(k == KC - 1))
                    mm.then_inc(stage_used if t else kv_mm, 1)
                pe.wait_ge(adt_ready, at(l, 1, 1))
                for t in range(TB):
                    for n, c0 in enumerate((C_AFTER, C_UPTO, C_FIRST, C_SECOND)):
                        o = (4 * t + n) * SSM_H
                        mm = MM(bank[:, 1, o:o + SSM_H], const[:, c0:c0 + P], adt[:, t, :], start=True, stop=True)
                mm.then_inc(decay_sums, 1)
                pe.wait_ge(decays_ready, at(l, 1, 1))
                xbc(0)
                for t in range(TB):
                    pe.wait_ge(q_roped, at(l, TB, t + 1))
                    for i in range(4):
                        mm = nc.tensor.transpose(bank[:, 4 + t, i * P:(i + 1) * P],
                                                 q_rot[:, t, 2 * i:2 * i + 2, :].rearrange("p h d -> p (h d)"), ident)
                    mm.then_inc(q_turned, 1)
                pe.wait_ge(k_roped, at(l, 2 * TB, 2 * TB))
                for g in range(KV_H):
                    for t in range(TB):
                        mm = nc.tensor.transpose(bank[:, 6, g * T + t * P:g * T + (t + 1) * P],
                                                 k_rot[:, t, g, :, :].rearrange("p a d -> p (a d)"), ident)
                mm.then_inc(k_turned, 1)
                xbc(1)
                pe.wait_ge(q_t_ready, at(l, TB, TB))
                pe.wait_ge(k_t_ready, at(l, 2, 2))
                score(0)
                score(1)
                pe.wait_ge(conv_ready, at(l, 8, 2))
                xbc(2)
                for c in (0, 1):
                    turn_probs(c)
                attend(0)
                attend(1)
                pe.wait_ge(conv_ready, at(l, 8, 4))
                xbc(3)
                for c in (2, 3):
                    pe.wait_ge(att_ready, at(l, 4, c - 1))
                    score(c)
                pe.wait_ge(conv_ready, at(l, 8, 6))
                wide(7, 0, 0, None)
                for c in (2, 3):
                    turn_probs(c)
                attend(2)
                attend(3)
                wide(8, 1, 0, z_mm)
                pe.wait_ge(probs_t_ready, at(l, 4, 4))
                for t in range(TB):
                    pe.wait_ge(seg_in_ready, at(l, TB, t + 1))
                    for hh in range(2):
                        if t:
                            pe.wait_ge(seg_exp, at(l, 2 * TB, hh + 1))
                        MM(bank[:, 6 + hh, :], after, nrm[:, t, 4 * hh:4 * hh + 4, :], start=True, stop=True)\
                            .then_inc(seg_mm, 1)
                pe.wait_ge(xbc_ready, at(l, 8, 8))
                pe.wait_ge(conv_ready, at(l, 8, 8))
                for t in range(TB):
                    for k in range(4):
                        mm = nc.tensor.transpose(bank[:, 2 + t, k * P:(k + 1) * P], conv[:, k, t * P:(t + 1) * P],
                                                 ident)
                    mm.then_inc(xs_turned, 1)
                pe.wait_ge(att_ready, at(l, 4, 4))
                for t in range(TB):
                    for g in range(GROUPS):
                        o = (t * GROUPS + g) * P
                        mm = nc.tensor.transpose(bank[:, 4, o:o + P], conv[:, 4 + g, t * P:(t + 1) * P], ident)
                mm.then_inc(b_turned, 1)
                for t in range(TB):
                    for g in range(GROUPS):
                        o = (t * GROUPS + g) * P
                        rows = slice(t * P, (t + 1) * P)
                        mm = MM(bank[:, 5, o:o + P], conv[:, 4 + g, rows], conv[:, 6 + g, rows], start=True, stop=True)
                mm.then_inc(gram_mm, 1)
                pe.wait_ge(b_ready, at(l, 1, 1))
                for c in range(3):
                    pe.wait_ge(xs_dec_ready, at(l, TB, c // 2 + 1))
                    half = ODD if c % 2 else EVEN
                    for g in range(GROUPS):
                        mm = MM(bank[:, 2 + c, 256 * g:256 * g + 256], b_nat[half, c // 2, P * g:P * g + P],
                                xs_dec[half, c // 2, 256 * g:256 * g + 256], start=True, stop=True)
                    mm.then_inc(state_mm, 1)
                for t in range(TB):
                    pe.wait_ge(mix_ready, at(l, 2 * TB, 2 * t + 2))
                    pe.wait_ge(z_ready, at(l, TB, t + 1))
                    for h in range(SSM_H):
                        mm = MM(bank[:, t, 64 * h:64 * h + 64], decay_l[:, t, h, :], xs_dt[:, t, 64 * h:64 * h + 64],
                                start=True, stop=True)
                    mm.then_inc(diag_mm, 1)
                pe.wait_ge(seg_exp, at(l, 2 * TB, 2 * TB))
                for c in range(1, 4):
                    pe.wait_ge(state_ready, at(l, 3, c))
                    for g in range(GROUPS):
                        mm = MM(bank[ODD if c % 2 else EVEN, 6 + c // 2, 256 * g:256 * g + 256],
                                conv[:, 6 + g, 64 * c:64 * c + 64], state[:, c - 1, 256 * g:256 * g + 256],
                                start=True, stop=True)
                    if c != 2:
                        mm.then_inc(off_mm, 1)
                def out_piece(n, k0, **flags):
                    weights(l, M + 9 + n)
                    rows_piece(M + 9 + n, lambda c, t: h_cols(k0 + c, t), **flags)

                pe.wait_ge(att_lo, at(l, 1, 1))
                out_piece(0, 4, start=True)
                out_piece(1, 6)
                for t in range(TB):
                    pe.wait_ge(ssd_ready, at(l, 2 * TB, 2 * t + 2))
                    for k in range(4):
                        mm = nc.tensor.transpose(bank[:, t, k * P:(k + 1) * P], xs_dec[:, t, k * P:(k + 1) * P], ident)
                    mm.then_inc(ssd_turned, 1)
                for t in range(TB):
                    pe.wait_ge(ssd_lo, at(l, TB, t + 1))
                out_piece(2, 0)
                out_piece(3, 2, stop=True, done=y_done)
                spread_gate(l, 1, 6)

            pe.sem_inc(stage_used, STAGES)
            pe.sem_inc(dt_mm, 1)
            pe.wait_ge(const_landed, 16)
            pe.wait_ge(rows_landed, 16 * (1 + 10 * DEPTH))
            nc.tensor.transpose(bank[:, 0, 0:KC], c_row[:, :], ident[0:KC, 0:KC]).then_inc(params_turned, 1)
            for l in range(DEPTH):
                nc.tensor.transpose(bank[:, 1, l * ROWS_A:(l + 1) * ROWS_A], prow_a[:, l, :], ident[0:ROWS_A, 0:ROWS_A])
                mm = nc.tensor.transpose(bank[:, 2, l * ROWS_B:(l + 1) * ROWS_B], prow_b[:, l, :],
                                         ident[0:ROWS_B, 0:ROWS_B])
            mm.then_inc(params_turned, 1)
            for r in range(ADA_AHEAD):
                if r:
                    ada(r, r % ADA_RING)
                else:
                    pe.wait_ge(ada_step, (ADA_RING + 1) * KC)
                    sum_columns(0)
            pe.wait_ge(zeros_ready, 1)
            pe.wait_ge(kt_zeroed, 1)

            with pe.Fori(0, DEPTH) as l:
                ada0 = l * ADA_PIECES + ADA_AHEAD
                for f, ff, q0 in FFNS:
                    site = 2 * ff
                    turn_rows(l, site)
                    gu_piece(l, ff, q0, 0)
                    gu_piece(l, ff, q0 + 1, 1)
                    open_y()
                    if ff:
                        for u in range(ADA_PRO):
                            ada(ada0 + (ADA_LOOP1 + ADA_EPI + u), u)
                    turn_products(l, ff, 0)
                    with pe.Fori(0, 5) as i:
                        for u in range(2):
                            q, j = q0 + 2 + 3 * u, i * 2 + (u + 1)
                            gu_piece(l, ff, q, 0, j, i)
                            ada(i * 4 + (ada0 + 2 * u), 0) if ff == 0 else ada(i * 2 + (ada0 + (26 + u)), u)
                            gu_piece(l, ff, q + 1, 1, j, i)
                            if ff == 0:
                                ada(i * 4 + (ada0 + (2 * u + 1)), 1)
                            weights(l, q + 2, i)
                            pe.wait_ge(hid_lo_ready, at(l, 2 * FSTEPS, FSTEPS * ff) + j)
                            rows_piece(q + 2, hid_cols, frees=True)
                            turn_products(l, ff, j)
                    spread_gate(l, site, 0)
                    weights(l, q0 + 32)
                    pe.wait_ge(hid_lo_ready, at(l, 2 * FSTEPS, FSTEPS * (ff + 1)))
                    rows_piece(q0 + 32, hid_cols, stop=True, done=y_done)
                    if ff == 0:
                        turn_rows(l, 1)
                        mixer(l)


INPUTS = ["x", "c", "ada_w", "ada_b", "ffn1_norm_pre", "ffn1_w_gate", "ffn1_w_up", "ffn1_w_down", "ffn1_norm_post",
          "mix_norm_pre", "w_in", "conv_w", "conv_b", "dt_bias", "a_log", "d_skip", "ssd_norm", "attn_sinks", "w_out",
          "mix_norm_post", "ffn2_norm_pre", "ffn2_w_gate", "ffn2_w_up", "ffn2_w_down", "ffn2_norm_post"]


def kernel(**inputs):
    import concourse.bacc as bacc
    from concourse.bass_utils import run_bass_kernel_spmd

    nc = bacc.Bacc("TRN2", target_bir_lowering=False, num_devices=1, dynamic_dma_scratch_size=1024)
    arrays, aps = {}, {}
    for name in INPUTS:
        arrays[name] = np.ascontiguousarray(inputs[name])
    arrays["const"] = constants()
    for name, v in arrays.items():
        aps[name] = nc.dram_tensor("in_" + name, v.shape, mybir.dt.from_np(v.dtype), kind="ExternalInput").ap()
    out = nc.dram_tensor("out_x", (1, T, D), F32, kind="ExternalOutput").ap()
    trunk(nc, aps, out)
    r = run_bass_kernel_spmd(nc, [{"in_" + name: v for name, v in arrays.items()}], core_ids=[0])
    return r.results[0]["out_x"]
```

```python
from contextlib import ExitStack

import numpy as np

import concourse.bass as bass
from concourse import mybir

ALU = mybir.AluOpType
ACT = mybir.ActivationFunctionType
AX_X = mybir.AxisListType.X
F32 = mybir.dt.float32
F32R = mybir.dt.float32r

P = 128
DEPTH, T, D, FF = 2, 256, 1024, 2816
CHUNK, HEAD, STATE = 64, 64, 128
SSM_H, GROUPS, D_SSM = 8, 2, 512
ATT_H, KV_H = 8, 2
CONV_W, CONV_DIM = 4, 1024
D_IN = D_SSM + CONV_DIM + SSM_H + ATT_H * HEAD + 2 * KV_H * HEAD
EPS = 1e-6
ROPE_THETA = 10000.0
TB = T // P
KC = D // P
FB = 256
FSTEPS = FF // FB
SITES = 3
ATT_SCALE = HEAD ** -0.5

COL_Z, COL_XBC = 0, D_SSM
COL_DT = COL_XBC + CONV_DIM
COL_Q = COL_DT + SSM_H
COL_KV = COL_Q + ATT_H * HEAD

PIECE = 2048
RING, STAGES = 6, 3
FFN_PIECES = 3 * FSTEPS
MIX_PIECES, MIX_PLACES = 13, 18
PLACES = 2 * FFN_PIECES + MIX_PLACES
PIECES = 2 * FFN_PIECES + MIX_PIECES
Q_MIX = FFN_PIECES
Q_FFN2 = FFN_PIECES + MIX_PLACES
assert PLACES % RING == 0 and RING % STAGES == 0 and DEPTH == 2


MIX = [Q_MIX + m for m in (0, 1, 2, 3, 4, 5, 6, 8, 9, 11, 12, 13, 14)]
assert len(MIX) == MIX_PIECES and MIX[-1] < Q_FFN2


def is_piece(q):
    return not Q_MIX <= q % PLACES < Q_FFN2 or q % PLACES in MIX


def number(q):
    return sum(is_piece(p) for p in range(q))


def before(q, ring):
    p = q - ring
    while not is_piece(p):
        p -= ring
    return number(p) if p >= 0 else number(p + PLACES) - PIECES


def uses(q):
    return sum(is_piece(p) for p in range(q % RING, q + 1, RING))


USES = [uses(PLACES - RING + s) for s in range(RING)]

ADA_W = 256
ADA_PIECES = 9 * D // ADA_W
ADA_RING = 2
ADA_AHEAD = 10
ADA_LOOP1, ADA_EPI, ADA_PRO = 20, 4, 2
FIRST_RING = 5
FIRST_VEC = 6
assert ADA_AHEAD % FIRST_RING == 0
assert ADA_AHEAD + ADA_LOOP1 + ADA_EPI + ADA_PRO == ADA_PIECES and ADA_PIECES % ADA_RING == 0

ROW_ADA = 0
ROW_PRE = [72, 80, 88]
ROW_POST = [96, 104, 112]
ROW_SSDN = 120
ROWS_A = 124
ROW_CONVB, ROW_CONVW = 0, 8
ROWS_B = 8 + 8 * CONV_W
PCOLS = ROWS_A + ROWS_B

C_IDENT, C_AFTER, C_UPTO, C_FIRST, C_SECOND, C_ONES, C_COS, C_SIN = 0, 128, 256, 384, 512, 640, 768, 896
C_WIDTH = 1024
SHIFT, SCALE, GATE = 0, 1, 2


def constants():
    c = np.zeros((P, C_WIDTH), np.float32)
    k, l = np.arange(P)[:, None], np.arange(P)[None, :]
    same = k // CHUNK == l // CHUNK
    c[:, C_IDENT:C_IDENT + P] = k == l
    c[:, C_AFTER:C_AFTER + P] = same & (k > l)
    c[:, C_UPTO:C_UPTO + P] = same & (k <= l)
    c[:, C_FIRST:C_FIRST + P] = k < CHUNK
    c[:, C_SECOND:C_SECOND + P] = k >= CHUNK
    c[:, C_ONES:C_ONES + P] = 1.0
    half = HEAD // 2
    inv_freq = np.float32(ROPE_THETA) ** (-np.arange(half, dtype=np.float32) / np.float32(half))
    ang = np.arange(T, dtype=np.float32)[:, None] * inv_freq[None, :]
    cos, sin = np.cos(ang).astype(np.float32), np.sin(ang).astype(np.float32)
    for t in range(TB):
        rows = slice(t * P, (t + 1) * P)
        c[:, C_COS + t * HEAD:C_COS + (t + 1) * HEAD] = np.concatenate([cos[rows], cos[rows]], 1)
        c[:, C_SIN + t * HEAD:C_SIN + (t + 1) * HEAD] = np.concatenate([-sin[rows], sin[rows]], 1)
    return c


VEC_STEPS = 7 + 3 * 2 * TB + 2 * 8 + 5 * 4 + 2 + 3 * TB


class Steps:

    def __init__(self, sem, per_layer):
        self.sem, self.per_layer = sem, per_layer

    def begin(self, l):
        self.l, self.n = l, 0

    def link(self, eng, ins):
        self.mark(ins)
        self.settle(eng)

    def mark(self, ins):
        ins.then_inc(self.sem, 1)
        self.n += 1

    def settle(self, eng):
        eng.wait_ge(self.sem, self.l * self.per_layer + self.n)

    def end(self):
        assert self.n == self.per_layer, (self.n, self.per_layer)


def trunk(nc, a, out):
    ctx = ExitStack()
    with ctx:
        def sb(name, shape, dt=F32):
            return ctx.enter_context(nc.sbuf_tensor(name, shape, dt))

        def sem(name):
            return ctx.enter_context(nc.semaphore(name))

        raw = sb("raw", [P, RING, PIECE])
        w_hi = sb("w_hi", [P, STAGES, PIECE], F32R)
        w_lo = sb("w_lo", [P, STAGES, PIECE], F32R)
        ada_raw = sb("ada_raw", [P, ADA_RING, KC, ADA_W])
        ada_acc = sb("ada_acc", [P, ADA_RING, ADA_W])
        x_sb = sb("x_sb", [P, TB, D])
        h_hi = sb("h_hi", [P, KC, T], F32R)
        h_lo = sb("h_lo", [P, KC, T], F32R)
        nrm = sb("nrm", [P, TB, KC, P])
        gate_rows = sb("gate_rows", [P, D])
        const = sb("const", [P, C_WIDTH])
        prow_a = sb("prow_a", [ROWS_A, DEPTH, P])
        prow_b = sb("prow_b", [ROWS_B, DEPTH, P])
        c_row = sb("c_row", [KC, P])
        pcol = sb("pcol", [P, DEPTH, PCOLS])
        c_col = sb("c_col", [P, KC])
        small = sb("small", [P, DEPTH, 4, 8])
        cur = sb("cur", [P, PCOLS])
        cur_small = sb("cur_small", [P, 4, 8])
        cur_sink = sb("cur_sink", [P, 4])
        mod = sb("mod", [P, 2 * ADA_PIECES])
        a_col = sb("a_col", [P, KC])
        g_col = sb("g_col", [P, KC])
        sq_sum = sb("sq_sum", [P, 2, TB])
        rstd = sb("rstd", [P, 2, TB])
        pow_in = sb("pow_in", [P, 2, TB])
        minus_half = sb("minus_half", [P, 4])
        zeros_r = sb("zeros_r", [P, 512], F32R)
        ffn_buf = sb("ffn_buf", [P, 1024])
        silu_sb = ffn_buf[:, 0:TB * FB].rearrange("p (t n) -> p t n", t=TB)
        prod = ffn_buf[:, TB * FB:2 * TB * FB].rearrange("p (t n) -> p t n", t=TB)
        hid_hi = sb("hid_hi", [P, 2, T], F32R)
        hid_lo = sb("hid_lo", [P, 2, T], F32R)
        w_dt_hi = sb("w_dt_hi", [P, KC, SSM_H], F32R)
        w_dt_lo = sb("w_dt_lo", [P, KC, SSM_H], F32R)
        soft = sb("soft", [P, 8, TB * SSM_H])
        w_dt = soft[:, 4:8, :].rearrange("p a (b h) -> p (a b) h", h=SSM_H)
        dt_sb = sb("dt_sb", [P, TB, SSM_H])
        adt = sb("adt", [P, TB, SSM_H])
        exp_a = sb("exp_a", [P, SSM_H])
        decays = sb("decays", [P, TB, 4, SSM_H])
        rope_buf = sb("rope_buf", [P, 2 * SSM_H * P])
        rope_t = rope_buf[:, 0:1024].rearrange("p (a h d) -> p a h d", a=2, d=HEAD)
        q_rot = rope_buf[:, 1024:2048].rearrange("p (t h d) -> p t h d", t=TB, d=HEAD)
        decay_l = rope_buf[:, :].rearrange("p (t h s) -> p t h s", t=TB, s=P)
        k_rot = sb("k_rot", [P, TB, KV_H, 2, HEAD])
        v_sb = sb("v_sb", [P, TB + 1, KV_H * HEAD])
        k_t = sb("k_t", [P, KV_H, 2, T])
        conv = sb("conv", [P, 8, T])
        tanh_b = sb("tanh_b", [P, 512])
        tanh_sb = tanh_b[:, :].rearrange("p (b n) -> p b n", b=2)
        dt_row = tanh_b[0:SSM_H, 0:T]
        b_nat = tanh_b[:, :].rearrange("p (t n) -> p t n", t=TB)
        probs = ffn_buf[:, :].rearrange("p (b i k) -> p b i k", b=2, i=4)
        z_tanh = ffn_buf[:, 0:512]
        gram = ffn_buf[:, 512:1024].rearrange("p (b l) -> p b l", b=4)
        z_silu = sb("z_silu", [P, TB, 512])
        xs_nat = sb("xs_nat", [P, TB, D_SSM])
        xs_dt = sb("xs_dt", [P, TB, D_SSM])
        probs_t = xs_dt[:, :, :].rearrange("p b (i q) -> p b i q", i=4)
        xs_dec = sb("xs_dec", [P, TB, D_SSM])
        q_t = xs_dec[:, :, :].rearrange("p b (i q) -> p (b i) q", i=2)
        state = sb("state", [P, 3, D_SSM])
        att = sb("att", [P, 4, T])
        sm = sb("sm", [P, 4, 6, 4])
        gsq = sb("gsq", [P, TB, GROUPS])
        gpow = sb("gpow", [P, TB, GROUPS])
        grstd = sb("grstd", [P, TB, GROUPS])

        first_raw = [ada_raw[:, 0], ada_raw[:, 1], conv[:, :, :],
                     rope_buf[:, :].rearrange("p (k n) -> p k n", k=KC),
                     raw[:, RING - 1, :].rearrange("p (k n) -> p k n", k=KC)]

        bank = ctx.enter_context(nc.psum_tensor("bank", [P, 8, 512], F32))

        ident = const[:, C_IDENT:C_IDENT + P]
        after = const[:, C_AFTER:C_AFTER + P]
        upto = const[:, C_UPTO:C_UPTO + P]
        ones = const[:, C_ONES:C_ONES + P]

        def pair(b):
            return bank[:, b:b + 2, :].rearrange("p a n -> p (a n)")

        x_landed = sem("x_landed")
        const_landed = sem("const_landed")
        c_landed = sem("c_landed")
        rows_landed = sem("rows_landed")
        small_landed = sem("small_landed")
        c_turned = sem("c_turned")
        params_turned = sem("params_turned")
        pcol_ready = sem("pcol_ready")
        c_ready = sem("c_ready")
        zeros_ready = sem("zeros_ready")
        half_ready = sem("half_ready")
        kt_zeroed = sem("kt_zeroed")
        out_landed = sem("out_landed")
        raw_landed = [sem(f"raw_landed{s}") for s in range(RING)]
        hi_ready = sem("hi_ready")
        lo_ready = sem("lo_ready")
        stage_used = sem("stage_used")
        ada_landed = [sem(f"ada_landed{s}") for s in range(ADA_RING)]
        first_landed = ada_landed + [sem(f"first_landed{s}") for s in range(ADA_RING, FIRST_RING)]
        first_step = sem("first_step")
        first_summed = sem("first_summed")
        ada_step = sem("ada_step")
        ada_summed = sem("ada_summed")
        mod_ready = sem("mod_ready")
        cur_ready = sem("cur_ready")
        x_ready = sem("x_ready")
        x_squared = sem("x_squared")
        y_squared = sem("y_squared")
        pow_arg = sem("pow_arg")
        x_rstd = sem("x_rstd")
        y_rstd = sem("y_rstd")
        xn_ready = sem("xn_ready")
        xn_turned = sem("xn_turned")
        a_ready = sem("a_ready")
        h_full = sem("h_full")
        h_hi_ready = sem("h_hi_ready")
        h_lo_ready = sem("h_lo_ready")
        gcol_ready = sem("gcol_ready")
        diag_ready = sem("diag_ready")
        gate_spread = sem("gate_spread")
        gate_ready = sem("gate_ready")
        y_done = sem("y_done")
        y_scaled = sem("y_scaled")
        gu_done = sem("gu_done")
        silu_done = sem("silu_done")
        prod_done = sem("prod_done")
        hid_turned = sem("hid_turned")
        hid_hi_ready = sem("hid_hi_ready")
        hid_lo_ready = sem("hid_lo_ready")
        vec_step = sem("vec_step")
        dtw_landed = sem("dtw_landed")
        dtw_hi = sem("dtw_hi")
        dtw_lo = sem("dtw_lo")
        dt_heads = sem("dt_heads")
        dt_row_ready = sem("dt_row_ready")
        dt_mm = sem("dt_mm")
        dt_x = sem("dt_x")
        dt_abs = sem("dt_abs")
        dt_exp = sem("dt_exp")
        dt_one = sem("dt_one")
        dt_ln = sem("dt_ln")
        exp_a_ready = sem("exp_a_ready")
        adt_ready = sem("adt_ready")
        decay_sums = sem("decay_sums")
        decays_ready = sem("decays_ready")
        q_mm = sem("q_mm")
        q_roped = sem("q_roped")
        k_roped = sem("k_roped")
        v_ready = sem("v_ready")
        q_turned = sem("q_turned")
        k_turned = sem("k_turned")
        q_t_ready = sem("q_t_ready")
        k_t_ready = sem("k_t_ready")
        xbc_mm = sem("xbc_mm")
        conv_begun = sem("conv_begun")
        conv_ready = sem("conv_ready")
        conv_tanh = sem("conv_tanh")
        tanh_plus = sem("tanh_plus")
        xbc_ready = sem("xbc_ready")
        z_mm = sem("z_mm")
        z_tanhed = sem("z_tanhed")
        z_ready = sem("z_ready")
        scores = sem("scores")
        row_max = sem("row_max")
        exps = sem("exps")
        sink_exp = sem("sink_exp")
        probs_ready = sem("probs_ready")
        probs_turned = sem("probs_turned")
        probs_t_ready = sem("probs_t_ready")
        att_mm = sem("att_mm")
        att_ready = sem("att_ready")
        att_hi = sem("att_hi")
        att_lo = sem("att_lo")
        seg_in_ready = sem("seg_in_ready")
        seg_mm = sem("seg_mm")
        seg_exp = sem("seg_exp")
        xs_turned = sem("xs_turned")
        xs_ready = sem("xs_ready")
        xs_dt_ready = sem("xs_dt_ready")
        xs_dec_ready = sem("xs_dec_ready")
        b_turned = sem("b_turned")
        b_ready = sem("b_ready")
        gram_mm = sem("gram_mm")
        gram_ready = sem("gram_ready")
        mix_ready = sem("mix_ready")
        skip_ready = sem("skip_ready")
        state_mm = sem("state_mm")
        state_ready = sem("state_ready")
        diag_mm = sem("diag_mm")
        off_mm = sem("off_mm")
        gated = sem("gated")
        g_squared = sem("g_squared")
        g_rstd = sem("g_rstd")
        ssd_ready = sem("ssd_ready")
        ssd_turned = sem("ssd_turned")
        ssd_full = sem("ssd_full")
        ssd_hi = sem("ssd_hi")
        ssd_lo = sem("ssd_lo")

        block = ctx.enter_context(nc.Block())

        def skip_of(t):
            return nrm[:, t, 4:8, :].rearrange("p k c -> p (k c)")

        def at(l, per_layer, k):
            return l * per_layer + k

        def piece_done(l, q, i=None):
            return at(l, PIECES, STAGES + number(q) + 1) + (0 if i is None else i * RING)

        def wait_apart(eng, signal, value):
            value = value if isinstance(value, int) else eng.to_reg(value)
            eng.wait_ge(kt_zeroed, 1)
            eng.wait_ge(signal, value)

        def wait_block(eng, signal, l, t, q):
            if t == 0:
                eng.wait_ge(signal, at(l, 1, 1))
            else:
                eng.wait_ge(stage_used, piece_done(l, q))

        FFNS = [("ffn1", 0, 0), ("ffn2", 1, Q_FFN2)]
        LAST_PIECE = [Q_MIX - 1, MIX[-1], PLACES - 1]
        ODD, EVEN = slice(64, 128), slice(0, 64)
        WINDOWS = [[(0, 64)], [(0, 128)], [(128, 64), (64, 64)], [(128, 128)]]
        KEYS = [sum(n for _, n in w) for w in WINDOWS]
        V_OF = [0, 0, 2, 1]
        DT_AT, DECAY_AT = 64, 128

        @block.sync
        def _(sp):
            def load(l, q, i, parts):
                n = before(q, RING) if i is None else number(q) - RING
                wait_apart(sp, lo_ready, at(l, PIECES, RING + n + 1) + (0 if i is None else i * RING))
                for dst, src in parts:
                    sp.dma_start(dst, src).then_inc(raw_landed[q % RING], 16)

            def slot(q, pattern, **sizes):
                return raw[:, q % RING, :].rearrange(pattern, **sizes)

            def load_gu(f, l, q, j, half, i=None):
                dst = slot(q, "p (g k n) -> p g k n", g=2, k=4)
                load(l, q, i, [(dst[:, g], a[f + w].rearrange("l (k p) n -> l p k n", p=P)
                                [l, :, 4 * half:4 * half + 4, bass.ds(j * FB, FB)])
                               for g, w in enumerate(("_w_gate", "_w_up"))])

            def load_down(f, l, q, j, i=None):
                dst = slot(q, "p (c n) -> p c n", c=2)
                src = a[f + "_w_down"].rearrange("l (j p) n -> l p j n", p=P)
                load(l, q, i, [(dst[:, c], src[l, :, bass.ds(j * 2 + c, 1), :].rearrange("p j n -> p (j n)"))
                               for c in range(2)])

            def load_ada(pos, slot_no, layer, r):
                wait_apart(sp, ada_step, (pos + 1) * KC)
                sp.dma_start(ada_raw[:, slot_no],
                             a["ada_w"].rearrange("l (k p) n -> l p k n", p=P)
                             [layer, :, :, bass.ds(r * ADA_W, ADA_W)]).then_inc(ada_landed[slot_no], 16)

            def load_first(r):
                if r >= FIRST_RING:
                    sp.wait_ge(first_summed, r - FIRST_RING + 1)
                sp.dma_start(first_raw[r % FIRST_RING], a["ada_w"].rearrange("l (k p) n -> l p k n", p=P)
                             [0, :, :, r * ADA_W:(r + 1) * ADA_W]).then_inc(first_landed[r % FIRST_RING], 16)

            sp.dma_start(c_row[:, :], a["c"].rearrange("b (k p) -> (b k) p", p=P)).then_inc(c_landed, 16)
            sp.dma_start(const[:, :], a["const"]).then_inc(const_landed, 16)
            for r in range(FIRST_RING):
                load_first(r)
            for l in range(DEPTH):
                def rows(name, tile, r0):
                    src = a[name][l]
                    src = src.rearrange("w (k p) -> (w k) p", p=P) if name == "conv_w" else \
                        src.rearrange("(k p) -> k p", p=P)
                    sp.dma_start(tile[r0:r0 + src.shape[0], l, :], src).then_inc(rows_landed, 16)
                rows("ada_b", prow_a, ROW_ADA)
                for s, name in enumerate(("ffn1", "mix", "ffn2")):
                    rows(name + "_norm_pre", prow_a, ROW_PRE[s])
                    rows(name + "_norm_post", prow_a, ROW_POST[s])
                rows("ssd_norm", prow_a, ROW_SSDN)
                rows("conv_b", prow_b, ROW_CONVB)
                rows("conv_w", prow_b, ROW_CONVW)
            for t in range(TB):
                sp.dma_start(x_sb[:, t, :], a["x"][0, t * P:(t + 1) * P, :]).then_inc(x_landed, 16)
            for n, name in enumerate(("dt_bias", "a_log", "d_skip", "attn_sinks")):
                for l in range(DEPTH):
                    sp.dma_start(small[:, l, n, :], a[name][l:l + 1, :].broadcast_to([P, 8])).then_inc(small_landed, 16)
            for r in range(FIRST_RING, ADA_AHEAD):
                load_first(r)

            with sp.Fori(0, DEPTH) as l:
                ada0 = l * ADA_PIECES + ADA_AHEAD
                for f, ff, q0 in FFNS:
                    load_gu(f, l, q0, 0, 0)
                    load_gu(f, l, q0 + 1, 0, 1)
                    if ff:
                        for u in range(ADA_PRO):
                            load_ada(ada0 + (ADA_LOOP1 + ADA_EPI + u), u, l, ADA_AHEAD + ADA_LOOP1 + ADA_EPI + u)
                    if ff == 0:
                        sp.wait_ge(first_summed, ADA_AHEAD)
                    if ff:
                        wait_apart(sp, lo_ready, at(l, PIECES, RING + number(MIX[-1]) + 1))
                    with sp.Fori(0, 5) as i:
                        for u in range(2):
                            q, j = q0 + 2 + 3 * u, i * 2 + (1 + u)
                            load_gu(f, l, q, j, 0, i)
                            load_gu(f, l, q + 1, j, 1, i)
                            if ff == 0:
                                load_ada(i * 4 + (ada0 + 2 * u), 0, l, i * 4 + (ADA_AHEAD + 2 * u))
                            load_down(f, l, q + 2, i * 2 + u, i)
                            if ff == 0:
                                load_ada(i * 4 + (ada0 + (2 * u + 1)), 1, l, i * 4 + (ADA_AHEAD + 2 * u + 1))
                            else:
                                load_ada(i * 2 + (ada0 + (26 + u)), u, 1 - l, i * 2 + u)
                    load_down(f, l, q0 + 32, FSTEPS - 1)
                    if ff == 0:
                        w_in = a["w_in"].rearrange("l (k p) n -> l p k n", p=P)
                        w_out = a["w_out"].rearrange("l (k p) n -> l p k n", p=P)
                        sp.dma_start(w_dt[:, :, :], w_in[l, :, :, COL_DT:COL_DT + SSM_H]).then_inc(dtw_landed, 16)

                        def load_wide(m, col, kh):
                            dst = slot(MIX[m], "p (k n) -> p k n", k=4)
                            load(l, MIX[m], None, [(dst[:, 2 * e:2 * e + 2],
                                 w_in[l, :, 4 * kh + 2 * e:4 * kh + 2 * e + 2, col:col + 512]) for e in range(2)])

                        def load_tall(m, col):
                            dst = slot(MIX[m], "p (k n) -> p k n", k=8)
                            load(l, MIX[m], None, [(dst[:, 4 * e:4 * e + 4],
                                 w_in[l, :, 4 * e:4 * e + 4, col:col + 256]) for e in range(2)])

                        load_wide(0, COL_Q, 0)
                        load_wide(1, COL_Q, 1)
                        load_tall(2, COL_KV)
                        for m in range(4):
                            load_ada(ada0 + (ADA_LOOP1 + m), m % ADA_RING, l, ADA_AHEAD + ADA_LOOP1 + m)
                            load_tall(3 + m, COL_XBC + 256 * m)
                        load_wide(7, COL_Z, 0)
                        load_wide(8, COL_Z, 1)
                        for n, k2 in enumerate((2, 3, 0, 1)):
                            dst = slot(MIX[9 + n], "p (c n) -> p c n", c=2)
                            load(l, MIX[9 + n], None, [(dst[:, c], w_out[l, :, 2 * k2 + c, :]) for c in range(2)])
            sp.wait_ge(x_ready, TB + DEPTH * SITES * TB)
            for t in range(TB):
                sp.dma_start(out[0, t * P:(t + 1) * P, :], x_sb[:, t, :]).then_inc(out_landed, 16)
            sp.wait_ge(out_landed, 16 * TB)

        @block.gpsimd
        def _(pool):
            pool.memset(minus_half[:, :], -0.5).then_inc(half_ready, 1)
            pool.memset(k_t[:, :, :, :], 0.0).then_inc(kt_zeroed, 1)
            pool.wait_ge(half_ready, 1)
            pool.wait_ge(x_landed, 16 * TB)
            pool.sem_inc(x_ready, TB)
            args = Steps(pow_arg, 4 * SITES + TB)

            def power(l, site, which):
                for t in range(TB):
                    k = at(l, SITES * TB, site * TB + t + 1)
                    wait_apart(pool, x_squared if which else y_squared, k)
                    args.link(pool, pool.tensor_scalar(pow_in[:, which, t:t + 1], sq_sum[:, which, t:t + 1],
                                                       EPS, None, ALU.add))
                    pool.tensor_tensor(rstd[:, which, t:t + 1], pow_in[:, which, t:t + 1], minus_half[:, 0:1],
                                       ALU.pow).then_inc(x_rstd if which else y_rstd, 1)

            def ada_reduce(l, p):
                pos, s = l * ADA_PIECES + (ADA_AHEAD + p), p % ADA_RING
                rows = ada_raw[:, s]
                pool.wait_ge(ada_step, (pos + ADA_RING) * KC)
                pool.wait_ge(mod_ready, pos + (1 - ADA_RING))
                pool.wait_ge(ada_landed[s], (l * (ADA_PIECES // 2) + (ADA_AHEAD // FIRST_RING + p // 2 + 1)) * 16)
                pool.tensor_tensor(rows, rows, c_col[:, :].unsqueeze(2).broadcast_to([P, KC, ADA_W]), ALU.mult)\
                    .then_inc(ada_step, 2)
                for n, (dst, k) in enumerate(((rows[:, 0:4], 4), (rows[:, 0:2], 2), (ada_acc[:, s, :], 1))):
                    pool.wait_ge(ada_step, (pos + ADA_RING) * KC + 2 * (n + 1))
                    one = k == 1
                    pool.tensor_tensor(dst, rows[:, 0] if one else rows[:, 0:k], rows[:, 1] if one else rows[:, k:2 * k],
                                       ALU.add).then_inc(ada_step, 2)

            with pool.Fori(0, DEPTH) as l:
                args.begin(l)
                power(l, 0, 1)
                power(l, 0, 0)
                power(l, 1, 1)
                for u in range(ADA_EPI):
                    ada_reduce(l, ADA_LOOP1 + u)
                for ct in range(8):
                    wait_apart(pool, conv_tanh, at(l, 8, ct + 1))
                    pool.tensor_scalar(tanh_sb[:, ct % 2, :], tanh_sb[:, ct % 2, :], 1.0, None, ALU.add)\
                        .then_inc(tanh_plus, 1)
                    pool.wait_ge(tanh_plus, at(l, 8, ct + 1))
                    pool.tensor_tensor(conv[:, ct, :], tanh_sb[:, ct % 2, :], conv[:, ct, :], ALU.mult)\
                        .then_inc(xbc_ready, 1)
                def heads_of(ap):
                    return ap.rearrange("p (h d) -> p h d", d=HEAD)

                def by_head(col):
                    return col.unsqueeze(2).broadcast_to([P, SSM_H, HEAD])

                for t in range(TB):
                    pool.wait_ge(xs_ready, at(l, TB, t + 1))
                    pool.tensor_tensor(heads_of(xs_dt[:, t, :]), heads_of(xs_nat[:, t, :]), by_head(dt_sb[:, t, :]),
                                       ALU.mult).then_inc(xs_dt_ready, 1)
                    pool.wait_ge(xs_dt_ready, at(l, TB, t + 1))
                    pool.tensor_tensor(heads_of(xs_dec[:, t, :]), heads_of(xs_dt[:, t, :]),
                                       by_head(decays[:, t, 0, :]), ALU.mult).then_inc(xs_dec_ready, 1)
                for t in range(TB):
                    pool.wait_ge(seg_exp, at(l, 2 * TB, 2 * t + 2))
                    pool.tensor_tensor(heads_of(skip_of(t)), heads_of(xs_nat[:, t, :]), by_head(cur_small[:, 2, :]),
                                       ALU.mult).then_inc(skip_ready, 1)
                for t in range(TB):
                    wait_apart(pool, g_squared, at(l, TB * GROUPS, GROUPS * (t + 1)))
                    args.link(pool, pool.tensor_scalar(gpow[:, t, :], gsq[:, t, :], EPS, None, ALU.add))
                    pool.tensor_tensor(grstd[:, t, :], gpow[:, t, :], minus_half[:, 0:GROUPS],
                                       ALU.pow).then_inc(g_rstd, 1)
                power(l, 1, 0)
                power(l, 2, 1)
                for u in range(ADA_PRO):
                    ada_reduce(l, ADA_LOOP1 + ADA_EPI + u)
                power(l, 2, 0)
                args.end()

        @block.scalar
        def _(act):
            def hi(l, q, i=None):
                n = before(q, STAGES) if i is None else number(q) - STAGES
                act.wait_ge(raw_landed[q % RING], (l * USES[q % RING] + (uses(q) if i is None else i + uses(q))) * 32)
                act.wait_ge(stage_used, at(l, PIECES, STAGES + n + 1) + (0 if i is None else i * RING))
                nc.scalar.activation(w_hi[:, q % STAGES], raw[:, q % RING], ACT.Copy).then_inc(hi_ready, 1)

            def squares(l, site, which, t):
                if which:
                    act.wait_ge(x_ready, at(l, SITES * TB, site * TB + t + 1))
                    src, signal = x_sb[:, t, :], x_squared
                else:
                    if t == 0:
                        act.wait_ge(y_done, at(l, SITES, site + 1))
                    else:
                        act.wait_ge(stage_used, piece_done(l, LAST_PIECE[site]))
                    src, signal = pair(2 + 2 * t), y_squared
                nc.scalar.activation(nrm[:, t, :, :].rearrange("p k c -> p (k c)"), src, ACT.Square,
                                     scale=D ** -0.5, accum_out=sq_sum[:, which, t:t + 1]).then_inc(signal, 1)

            def h_whole(l, site, t, e):
                act.wait_ge(xn_turned, at(l, 2 * TB * SITES, 2 * TB * site + 2 * t + e + 1))
                for k in range(4 * e, 4 * e + 4):
                    c0 = KC * (3 * site + SHIFT) + k
                    nc.scalar.activation(nrm[:, t, k, :], bank[:, 2 * t + e, (k % 4) * P:(k % 4 + 1) * P],
                                         ACT.Identity, bias=mod[:, c0:c0 + 1], scale=a_col[:, k:k + 1])\
                       .then_inc(h_full, 1)

            def h_high(l, site, t, e):
                act.wait_ge(h_full, at(l, 16 * SITES, 16 * site + 4 * (2 * t + e + 1)))
                nc.scalar.activation(h_hi[:, 4 * e:4 * e + 4, t * P:(t + 1) * P],
                                     nrm[:, t, 4 * e:4 * e + 4, :], ACT.Copy).then_inc(h_hi_ready, 1)

            def operand(l, site, pieces=()):
                squares(l, site, 1, 0)
                squares(l, site, 1, 1)
                for q in pieces:
                    hi(l, q)
                act.wait_ge(a_ready, at(l, SITES, site + 1))
                for t in range(TB):
                    for e in range(2):
                        h_whole(l, site, t, e)
                        h_high(l, site, t, e)

            def gate(l, site, b):
                act.wait_ge(gate_spread, at(l, SITES, site + 1))
                nc.scalar.activation(gate_rows[:, :], pair(b), ACT.Copy).then_inc(gate_ready, 1)

            def silu(l, ff, j, t):
                act.wait_ge(gu_done, at(l, 4 * FSTEPS, 2 * FSTEPS * ff + t + 1) + j * 2)
                nc.scalar.activation(silu_sb[:, t], bank[:, t, 0:FB], ACT.Silu).then_inc(silu_done, 1)

            def hid(l, ff, j):
                act.wait_ge(hid_turned, at(l, 2 * FSTEPS, FSTEPS * ff + 1) + j)
                nc.scalar.activation(hid_hi[:, :, :], bank[:, 6, :].rearrange("p (c t) -> p c t", c=2),
                                     ACT.Copy).then_inc(hid_hi_ready, 1)

            def mixer(l):
                def dt_part():
                    act.wait_ge(dt_heads, at(l, 1, 1))
                    nc.scalar.activation(dt_row[:, :], bank[0:SSM_H, 7, T:2 * T], ACT.Copy).then_inc(dt_row_ready, 1)
                    act.wait_ge(cur_ready, at(l, 5, 5))
                    nc.scalar.activation(exp_a[:, :], cur_small[:, 1, :], ACT.Exp).then_inc(exp_a_ready, 1)
                    hi(l, MIX[4])
                    act.wait_ge(dt_abs, at(l, 1, 1))
                    nc.scalar.activation(soft[:, 3, :], soft[:, 2, :], ACT.Exp, scale=-1.0).then_inc(dt_exp, 1)
                    act.wait_ge(dt_one, at(l, 1, 1))
                    nc.scalar.activation(soft[:, 5, :], soft[:, 4, :], ACT.Ln).then_inc(dt_ln, 1)

                def decay_part():
                    act.wait_ge(decay_sums, at(l, 1, 1))
                    nc.scalar.activation(decays[:, :, :, :], bank[:, 7, DECAY_AT:DECAY_AT + 8 * SSM_H].rearrange(
                        "p (t a h) -> p t a h", t=TB, a=4), ACT.Exp).then_inc(decays_ready, 1)

                def conv_first(ct):
                    w, b = (cur[:, c0 + ct:c0 + ct + 1] for c0 in
                            (ROWS_A + ROW_CONVW + 8 * (CONV_W - 1), ROWS_A + ROW_CONVB))
                    if ct % 2 == 0:
                        act.wait_ge(xbc_mm, at(l, 4, ct // 2 + 1))
                    else:
                        act.wait_ge(stage_used, piece_done(l, MIX[3 + ct // 2]))
                    nc.scalar.activation(conv[:, ct, :], bank[:, ct % 4, 0:T], ACT.Identity, bias=b, scale=w)\
                       .then_inc(conv_begun, 1)

                def tanh(ct):
                    act.wait_ge(conv_ready, at(l, 8, ct + 1))
                    if ct >= 2:
                        act.wait_ge(xbc_ready, at(l, 8, ct - 1))
                    nc.scalar.activation(tanh_sb[:, ct % 2, :], conv[:, ct, :], ACT.Tanh).then_inc(conv_tanh, 1)

                def exp_scores(c):
                    act.wait_ge(row_max, at(l, 4, c + 1))
                    for i in range(4):
                        nc.scalar.activation(probs[:, c % 2, i, 0:KEYS[c]], bank[:, 4 + c % 2, i * P:i * P + KEYS[c]],
                                             ACT.Exp, bias=sm[:, c, 2, i:i + 1], scale=ATT_SCALE,
                                             accum_out=sm[:, c, 3, i:i + 1]).then_inc(exps, 1)
                    nc.scalar.activation(sm[:, c, 4, :], sm[:, c, 1, :], ACT.Exp).then_inc(sink_exp, 1)

                def probs_part(c):
                    act.wait_ge(probs_turned, at(l, 4, c + 1))
                    nc.scalar.activation(probs_t[0:KEYS[c], c % 2, :, :], bank[0:KEYS[c], 6 + c % 2, :].rearrange(
                        "p (i q) -> p i q", i=4), ACT.Copy).then_inc(probs_t_ready, 1)

                def att_part(c):
                    act.wait_ge(att_mm, at(l, 4, c + 1))
                    nc.scalar.activation(att[:, :, 64 * c:64 * c + 64], bank[:, 4 + c % 2, 0:256].rearrange(
                        "p (i q) -> p i q", i=4), ACT.Copy).then_inc(att_ready, 1)

                hi(l, MIX[2])
                hi(l, MIX[3])
                dt_part()
                for t in range(TB):
                    act.wait_ge(stage_used, piece_done(l, MIX[2]))
                    nc.scalar.activation(v_sb[:, t, :], bank[:, 6, 256 * t + 128:256 * t + 256], ACT.Copy)\
                       .then_inc(v_ready, 1)
                for t, half in ((1, EVEN), (0, ODD)):
                    act.wait_ge(v_ready, at(l, TB + 2, TB))
                    nc.scalar.activation(v_sb[half, 2, :], v_sb[half, t, :], ACT.Copy).then_inc(v_ready, 1)
                conv_first(0)
                conv_first(1)
                hi(l, MIX[5])
                decay_part()
                for t in range(TB):
                    act.wait_ge(q_turned, at(l, TB, t + 1))
                    nc.scalar.activation(q_t[:, :, t * P:(t + 1) * P], bank[:, 4 + t, :].rearrange(
                        "p (i q) -> p i q", i=4), ACT.Copy).then_inc(q_t_ready, 1)
                act.wait_ge(k_turned, at(l, 1, 1))
                for e, half in enumerate((EVEN, ODD)):
                    nc.scalar.activation(k_t[half, :, e, :], bank[half, 6, :].rearrange("p (g q) -> p g q", g=2),
                                         ACT.Copy).then_inc(k_t_ready, 1)
                hi(l, MIX[6])
                tanh(0)
                tanh(1)
                conv_first(2)
                conv_first(3)
                exp_scores(0)
                exp_scores(1)
                tanh(2)
                tanh(3)
                conv_first(4)
                conv_first(5)
                probs_part(0)
                probs_part(1)
                hi(l, MIX[7])
                att_part(0)
                att_part(1)
                tanh(4)
                tanh(5)
                conv_first(6)
                conv_first(7)
                exp_scores(2)
                exp_scores(3)
                hi(l, MIX[8])
                tanh(6)
                tanh(7)
                probs_part(2)
                probs_part(3)
                att_part(2)
                att_part(3)
                hi(l, MIX[9])
                for t in range(TB):
                    act.wait_ge(xs_turned, at(l, TB, t + 1))
                    nc.scalar.activation(xs_nat[:, t, :], bank[:, 2 + t, :], ACT.Copy).then_inc(xs_ready, 1)
                for t in range(TB):
                    if t:
                        act.wait_ge(b_turned, at(l, 1, 1))
                        nc.scalar.activation(b_nat[:, :, :], bank[:, 4, :].rearrange("p (t n) -> p t n", t=TB),
                                             ACT.Copy).then_inc(b_ready, 1)
                    for hh in range(2):
                        act.wait_ge(seg_mm, at(l, 2 * TB, 2 * t + hh + 1))
                        nc.scalar.activation(decay_l[:, t, 4 * hh:4 * hh + 4, :], bank[:, 6 + hh, :].rearrange(
                            "p (h s) -> p h s", h=4), ACT.Exp).then_inc(seg_exp, 1)
                for t in range(TB):
                    wait_block(act, z_mm, l, t, MIX[8])
                    if t:
                        act.wait_ge(z_ready, at(l, TB, t))
                    nc.scalar.activation(z_tanh, bank[:, t, :], ACT.Tanh, scale=0.5).then_inc(z_tanhed, 1)
                act.wait_ge(att_ready, at(l, 4, 4))
                nc.scalar.activation(h_hi[:, 4:8, :], att[:, :, :], ACT.Copy).then_inc(att_hi, 1)
                hi(l, MIX[10])
                hi(l, MIX[11])
                for t in range(TB):
                    act.wait_ge(gated, at(l, TB, t + 1))
                    for g in range(GROUPS):
                        nc.scalar.activation(nrm[:, t, 4 + 2 * g:6 + 2 * g, :].rearrange("p k c -> p (k c)"),
                                             xs_dec[:, t, 256 * g:256 * g + 256], ACT.Square,
                                             scale=(D_SSM // GROUPS) ** -0.5,
                                             accum_out=gsq[:, t, g:g + 1]).then_inc(g_squared, 1)
                hi(l, MIX[12])
                for t in range(TB):
                    act.wait_ge(ssd_turned, at(l, TB, t + 1))
                    for k in range(4):
                        nc.scalar.activation(nrm[:, t, k, :], bank[:, t, k * P:(k + 1) * P], ACT.Copy,
                                             scale=cur[:, ROW_SSDN + k:ROW_SSDN + k + 1]).then_inc(ssd_full, 1)
                    act.wait_ge(ssd_full, at(l, 4 * TB, 4 * t + 4))
                    nc.scalar.activation(h_hi[:, 0:4, t * P:(t + 1) * P], nrm[:, t, 0:4, :], ACT.Copy)\
                       .then_inc(ssd_hi, 1)

            act.wait_ge(kt_zeroed, 1)
            nc.scalar.activation(zeros_r[:, :], k_t[:, :, :, :].rearrange("p g e q -> p (g e q)")[:, 0:512],
                                 ACT.Copy).then_inc(zeros_ready, 1)
            act.wait_ge(c_turned, 1)
            nc.scalar.activation(c_col[:, :], bank[:, 0, 0:KC], ACT.Silu).then_inc(c_ready, 1)

            with act.Fori(0, DEPTH) as l:
                for f, ff, q0 in FFNS:
                    site = 2 * ff
                    operand(l, site, (q0, q0 + 1) if ff == 0 else ())
                    with act.Fori(0, 5) as i:
                        for u in range(2):
                            q, j = q0 + 2 + 3 * u, i * 2 + u
                            hi(l, q, i)
                            silu(l, ff, j, 0)
                            silu(l, ff, j, 1)
                            hi(l, q + 1, i)
                            hid(l, ff, j)
                            hi(l, q + 2, i)
                    hi(l, q0 + 32)
                    silu(l, ff, FSTEPS - 1, 0)
                    silu(l, ff, FSTEPS - 1, 1)
                    if ff == 0:
                        hi(l, MIX[0])
                    hid(l, ff, FSTEPS - 1)
                    if ff == 0:
                        hi(l, MIX[1])
                        act.wait_ge(dtw_landed, at(l, 1, 1) * 16)
                        nc.scalar.activation(w_dt_hi[:, :, :], w_dt[:, :, :], ACT.Copy).then_inc(dtw_hi, 1)
                    gate(l, site, 0)
                    squares(l, site, 0, 0)
                    squares(l, site, 0, 1)
                    if ff == 0:
                        operand(l, 1)
                        mixer(l)
                        hi(l, Q_FFN2)
                        gate(l, 1, 6)
                        hi(l, Q_FFN2 + 1)
                        squares(l, 1, 0, 0)
                        squares(l, 1, 0, 1)

        @block.vector
        def _(dve):
            V = nc.vector
            steps = Steps(vec_step, VEC_STEPS)

            def lo(l, q, i=None):
                n = number(q) + 1
                dve.wait_ge(hi_ready, at(l, PIECES, n) + (0 if i is None else i * RING))
                V.tensor_tensor(w_lo[:, q % STAGES], raw[:, q % RING], w_hi[:, q % STAGES], ALU.subtract)\
                 .then_inc(lo_ready, 1)

            def ada_reduce(pos, s, use):
                dve.wait_ge(ada_landed[s], use * 16)
                V.tensor_scalar(ada_acc[:, s, :], ada_raw[:, s, 0, :], c_col[:, 0:1], None, ALU.mult)\
                 .then_inc(ada_step, 1)
                for k in range(1, KC):
                    dve.wait_ge(ada_step, (pos + ADA_RING) * KC + k)
                    V.scalar_tensor_tensor(out=ada_acc[:, s, :], in0=ada_raw[:, s, k, :], scalar=c_col[:, k:k + 1],
                                           in1=ada_acc[:, s, :], op0=ALU.mult, op1=ALU.add).then_inc(ada_step, 1)

            def ada_store(pos, layer, r):
                wait_apart(dve, ada_summed, pos + (1 - ADA_AHEAD))
                bias = pcol[:, layer, bass.ds(r * 2 + ROW_ADA, 2)]
                V.tensor_tensor(mod[:, bass.ds(r * 2, 2)], bank[:, 7, 0:2], bias, ALU.add).then_inc(mod_ready, 1)

            def scale_col(l, site, mods):
                dve.wait_ge(mod_ready, mods)
                c0 = KC * (3 * site + SCALE)
                V.scalar_tensor_tensor(out=a_col[:, :], in0=mod[:, c0:c0 + KC], scalar=1.0,
                                       in1=cur[:, ROW_PRE[site]:ROW_PRE[site] + KC], op0=ALU.add, op1=ALU.mult)\
                 .then_inc(a_ready, 1)

            def gate_diag(l, site, mods, weight):
                dve.wait_ge(mod_ready, mods)
                c0 = KC * (3 * site + GATE)
                V.scalar_tensor_tensor(out=g_col[:, :], in0=mod[:, c0:c0 + KC], scalar=weight,
                                       in1=cur[:, ROW_POST[site]:ROW_POST[site] + KC], op0=ALU.mult, op1=ALU.mult)\
                 .then_inc(gcol_ready, 1)
                dve.wait_ge(gcol_ready, at(l, SITES, site + 1))
                V.tensor_tensor(nrm[:, 0, :, :], ident.unsqueeze(1).broadcast_to([P, KC, P]),
                                g_col[:, :].unsqueeze(2).broadcast_to([P, KC, P]), ALU.mult).then_inc(diag_ready, 1)

            def post(l, site):
                dve.wait_ge(gate_ready, at(l, SITES, site + 1))
                for t in range(TB):
                    k = at(l, SITES * TB, site * TB + t + 1)
                    dve.wait_ge(y_rstd, k)
                    scaled = nrm[:, t, :, :].rearrange("p k c -> p (k c)")
                    V.scalar_tensor_tensor(out=scaled, in0=pair(2 + 2 * t), scalar=rstd[:, 0, t:t + 1],
                                           in1=gate_rows[:, :], op0=ALU.mult, op1=ALU.mult).then_inc(y_scaled, 1)
                    dve.wait_ge(y_scaled, k)
                    V.tensor_tensor(x_sb[:, t, :], x_sb[:, t, :], scaled, ALU.add).then_inc(x_ready, 1)

            def normalise(l, site, t):
                dve.wait_ge(x_rstd, at(l, SITES * TB, site * TB + t + 1))
                V.tensor_scalar(nrm[:, t, :, :].rearrange("p k c -> p (k c)"), x_sb[:, t, :],
                                rstd[:, 1, t:t + 1], None, ALU.mult).then_inc(xn_ready, 1)

            def h_low(l, site, t, e):
                dve.wait_ge(h_hi_ready, at(l, 4 * SITES, 4 * site + 2 * t + e + 1))
                part = h_hi[:, 4 * e:4 * e + 4, t * P:(t + 1) * P]
                V.tensor_tensor(h_lo[:, 4 * e:4 * e + 4, t * P:(t + 1) * P], nrm[:, t, 4 * e:4 * e + 4, :],
                                part, ALU.subtract).then_inc(h_lo_ready, 1)

            def operand(l, site, pieces=()):
                normalise(l, site, 0)
                normalise(l, site, 1)
                for q in pieces:
                    lo(l, q)
                h_low(l, site, 0, 0)
                h_low(l, site, 0, 1)
                h_low(l, site, 1, 0)
                h_low(l, site, 1, 1)

            def product(l, ff, j):
                for t in range(TB):
                    dve.wait_ge(silu_done, at(l, 4 * FSTEPS, 2 * FSTEPS * ff + t + 1) + j * 2)
                    V.tensor_tensor(prod[:, t], silu_sb[:, t], bank[:, t, FB:2 * FB], ALU.mult).then_inc(prod_done, 1)

            def hid_low(l, ff, j):
                dve.wait_ge(hid_hi_ready, at(l, 2 * FSTEPS, FSTEPS * ff + 1) + j)
                V.tensor_tensor(hid_lo[:, :, :], bank[:, 6, :].rearrange("p (c t) -> p c t", c=2), hid_hi[:, :, :],
                                ALU.subtract).then_inc(hid_lo_ready, 1)

            def take_columns(l):
                V.tensor_copy(cur[:, :], pcol[:, bass.ds(l, 1), :].rearrange("p a n -> p (a n)")).then_inc(cur_ready, 1)
                V.tensor_copy(cur_small[:, :, :], small[:, bass.ds(l, 1), :, :].rearrange("p a b n -> p (a b) n"))\
                 .then_inc(cur_ready, 1)
                dve.wait_ge(cur_ready, at(l, 5, 2))
                sinks = cur_small[:, 3, :].rearrange("p (i e) -> p e i", e=2)
                for e, half in enumerate((EVEN, ODD)):
                    V.tensor_copy(cur_sink[half, :], sinks[half, e, :]).then_inc(cur_ready, 1)
                cb = cur[:, ROWS_A:PCOLS]
                V.tensor_scalar(cb, cb, 0.5, None, ALU.mult).then_inc(cur_ready, 1)
                dve.wait_ge(cur_ready, at(l, 5, 5))

            def mixer(l):
                steps.begin(l)

                def link(ins):
                    steps.link(dve, ins)

                def dt_part():
                    bias = cur_small[:, 0, :].unsqueeze(1).broadcast_to([P, TB, SSM_H])
                    v, mx, ab, ex, one, ln, t6, t7 = (soft[:, n, :] for n in range(8))
                    dve.wait_ge(dt_mm, at(l, 1, 1))
                    V.tensor_tensor(v.rearrange("p (t h) -> p t h", t=TB),
                                    bank[:, 7, DT_AT:DT_AT + TB * SSM_H].rearrange("p (t h) -> p t h", t=TB), bias, ALU.add)\
                     .then_inc(dt_x, 1)
                    dve.wait_ge(dt_x, at(l, 1, 1))
                    V.scalar_tensor_tensor(out=ab, in0=v, scalar=-1.0, in1=v, op0=ALU.mult, op1=ALU.max)\
                     .then_inc(dt_abs, 1)
                    link(V.tensor_scalar(mx, v, 0.0, None, ALU.max))
                    dve.wait_ge(dt_exp, at(l, 1, 1))
                    V.tensor_scalar(one, ex, 1.0, None, ALU.add).then_inc(dt_one, 1)
                    dve.wait_ge(dt_one, at(l, 1, 1))
                    link(V.tensor_scalar(t6, one, -1.0, None, ALU.add))
                    link(V.tensor_tensor(t6, ex, t6, ALU.subtract))
                    link(V.reciprocal(t7, one))
                    link(V.tensor_tensor(t6, t6, t7, ALU.mult))
                    link(V.tensor_tensor(t6, t6, mx, ALU.add))
                    dve.wait_ge(dt_ln, at(l, 1, 1))
                    link(V.tensor_tensor(dt_sb[:, :, :].rearrange("p t h -> p (t h)"), ln, t6, ALU.add))
                    dve.wait_ge(exp_a_ready, at(l, 1, 1))
                    V.scalar_tensor_tensor(out=adt[:, :, :], in0=dt_sb[:, :, :], scalar=-1.0,
                                           in1=exp_a[:, :].unsqueeze(1).broadcast_to([P, TB, SSM_H]),
                                           op0=ALU.mult, op1=ALU.mult).then_inc(adt_ready, 1)

                def rope(src, t, heads, outs, signal):
                    v = src.rearrange("p (h d) -> p h d", d=HEAD)
                    cos = const[:, C_COS + t * HEAD:C_COS + (t + 1) * HEAD].unsqueeze(1)
                    sin = const[:, C_SIN + t * HEAD:C_SIN + (t + 1) * HEAD].unsqueeze(1)
                    c_part, s_part = rope_t[:, 0, 0:heads, :], rope_t[:, 1, 0:heads, :]
                    steps.mark(V.tensor_tensor(c_part, v, cos.broadcast_to([P, heads, HEAD]), ALU.mult))
                    for lo_, hi_ in ((0, 32), (32, 0)):
                        steps.mark(V.tensor_tensor(s_part[:, :, lo_:lo_ + 32], v[:, :, hi_:hi_ + 32],
                                                   sin[:, :, lo_:lo_ + 32].broadcast_to([P, heads, 32]), ALU.mult))
                    steps.settle(dve)
                    for dst in outs:
                        ins = V.tensor_tensor(dst, c_part, s_part, ALU.add)
                        ins.then_inc(signal, 1)
                    return ins

                def conv_part(ct):
                    src = bank[:, ct % 4, 0:T]
                    w = [cur[:, ROWS_A + ROW_CONVW + 8 * tap + ct:ROWS_A + ROW_CONVW + 8 * tap + ct + 1]
                         for tap in range(CONV_W)]
                    dve.wait_ge(conv_begun, at(l, 8, ct + 1))
                    for back in range(1, CONV_W):
                        ins = V.scalar_tensor_tensor(out=conv[:, ct, back:T], in0=src[:, 0:T - back],
                                                     scalar=w[CONV_W - 1 - back], in1=conv[:, ct, back:T],
                                                     op0=ALU.mult, op1=ALU.add)
                        if back < CONV_W - 1:
                            link(ins)
                        else:
                            ins.then_inc(conv_ready, 1)

                def soft_max(c):
                    dve.wait_ge(scores, at(l, 4, c + 1))
                    link(V.tensor_reduce(sm[:, c, 0, :], bank[:, 4 + c % 2, :].rearrange("p (i k) -> p i k", i=4)
                                         [:, :, 0:KEYS[c]], AX_X, ALU.max))
                    link(V.scalar_tensor_tensor(out=sm[:, c, 0, :], in0=sm[:, c, 0, :], scalar=ATT_SCALE,
                                                in1=cur_sink[:, :], op0=ALU.mult, op1=ALU.max))
                    link(V.tensor_tensor(sm[:, c, 1, :], cur_sink[:, :], sm[:, c, 0, :], ALU.subtract))
                    V.tensor_scalar(sm[:, c, 2, :], sm[:, c, 0, :], -1.0, None, ALU.mult).then_inc(row_max, 1)

                def soft_divide(c):
                    dve.wait_ge(exps, at(l, 16, 4 * c + 4))
                    dve.wait_ge(sink_exp, at(l, 4, c + 1))
                    link(V.tensor_tensor(sm[:, c, 5, :], sm[:, c, 3, :], sm[:, c, 4, :], ALU.add))
                    link(V.reciprocal(sm[:, c, 5, :], sm[:, c, 5, :]))
                    p = probs[:, c % 2, :, 0:KEYS[c]]
                    V.tensor_tensor(p, p, sm[:, c, 5, :].unsqueeze(2).broadcast_to([P, 4, KEYS[c]]), ALU.mult)\
                     .then_inc(probs_ready, 1)

                def by_head(col):
                    return col.unsqueeze(2).broadcast_to([col.shape[0], SSM_H, HEAD])

                def heads_of(ap):
                    return ap.rearrange("p (h d) -> p h d", d=HEAD)

                def conditioning_store(u):
                    p = ADA_AHEAD + ADA_LOOP1 + u
                    ada_store(l * ADA_PIECES + p, l, p)

                conditioning_store(0)
                lo(l, MIX[2])
                lo(l, MIX[3])
                for t in range(TB):
                    wait_block(dve, q_mm, l, t, MIX[1])
                    if t:
                        dve.wait_ge(q_roped, at(l, TB, t))
                    rope(bank[:, 4 + t, :], t, ATT_H, [q_rot[:, t]], q_roped)
                dt_part()
                lo(l, MIX[4])
                for t in range(TB):
                    dve.wait_ge(v_ready, at(l, TB + 2, TB))
                    if t == 0:
                        dve.wait_ge(q_roped, at(l, TB, TB))
                    else:
                        dve.wait_ge(k_roped, at(l, 2 * TB, 2 * t))
                    rope(bank[:, 6, 256 * t:256 * t + 128], t, KV_H, [k_rot[:, t, :, n, :] for n in range(2)], k_roped)
                conditioning_store(1)
                conditioning_store(2)
                conv_part(0)
                conv_part(1)
                conditioning_store(3)
                lo(l, MIX[5])
                lo(l, MIX[6])
                soft_max(0)
                soft_max(1)
                conv_part(2)
                conv_part(3)
                soft_divide(0)
                soft_divide(1)
                conv_part(4)
                conv_part(5)
                lo(l, MIX[7])
                soft_max(2)
                soft_max(3)
                conv_part(6)
                conv_part(7)
                soft_divide(2)
                soft_divide(3)
                lo(l, MIX[8])
                for t in range(TB):
                    V.tensor_tensor(nrm[:, t, :, :], upto.unsqueeze(1).broadcast_to([P, SSM_H, P]),
                                    adt[:, t, :].unsqueeze(2).broadcast_to([P, SSM_H, P]), ALU.mult)\
                     .then_inc(seg_in_ready, 1)
                lo(l, MIX[9])

                def z_part(t):
                    dve.wait_ge(z_tanhed, at(l, TB, t + 1))
                    V.scalar_tensor_tensor(out=z_silu[:, t, :], in0=z_tanh, scalar=1.0, in1=bank[:, t, :],
                                           op0=ALU.add, op1=ALU.mult).then_inc(z_ready, 1)

                def mix_part(t):
                    dve.wait_ge(seg_exp, at(l, 2 * TB, 2 * t + 2))
                    for g in range(GROUPS):
                        m = decay_l[:, t, 4 * g:4 * g + 4, :]
                        V.tensor_tensor(m, m, gram[:, 2 * t + g, :].unsqueeze(1).broadcast_to([P, 4, P]), ALU.mult)\
                         .then_inc(mix_ready, 1)

                dve.wait_ge(gram_mm, at(l, 1, 1))
                V.tensor_tensor(gram[:, :, :], bank[:, 5, :].rearrange("p (b l) -> p b l", b=4),
                                upto.unsqueeze(1).broadcast_to([P, 4, P]), ALU.mult).then_inc(gram_ready, 1)
                dve.wait_ge(gram_ready, at(l, 1, 1))
                mix_part(0)
                mix_part(1)
                z_part(0)
                dve.wait_ge(state_mm, at(l, 3, 1))
                V.tensor_copy(state[:, 0, :], bank[:, 2, :]).then_inc(state_ready, 1)
                z_part(1)
                for c in (1, 2):
                    dve.wait_ge(state_ready, at(l, 3, c))
                    link(V.tensor_tensor(heads_of(state[:, c, :]), heads_of(state[:, c - 1, :]),
                                         by_head(decays[:, c // 2, 2 + c % 2, :]), ALU.mult))
                    dve.wait_ge(state_mm, at(l, 3, c + 1))
                    V.tensor_tensor(state[:, c, :], state[:, c, :], bank[:, 2 + c, :], ALU.add)\
                     .then_inc(state_ready, 1)
                dve.wait_ge(att_hi, at(l, 1, 1))
                V.tensor_tensor(h_lo[:, 4:8, :], att[:, :, :], h_hi[:, 4:8, :], ALU.subtract).then_inc(att_lo, 1)
                lo(l, MIX[10])
                for t in range(TB):
                    y = xs_dec[:, t, :]
                    tmp = nrm[:, t, 0:4, :].rearrange("p k c -> p (k c)")
                    r = ODD if t == 0 else slice(0, P)
                    dve.wait_ge(skip_ready, at(l, TB, t + 1))
                    dve.wait_ge(diag_mm, at(l, TB, t + 1))
                    link(V.tensor_tensor(y, skip_of(t), bank[:, t, :], ALU.add))
                    dve.wait_ge(off_mm, at(l, TB, t + 1))
                    link(V.tensor_tensor(heads_of(tmp[r]), heads_of(bank[r, 6 + t, :]), by_head(decays[r, t, 1, :]),
                                         ALU.mult))
                    link(V.tensor_tensor(y[r], y[r], tmp[r], ALU.add))
                    V.scalar_tensor_tensor(out=y, in0=y, scalar=0.5, in1=z_silu[:, t, :], op0=ALU.mult,
                                           op1=ALU.mult).then_inc(gated, 1)
                for t in range(TB):
                    dve.wait_ge(g_rstd, at(l, TB, t + 1))
                    for g in range(GROUPS):
                        y = xs_dec[:, t, 256 * g:256 * g + 256]
                        V.tensor_scalar(y, y, grstd[:, t, g:g + 1], None, ALU.mult).then_inc(ssd_ready, 1)
                lo(l, MIX[11])
                lo(l, MIX[12])
                for t in range(TB):
                    dve.wait_ge(ssd_hi, at(l, TB, t + 1))
                    V.tensor_tensor(h_lo[:, 0:4, t * P:(t + 1) * P], nrm[:, t, 0:4, :],
                                    h_hi[:, 0:4, t * P:(t + 1) * P], ALU.subtract).then_inc(ssd_lo, 1)
                steps.end()

            dve.sem_inc(lo_ready, RING)
            dve.sem_inc(ada_step, KC * (ADA_AHEAD + ADA_RING))
            dve.wait_ge(const_landed, 16)
            dve.wait_ge(c_ready, 1)
            for r in range(ADA_AHEAD):
                src, acc = first_raw[r % FIRST_RING], ada_acc[:, r % ADA_RING, :]
                dve.wait_ge(first_landed[r % FIRST_RING], 16 * (r // FIRST_RING + 1))
                if r >= ADA_RING:
                    dve.wait_ge(first_summed, r - ADA_RING + 1)
                V.tensor_scalar(acc, src[:, 0, :], c_col[:, 0:1], None, ALU.mult).then_inc(first_step, 1)
                for k in range(1, FIRST_VEC):
                    dve.wait_ge(first_step, r * FIRST_VEC + k)
                    V.scalar_tensor_tensor(out=acc, in0=src[:, k, :], scalar=c_col[:, k:k + 1], in1=acc,
                                           op0=ALU.mult, op1=ALU.add).then_inc(first_step, 1)
            dve.wait_ge(params_turned, 1)
            V.tensor_copy(pcol[:, :, 0:ROWS_A], bank[:, 1, 0:DEPTH * ROWS_A].rearrange("p (l n) -> p l n", l=DEPTH))\
             .then_inc(pcol_ready, 1)
            V.tensor_copy(pcol[:, :, ROWS_A:PCOLS], bank[:, 2, 0:DEPTH * ROWS_B].rearrange("p (l n) -> p l n", l=DEPTH))\
             .then_inc(pcol_ready, 1)
            dve.wait_ge(pcol_ready, 2)
            dve.wait_ge(first_summed, ADA_AHEAD)
            n = 2 * ADA_AHEAD
            V.tensor_tensor(mod[:, 0:n], bank[:, 7, 0:n], pcol[:, 0, ROW_ADA:ROW_ADA + n], ALU.add)\
             .then_inc(mod_ready, ADA_AHEAD)
            dve.wait_ge(small_landed, 16 * 4 * DEPTH)

            with dve.Fori(0, DEPTH) as l:
                ada0 = l * ADA_PIECES + ADA_AHEAD
                use0 = l * (ADA_PIECES // 2) + ADA_AHEAD // FIRST_RING
                take_columns(l)
                for f, ff, q0 in FFNS:
                    site = 2 * ff
                    scale_col(l, site, ada0 if ff == 0 else ada0 + (ADA_LOOP1 + ADA_EPI))
                    operand(l, site, (q0, q0 + 1) if ff == 0 else ())
                    if ff:
                        for u in range(ADA_PRO):
                            p = ADA_LOOP1 + ADA_EPI + u
                            ada_store(ada0 + p, l, ADA_AHEAD + p)
                    with dve.Fori(0, 5) as i:
                        for u in range(2):
                            q, j = q0 + 2 + 3 * u, i * 2 + u
                            lo(l, q, i)
                            product(l, ff, j)
                            if ff == 0:
                                p, r, use = i * 4 + (ada0 + 2 * u), i * 4 + (ADA_AHEAD + 2 * u), i * 2 + (use0 + u + 1)
                                if u:
                                    ada_store(p - 1, l, r - 1)
                                lo(l, q + 1, i)
                                ada_reduce(p, 0, use)
                                hid_low(l, ff, j)
                                lo(l, q + 2, i)
                                ada_reduce(p + 1, 1, use)
                                ada_store(p, l, r)
                                if u:
                                    ada_store(p + 1, l, r + 1)
                            else:
                                p, r, use = i * 2 + (ada0 + (26 + u)), i * 2 + u, i + (use0 + 14)
                                lo(l, q + 1, i)
                                ada_reduce(p, u, use)
                                hid_low(l, ff, j)
                                lo(l, q + 2, i)
                                ada_store(p, 1 - l, r)
                    gate_diag(l, site, ada0 + (ADA_LOOP1 if ff == 0 else 26), 0.5)
                    lo(l, q0 + 32)
                    product(l, ff, FSTEPS - 1)
                    if ff == 0:
                        lo(l, MIX[0])
                    hid_low(l, ff, FSTEPS - 1)
                    if ff == 0:
                        lo(l, MIX[1])
                        dve.wait_ge(dtw_hi, at(l, 1, 1))
                        V.tensor_tensor(w_dt_lo[:, :, :], w_dt[:, :, :], w_dt_hi[:, :, :], ALU.subtract)\
                         .then_inc(dtw_lo, 1)
                    post(l, site)
                    if ff == 0:
                        scale_col(l, 1, ada0 + ADA_LOOP1)
                        operand(l, 1)
                        mixer(l)
                        gate_diag(l, 1, ada0 + (ADA_LOOP1 + ADA_EPI), 1.0)
                        lo(l, Q_FFN2)
                        lo(l, Q_FFN2 + 1)
                        post(l, 1)

        @block.tensor
        def _(pe):
            MM = nc.tensor.matmul

            def split(dst, xs, ys, start=False, stop=False):
                first = MM(dst, xs[0], ys[0], start=start, stop=False)
                MM(dst, xs[0], ys[1], start=False, stop=False)
                return first, MM(dst, xs[1], ys[0], start=False, stop=stop)

            def weights(l, q, i=None):
                pe.wait_ge(lo_ready, at(l, PIECES, RING + number(q) + 1) + (0 if i is None else i * RING))

            def stage(q, pattern, **sizes):
                return [w[:, q % STAGES, :].rearrange(pattern, **sizes) for w in (w_hi, w_lo)]

            def h_cols(k, t):
                return h_hi[:, k, t * P:(t + 1) * P], h_lo[:, k, t * P:(t + 1) * P]

            def hid_cols(c, t):
                return hid_hi[:, c, t * P:(t + 1) * P], hid_lo[:, c, t * P:(t + 1) * P]

            def h_parts(l, site, t, e):
                pe.wait_ge(h_lo_ready, at(l, 4 * SITES, 4 * site + 2 * t + e + 1))

            def gu_piece(l, ff, q, half, j=None, i=None):
                weights(l, q, i)
                wh, wl = stage(q, "p (g k n) -> p g k n", g=2, k=4)
                for t in range(TB):
                    if i is None:
                        h_parts(l, 2 * ff, t, half)
                    elif half == 0:
                        pe.wait_ge(prod_done, at(l, 4 * FSTEPS, 2 * FSTEPS * ff + t - 1) + j * 2)
                    for k in range(4):
                        _, mm = split(bank[:, t, :], h_cols(4 * half + k, t), (wh[:, :, k, :], wl[:, :, k, :]),
                                      start=(half == 0 and k == 0), stop=(half == 1 and k == 3))
                    if half == 1:
                        mm.then_inc(gu_done, 1)
                if half == 0:
                    mm.then_inc(stage_used, 1)

            def turn_products(l, ff, j):
                for t in range(TB):
                    pe.wait_ge(prod_done, at(l, 4 * FSTEPS, 2 * FSTEPS * ff + t + 1) + j * 2)
                    for c in range(2):
                        o = c * T + t * P
                        mm = nc.tensor.transpose(bank[:, 6, o:o + P], prod[:, t, c * P:(c + 1) * P], ident)
                mm.then_inc(hid_turned, 1)

            def rows_piece(q, cols, start=False, stop=False, frees=False, done=None):
                wh, wl = stage(q, "p (c n) -> p c n", c=2)
                for t in range(TB):
                    for half in range(2):
                        n = slice(512 * half, 512 * half + 512)
                        for c in range(2):
                            first, mm = split(bank[:, 2 + 2 * t + half, :], cols(c, t), (wh[:, c, n], wl[:, c, n]),
                                              start=(start and c == 0), stop=(stop and c == 1))
                            if frees and (t, half, c) == (0, 0, 0):
                                first.then_inc(stage_used, 1)
                    if done is not None and t == 0:
                        mm.then_inc(done, 1)
                mm.then_inc(stage_used, 1)

            def open_y():
                for b in range(2, 6):
                    mm = MM(bank[:, b, :], zeros_r[:, 0:P], zeros_r[:, :], start=True, stop=False)
                    if b == 2:
                        mm.then_inc(stage_used, 1)

            def sum_columns(s):
                for e in range(2):
                    mm = MM(bank[:, 7, e:e + 1], ada_acc[:, s, e * P:(e + 1) * P], ones[:, 0:1], start=True, stop=True)
                mm.then_inc(ada_summed, 1)

            def ada(pos, s):
                pe.wait_ge(ada_step, (pos + (ADA_RING + 1)) * KC)
                pe.wait_ge(mod_ready, pos)
                sum_columns(s)

            def turn_rows(l, site):
                for t in range(TB):
                    pe.wait_ge(xn_ready, at(l, SITES * TB, site * TB + t + 1))
                    for e in range(2):
                        for k in range(4):
                            mm = nc.tensor.transpose(bank[:, 2 * t + e, k * P:(k + 1) * P], nrm[:, t, 4 * e + k, :],
                                                     ident)
                        mm.then_inc(xn_turned, 1)

            def spread_gate(l, site, b):
                pe.wait_ge(diag_ready, at(l, SITES, site + 1))
                for e in range(2):
                    mm = MM(bank[:, b + e, :], ones, nrm[:, 0, 4 * e:4 * e + 4, :], start=True, stop=True)
                mm.then_inc(gate_spread, 1)

            def mixer(l):

                def wide(m, kh, b, signal):
                    weights(l, MIX[m])
                    wh, wl = stage(MIX[m], "p (k n) -> p k n", k=4)
                    for t in range(TB):
                        if m < 2:
                            h_parts(l, 1, t, kh)
                        for k in range(4):
                            _, mm = split(bank[:, b + t, :], h_cols(4 * kh + k, t), (wh[:, k, :], wl[:, k, :]),
                                          start=(kh == 0 and k == 0), stop=(kh == 1 and k == 3))
                        if kh == 1 and t == 0:
                            mm.then_inc(signal, 1)
                    mm.then_inc(stage_used, 1)

                def xbc(m):
                    weights(l, MIX[3 + m])
                    wh, wl = stage(MIX[3 + m], "p (k n) -> p k n", k=KC)
                    for e in range(2):
                        for k in range(KC):
                            cols = slice(e * P, (e + 1) * P)
                            _, mm = split(bank[:, (2 * m + e) % 4, 0:T], (wh[:, k, cols], wl[:, k, cols]),
                                          (h_hi[:, k, :], h_lo[:, k, :]), start=(k == 0), stop=(k == KC - 1))
                        mm.then_inc(stage_used if e else xbc_mm, 1)

                def score(c):
                    for i in range(4):
                        for e in range(2):
                            o = i * P
                            for k0, n in WINDOWS[c]:
                                mm = MM(bank[64 * e:64 * e + 64, 4 + c % 2, o:o + n], q_t[:, i, 64 * c:64 * c + 64],
                                        k_t[:, i // 2, e, k0:k0 + n], start=True, stop=True)
                                o += n
                    mm.then_inc(scores, 1)

                def turn_probs(c):
                    wait_apart(pe, probs_ready, at(l, 4, c + 1))
                    for i in range(4):
                        mm = nc.tensor.transpose(bank[0:KEYS[c], 6 + c % 2, i * P:(i + 1) * P],
                                                 probs[:, c % 2, i, 0:KEYS[c]], ident)
                    mm.then_inc(probs_turned, 1)

                def attend(c):
                    wait_apart(pe, probs_t_ready, at(l, 4, c + 1))
                    n = KEYS[c]
                    for i in range(4):
                        for e in range(2):
                            mm = MM(bank[64 * e:64 * e + 64, 4 + c % 2, 64 * i:64 * i + 64],
                                    v_sb[0:n, V_OF[c], 64 * (i // 2):64 * (i // 2) + 64],
                                    probs_t[0:n, c % 2, i, 64 * e:64 * e + 64], start=True, stop=True)
                    mm.then_inc(att_mm, 1)

                def conditioning(u):
                    ada(l * ADA_PIECES + (ADA_AHEAD + ADA_LOOP1 + u), u % ADA_RING)

                wide(0, 0, 4, None)
                conditioning(0)
                for e in range(2):
                    for t in range(TB):
                        h_parts(l, 1, t, e)
                pe.wait_ge(dtw_lo, at(l, 1, 1))
                pe.wait_ge(mod_ready, l * ADA_PIECES + (ADA_AHEAD + ADA_LOOP1 + 1))
                for k in range(KC):
                    _, mm = split(bank[0:SSM_H, 7, T:2 * T], (w_dt_hi[:, k, :], w_dt_lo[:, k, :]),
                                  (h_hi[:, k, :], h_lo[:, k, :]), start=(k == 0), stop=(k == KC - 1))
                mm.then_inc(dt_heads, 1)
                wide(1, 1, 4, q_mm)
                wait_apart(pe, dt_row_ready, at(l, 1, 1))
                for t in range(TB):
                    o = DT_AT + t * SSM_H
                    mm = nc.tensor.transpose(bank[:, 7, o:o + SSM_H], dt_row[:, t * P:(t + 1) * P],
                                             ident[0:SSM_H, 0:SSM_H])
                mm.then_inc(dt_mm, 1)
                weights(l, MIX[2])
                wh, wl = stage(MIX[2], "p (k n) -> p k n", k=KC)
                for t in range(TB):
                    for k in range(KC):
                        _, mm = split(bank[:, 6, 256 * t:256 * t + 256], h_cols(k, t), (wh[:, k, :], wl[:, k, :]),
                                      start=(k == 0), stop=(k == KC - 1))
                mm.then_inc(stage_used, 1)
                pe.wait_ge(dt_x, at(l, 1, 1))
                conditioning(1)
                xbc(0)
                pe.wait_ge(mod_ready, l * ADA_PIECES + (ADA_AHEAD + ADA_LOOP1 + 2))
                pe.wait_ge(adt_ready, at(l, 1, 1))
                for t in range(TB):
                    for n, c0 in enumerate((C_AFTER, C_UPTO, C_FIRST, C_SECOND)):
                        o = DECAY_AT + (4 * t + n) * SSM_H
                        mm = MM(bank[:, 7, o:o + SSM_H], const[:, c0:c0 + P], adt[:, t, :], start=True, stop=True)
                mm.then_inc(decay_sums, 1)
                for t in range(TB):
                    pe.wait_ge(q_roped, at(l, TB, t + 1))
                    for i in range(4):
                        mm = nc.tensor.transpose(bank[:, 4 + t, i * P:(i + 1) * P],
                                                 q_rot[:, t, 2 * i:2 * i + 2, :].rearrange("p h d -> p (h d)"), ident)
                    mm.then_inc(q_turned, 1)
                pe.wait_ge(k_roped, at(l, 2 * TB, 2 * TB))
                for g in range(KV_H):
                    for t in range(TB):
                        mm = nc.tensor.transpose(bank[:, 6, g * T + t * P:g * T + (t + 1) * P],
                                                 k_rot[:, t, g, :, :].rearrange("p a d -> p (a d)"), ident)
                mm.then_inc(k_turned, 1)
                pe.wait_ge(decays_ready, at(l, 1, 1))
                conditioning(2)
                xbc(1)
                conditioning(3)
                pe.wait_ge(mod_ready, l * ADA_PIECES + (ADA_AHEAD + ADA_LOOP1 + ADA_EPI))
                pe.wait_ge(q_t_ready, at(l, TB, TB))
                pe.wait_ge(k_t_ready, at(l, 2, 2))
                score(0)
                score(1)
                pe.wait_ge(conv_ready, at(l, 8, 2))
                xbc(2)
                pe.wait_ge(conv_ready, at(l, 8, 4))
                xbc(3)
                for c in (0, 1):
                    turn_probs(c)
                attend(0)
                attend(1)
                for c in (2, 3):
                    pe.wait_ge(att_ready, at(l, 4, c - 1))
                    score(c)
                pe.wait_ge(conv_ready, at(l, 8, 6))
                wide(7, 0, 0, None)
                for c in (2, 3):
                    turn_probs(c)
                attend(2)
                attend(3)
                pe.wait_ge(xbc_ready, at(l, 8, 8))
                pe.wait_ge(conv_ready, at(l, 8, 8))
                for t in range(TB):
                    for k in range(4):
                        mm = nc.tensor.transpose(bank[:, 2 + t, k * P:(k + 1) * P], conv[:, k, t * P:(t + 1) * P],
                                                 ident)
                    mm.then_inc(xs_turned, 1)
                def log_decays(t):
                    pe.wait_ge(seg_in_ready, at(l, TB, t + 1))
                    for hh in range(2):
                        if t:
                            pe.wait_ge(seg_exp, at(l, 2 * TB, hh + 1))
                        MM(bank[:, 6 + hh, :], after, nrm[:, t, 4 * hh:4 * hh + 4, :], start=True, stop=True)\
                            .then_inc(seg_mm, 1)

                pe.wait_ge(probs_t_ready, at(l, 4, 4))
                log_decays(0)
                pe.wait_ge(att_ready, at(l, 4, 4))
                for t in range(TB):
                    for g in range(GROUPS):
                        o = (t * GROUPS + g) * P
                        mm = nc.tensor.transpose(bank[:, 4, o:o + P], conv[:, 4 + g, t * P:(t + 1) * P], ident)
                mm.then_inc(b_turned, 1)
                for t in range(TB):
                    for g in range(GROUPS):
                        o = (t * GROUPS + g) * P
                        rows = slice(t * P, (t + 1) * P)
                        mm = MM(bank[:, 5, o:o + P], conv[:, 4 + g, rows], conv[:, 6 + g, rows], start=True, stop=True)
                mm.then_inc(gram_mm, 1)
                log_decays(1)

                wide(8, 1, 0, z_mm)
                pe.wait_ge(xs_ready, at(l, TB, TB))
                pe.wait_ge(b_ready, at(l, 1, 1))
                for c in range(3):
                    pe.wait_ge(xs_dec_ready, at(l, TB, c // 2 + 1))
                    half = ODD if c % 2 else EVEN
                    for g in range(GROUPS):
                        mm = MM(bank[:, 2 + c, 256 * g:256 * g + 256], b_nat[half, c // 2, P * g:P * g + P],
                                xs_dec[half, c // 2, 256 * g:256 * g + 256], start=True, stop=True)
                    mm.then_inc(state_mm, 1)
                for t in range(TB):
                    pe.wait_ge(mix_ready, at(l, 2 * TB, 2 * t + 2))
                    pe.wait_ge(z_ready, at(l, TB, t + 1))
                    for h in range(SSM_H):
                        mm = MM(bank[:, t, 64 * h:64 * h + 64], decay_l[:, t, h, :], xs_dt[:, t, 64 * h:64 * h + 64],
                                start=True, stop=True)
                    mm.then_inc(diag_mm, 1)
                pe.wait_ge(seg_exp, at(l, 2 * TB, 2 * TB))
                for c in range(1, 4):
                    pe.wait_ge(state_ready, at(l, 3, c))
                    for g in range(GROUPS):
                        mm = MM(bank[ODD if c % 2 else EVEN, 6 + c // 2, 256 * g:256 * g + 256],
                                conv[:, 6 + g, 64 * c:64 * c + 64], state[:, c - 1, 256 * g:256 * g + 256],
                                start=True, stop=True)
                    if c != 2:
                        mm.then_inc(off_mm, 1)
                def out_piece(n, k0, **flags):
                    weights(l, MIX[9 + n])
                    rows_piece(MIX[9 + n], lambda c, t: h_cols(k0 + c, t), **flags)

                pe.wait_ge(att_lo, at(l, 1, 1))
                pe.wait_ge(gram_ready, at(l, 1, 1))
                out_piece(0, 4, start=True)
                out_piece(1, 6)
                for t in range(TB):
                    pe.wait_ge(ssd_ready, at(l, 2 * TB, 2 * t + 2))
                    for k in range(4):
                        mm = nc.tensor.transpose(bank[:, t, k * P:(k + 1) * P], xs_dec[:, t, k * P:(k + 1) * P], ident)
                    mm.then_inc(ssd_turned, 1)
                for t in range(TB):
                    pe.wait_ge(ssd_lo, at(l, TB, t + 1))
                out_piece(2, 0)
                spread_gate(l, 1, 6)
                out_piece(3, 2, stop=True, done=y_done)

            pe.sem_inc(stage_used, STAGES)
            pe.wait_ge(const_landed, 16)
            pe.wait_ge(c_landed, 16)
            nc.tensor.transpose(bank[:, 0, 0:KC], c_row[:, :], ident[0:KC, 0:KC]).then_inc(c_turned, 1)
            pe.wait_ge(c_ready, 1)
            for r in range(ADA_AHEAD):
                pe.wait_ge(first_landed[r % FIRST_RING], 16 * (r // FIRST_RING + 1))
                for e in range(2):
                    dst, cols = bank[:, 7, 2 * r + e:2 * r + e + 1], slice(e * P, (e + 1) * P)
                    for k in range(FIRST_VEC, KC):
                        MM(dst, first_raw[r % FIRST_RING][:, k, cols], c_col[:, k:k + 1], start=(k == FIRST_VEC),
                           stop=False)
                    if e == 0:
                        pe.wait_ge(first_step, FIRST_VEC * (r + 1))
                    mm = MM(dst, ada_acc[:, r % ADA_RING, cols], ones[:, 0:1], start=False, stop=True)
                mm.then_inc(first_summed, 1)
            pe.wait_ge(rows_landed, 16 * (10 * DEPTH))
            for l in range(DEPTH):
                nc.tensor.transpose(bank[:, 1, l * ROWS_A:(l + 1) * ROWS_A], prow_a[:, l, :], ident[0:ROWS_A, 0:ROWS_A])
                mm = nc.tensor.transpose(bank[:, 2, l * ROWS_B:(l + 1) * ROWS_B], prow_b[:, l, :],
                                         ident[0:ROWS_B, 0:ROWS_B])
            mm.then_inc(params_turned, 1)
            pe.wait_ge(zeros_ready, 1)
            pe.wait_ge(kt_zeroed, 1)

            with pe.Fori(0, DEPTH) as l:
                ada0 = l * ADA_PIECES + ADA_AHEAD
                for f, ff, q0 in FFNS:
                    site = 2 * ff
                    turn_rows(l, site)
                    gu_piece(l, ff, q0, 0)
                    gu_piece(l, ff, q0 + 1, 1)
                    open_y()
                    if ff:
                        for u in range(ADA_PRO):
                            ada(ada0 + (ADA_LOOP1 + ADA_EPI + u), u)
                    turn_products(l, ff, 0)
                    with pe.Fori(0, 5) as i:
                        for u in range(2):
                            q, j = q0 + 2 + 3 * u, i * 2 + (u + 1)
                            gu_piece(l, ff, q, 0, j, i)
                            ada(i * 4 + (ada0 + 2 * u), 0) if ff == 0 else ada(i * 2 + (ada0 + (26 + u)), u)
                            gu_piece(l, ff, q + 1, 1, j, i)
                            if ff == 0:
                                ada(i * 4 + (ada0 + (2 * u + 1)), 1)
                            weights(l, q + 2, i)
                            pe.wait_ge(hid_lo_ready, at(l, 2 * FSTEPS, FSTEPS * ff) + j)
                            rows_piece(q + 2, hid_cols, frees=True)
                            turn_products(l, ff, j)
                    spread_gate(l, site, 0)
                    weights(l, q0 + 32)
                    pe.wait_ge(hid_lo_ready, at(l, 2 * FSTEPS, FSTEPS * (ff + 1)))
                    rows_piece(q0 + 32, hid_cols, stop=True, done=y_done)
                    if ff == 0:
                        turn_rows(l, 1)
                        mixer(l)


INPUTS = ["x", "c", "ada_w", "ada_b", "ffn1_norm_pre", "ffn1_w_gate", "ffn1_w_up", "ffn1_w_down", "ffn1_norm_post",
          "mix_norm_pre", "w_in", "conv_w", "conv_b", "dt_bias", "a_log", "d_skip", "ssd_norm", "attn_sinks", "w_out",
          "mix_norm_post", "ffn2_norm_pre", "ffn2_w_gate", "ffn2_w_up", "ffn2_w_down", "ffn2_norm_post"]


def kernel(**inputs):
    import concourse.bacc as bacc
    from concourse.bass_utils import run_bass_kernel_spmd

    nc = bacc.Bacc("TRN2", target_bir_lowering=False, num_devices=1, dynamic_dma_scratch_size=1024)
    arrays, aps = {}, {}
    for name in INPUTS:
        arrays[name] = np.ascontiguousarray(inputs[name])
    arrays["const"] = constants()
    for name, v in arrays.items():
        aps[name] = nc.dram_tensor("in_" + name, v.shape, mybir.dt.from_np(v.dtype), kind="ExternalInput").ap()
    out = nc.dram_tensor("out_x", (1, T, D), F32, kind="ExternalOutput").ap()
    trunk(nc, aps, out)
    r = run_bass_kernel_spmd(nc, [{"in_" + name: v for name, v in arrays.items()}], core_ids=[0])
    return r.results[0]["out_x"]
```

```python
from contextlib import ExitStack

import numpy as np

import concourse.bass as bass
from concourse import mybir

ALU = mybir.AluOpType
ACT = mybir.ActivationFunctionType
AX_X = mybir.AxisListType.X
F32 = mybir.dt.float32
F32R = mybir.dt.float32r

P = 128
DEPTH, T, D, FF = 2, 256, 1024, 2816
CHUNK, HEAD, STATE = 64, 64, 128
SSM_H, GROUPS, D_SSM = 8, 2, 512
ATT_H, KV_H = 8, 2
CONV_W, CONV_DIM = 4, 1024
D_IN = D_SSM + CONV_DIM + SSM_H + ATT_H * HEAD + 2 * KV_H * HEAD
EPS = 1e-6
ROPE_THETA = 10000.0
TB = T // P
KC = D // P
FB = 256
FSTEPS = FF // FB
SITES = 3
ATT_SCALE = HEAD ** -0.5

COL_Z, COL_XBC = 0, D_SSM
COL_DT = COL_XBC + CONV_DIM
COL_Q = COL_DT + SSM_H
COL_KV = COL_Q + ATT_H * HEAD

PIECE = 2048
RING, STAGES = 6, 3
FFN_PIECES = 3 * FSTEPS
MIX_PIECES, MIX_PLACES = 13, 18
PLACES = 2 * FFN_PIECES + MIX_PLACES
PIECES = 2 * FFN_PIECES + MIX_PIECES
Q_MIX = FFN_PIECES
Q_FFN2 = FFN_PIECES + MIX_PLACES
assert PLACES % RING == 0 and RING % STAGES == 0 and DEPTH == 2


MIX = [Q_MIX + m for m in (0, 1, 2, 3, 4, 5, 6, 8, 9, 11, 12, 13, 14)]
assert len(MIX) == MIX_PIECES and MIX[-1] < Q_FFN2


def is_piece(q):
    return not Q_MIX <= q % PLACES < Q_FFN2 or q % PLACES in MIX


def number(q):
    return sum(is_piece(p) for p in range(q))


def before(q, ring):
    p = q - ring
    while not is_piece(p):
        p -= ring
    return number(p) if p >= 0 else number(p + PLACES) - PIECES


def uses(q):
    return sum(is_piece(p) for p in range(q % RING, q + 1, RING))


USES = [uses(PLACES - RING + s) for s in range(RING)]

ADA_W = 256
ADA_PIECES = 9 * D // ADA_W
ADA_RING = 2
ADA_AHEAD = 8
ADA_LOOP1, ADA_EPI, ADA_PRO = 20, 4, 2
FIRST_RING = 4
FIRST_VEC = 6
assert ADA_AHEAD % FIRST_RING == 0
ADA_LOOP2 = ADA_LOOP1 + ADA_EPI + ADA_PRO
assert ADA_AHEAD + ADA_LOOP2 + FSTEPS - 1 == ADA_PIECES + ADA_AHEAD and ADA_PIECES % ADA_RING == 0

ROW_ADA = 0
ROW_PRE = [72, 80, 88]
ROW_POST = [96, 104, 112]
ROW_SSDN = 120
ROWS_A = 124
ROW_CONVB, ROW_CONVW = 0, 8
ROWS_B = 8 + 8 * CONV_W
PCOLS = ROWS_A + ROWS_B

C_IDENT, C_AFTER, C_UPTO, C_FIRST, C_SECOND, C_ONES, C_COS, C_SIN = 0, 128, 256, 384, 512, 640, 768, 896
C_WIDTH = 1024
SHIFT, SCALE, GATE = 0, 1, 2


def constants():
    c = np.zeros((P, C_WIDTH), np.float32)
    k, l = np.arange(P)[:, None], np.arange(P)[None, :]
    same = k // CHUNK == l // CHUNK
    c[:, C_IDENT:C_IDENT + P] = k == l
    c[:, C_AFTER:C_AFTER + P] = same & (k > l)
    c[:, C_UPTO:C_UPTO + P] = same & (k <= l)
    c[:, C_FIRST:C_FIRST + P] = k < CHUNK
    c[:, C_SECOND:C_SECOND + P] = k >= CHUNK
    c[:, C_ONES:C_ONES + P] = 1.0
    half = HEAD // 2
    inv_freq = np.float32(ROPE_THETA) ** (-np.arange(half, dtype=np.float32) / np.float32(half))
    ang = np.arange(T, dtype=np.float32)[:, None] * inv_freq[None, :]
    cos, sin = np.cos(ang).astype(np.float32), np.sin(ang).astype(np.float32)
    for t in range(TB):
        rows = slice(t * P, (t + 1) * P)
        c[:, C_COS + t * HEAD:C_COS + (t + 1) * HEAD] = np.concatenate([cos[rows], cos[rows]], 1)
        c[:, C_SIN + t * HEAD:C_SIN + (t + 1) * HEAD] = np.concatenate([-sin[rows], sin[rows]], 1)
    return c


VEC_STEPS = 7 + 3 * 2 * TB + 2 * 8 + 5 * 4 + 2 + 3 * TB


class Steps:

    def __init__(self, sem, per_layer):
        self.sem, self.per_layer = sem, per_layer

    def begin(self, l):
        self.l, self.n = l, 0

    def link(self, eng, ins):
        self.mark(ins)
        self.settle(eng)

    def mark(self, ins):
        ins.then_inc(self.sem, 1)
        self.n += 1

    def settle(self, eng):
        eng.wait_ge(self.sem, self.l * self.per_layer + self.n)

    def end(self):
        assert self.n == self.per_layer, (self.n, self.per_layer)


def trunk(nc, a, out):
    ctx = ExitStack()
    with ctx:
        def sb(name, shape, dt=F32):
            return ctx.enter_context(nc.sbuf_tensor(name, shape, dt))

        def sem(name):
            return ctx.enter_context(nc.semaphore(name))

        raw = sb("raw", [P, RING, PIECE])
        w_hi = sb("w_hi", [P, STAGES, PIECE], F32R)
        w_lo = sb("w_lo", [P, STAGES, PIECE], F32R)
        ada_raw = sb("ada_raw", [P, ADA_RING, KC, ADA_W])
        ada_acc = sb("ada_acc", [P, ADA_RING, ADA_W])
        x_sb = sb("x_sb", [P, TB, D])
        h_hi = sb("h_hi", [P, KC, T], F32R)
        h_lo = sb("h_lo", [P, KC, T], F32R)
        nrm = sb("nrm", [P, TB, KC, P])
        gate_rows = sb("gate_rows", [P, D])
        const = sb("const", [P, C_WIDTH])
        prow_a = sb("prow_a", [ROWS_A, DEPTH, P])
        prow_b = sb("prow_b", [ROWS_B, DEPTH, P])
        c_row = sb("c_row", [KC, P])
        pcol = sb("pcol", [P, DEPTH, PCOLS])
        c_col = sb("c_col", [P, KC])
        small = sb("small", [P, DEPTH, 4, 8])
        cur = sb("cur", [P, PCOLS])
        cur_small = sb("cur_small", [P, 4, 8])
        cur_sink = sb("cur_sink", [P, 4])
        mod = sb("mod", [P, 2 * ADA_PIECES])
        a_col = sb("a_col", [P, KC])
        g_col = sb("g_col", [P, KC])
        sq_x = sb("sq_x", [P, TB])
        sq_y = sb("sq_y", [P, TB, 2])
        rstd = sb("rstd", [P, 2, TB])
        pow_in = sb("pow_in", [P, 2, TB])
        minus_half = sb("minus_half", [P, 4])
        zeros_r = sb("zeros_r", [P, 512], F32R)
        ffn_buf = sb("ffn_buf", [P, 1024])
        silu_sb = ffn_buf[:, 0:TB * FB].rearrange("p (t n) -> p t n", t=TB)
        prod = ffn_buf[:, TB * FB:2 * TB * FB].rearrange("p (t n) -> p t n", t=TB)
        hid_hi = sb("hid_hi", [P, 2, T], F32R)
        hid_lo = sb("hid_lo", [P, 2, T], F32R)
        w_dt_hi = sb("w_dt_hi", [P, KC, SSM_H], F32R)
        w_dt_lo = sb("w_dt_lo", [P, KC, SSM_H], F32R)
        soft = sb("soft", [P, 8, TB * SSM_H])
        w_dt = soft[:, 4:8, :].rearrange("p a (b h) -> p (a b) h", h=SSM_H)
        dt_sb = sb("dt_sb", [P, TB, SSM_H])
        adt = sb("adt", [P, TB, SSM_H])
        exp_a = sb("exp_a", [P, SSM_H])
        decays = sb("decays", [P, TB, 4, SSM_H])
        rope_buf = sb("rope_buf", [P, 2 * SSM_H * P])
        rope_t = rope_buf[:, 0:1024].rearrange("p (a h d) -> p a h d", a=2, d=HEAD)
        q_rot = rope_buf[:, 1024:2048].rearrange("p (t h d) -> p t h d", t=TB, d=HEAD)
        decay_l = rope_buf[:, :].rearrange("p (t h s) -> p t h s", t=TB, s=P)
        k_rot = sb("k_rot", [P, TB, KV_H, 2, HEAD])
        v_sb = sb("v_sb", [P, TB + 1, KV_H * HEAD])
        k_t = sb("k_t", [P, KV_H, 2, T])
        conv = sb("conv", [P, 8, T])
        tanh_b = sb("tanh_b", [P, 512])
        tanh_sb = tanh_b[:, :].rearrange("p (b n) -> p b n", b=2)
        dt_row = tanh_b[0:SSM_H, 0:T]
        b_nat = tanh_b[:, :].rearrange("p (t n) -> p t n", t=TB)
        probs = ffn_buf[:, :].rearrange("p (b i k) -> p b i k", b=2, i=4)
        z_tanh = ffn_buf[:, 0:512]
        gram = ffn_buf[:, 512:1024].rearrange("p (b l) -> p b l", b=4)
        z_silu = sb("z_silu", [P, TB, 512])
        xs_nat = sb("xs_nat", [P, TB, D_SSM])
        xs_dt = sb("xs_dt", [P, TB, D_SSM])
        probs_t = xs_dt[:, :, :].rearrange("p b (i q) -> p b i q", i=4)
        xs_dec = sb("xs_dec", [P, TB, D_SSM])
        q_t = xs_dec[:, :, :].rearrange("p b (i q) -> p (b i) q", i=2)
        state = sb("state", [P, 3, D_SSM])
        att = sb("att", [P, 4, T])
        sm = sb("sm", [P, 4, 6, 4])
        gsq = sb("gsq", [P, TB, GROUPS])
        gpow = sb("gpow", [P, TB, GROUPS])
        grstd = sb("grstd", [P, TB, GROUPS])

        first_raw = [ada_raw[:, 0], ada_raw[:, 1], conv[:, :, :],
                     rope_buf[:, :].rearrange("p (k n) -> p k n", k=KC)]

        bank = ctx.enter_context(nc.psum_tensor("bank", [P, 8, 512], F32))

        ident = const[:, C_IDENT:C_IDENT + P]
        after = const[:, C_AFTER:C_AFTER + P]
        upto = const[:, C_UPTO:C_UPTO + P]
        ones = const[:, C_ONES:C_ONES + P]

        def pair(b):
            return bank[:, b:b + 2, :].rearrange("p a n -> p (a n)")

        x_landed = sem("x_landed")
        const_landed = sem("const_landed")
        c_landed = sem("c_landed")
        rows_landed = sem("rows_landed")
        small_landed = sem("small_landed")
        c_turned = sem("c_turned")
        params_turned = sem("params_turned")
        pcol_ready = sem("pcol_ready")
        c_ready = sem("c_ready")
        zeros_ready = sem("zeros_ready")
        half_ready = sem("half_ready")
        kt_zeroed = sem("kt_zeroed")
        out_landed = sem("out_landed")
        raw_landed = [sem(f"raw_landed{s}") for s in range(RING)]
        hi_ready = sem("hi_ready")
        lo_ready = sem("lo_ready")
        stage_used = sem("stage_used")
        ada_landed = [sem(f"ada_landed{s}") for s in range(ADA_RING)]
        first_landed = ada_landed + [sem(f"first_landed{s}") for s in range(ADA_RING, FIRST_RING)]
        first_step = sem("first_step")
        first_summed = sem("first_summed")
        ada_step = [sem(f"ada_step{s}") for s in range(ADA_RING)]
        ada_summed = sem("ada_summed")
        mod_ready = sem("mod_ready")
        mod_biased = sem("mod_biased")
        cur_ready = sem("cur_ready")
        x_ready = sem("x_ready")
        x_squared = sem("x_squared")
        y_first_squared = sem("y_first_squared")
        y_squared = sem("y_squared")
        y_second_gated = sem("y_second_gated")
        pow_arg = sem("pow_arg")
        x_rstd = sem("x_rstd")
        y_rstd = sem("y_rstd")
        xn_ready = sem("xn_ready")
        xn_turned = sem("xn_turned")
        a_ready = sem("a_ready")
        h_full = sem("h_full")
        h_hi_ready = sem("h_hi_ready")
        h_lo_ready = sem("h_lo_ready")
        gcol_ready = sem("gcol_ready")
        diag_ready = sem("diag_ready")
        gate_spread = sem("gate_spread")
        gate_ready = sem("gate_ready")
        y_done = sem("y_done")
        y_gated = sem("y_gated")
        gu_done = sem("gu_done")
        silu_done = sem("silu_done")
        prod_done = sem("prod_done")
        hid_hi_ready = sem("hid_hi_ready")
        hid_lo_ready = sem("hid_lo_ready")
        vec_step = sem("vec_step")
        dtw_landed = sem("dtw_landed")
        dtw_hi = sem("dtw_hi")
        dtw_lo = sem("dtw_lo")
        dt_heads = sem("dt_heads")
        dt_row_ready = sem("dt_row_ready")
        dt_mm = sem("dt_mm")
        dt_x = sem("dt_x")
        dt_abs = sem("dt_abs")
        dt_exp = sem("dt_exp")
        dt_one = sem("dt_one")
        dt_ln = sem("dt_ln")
        exp_a_ready = sem("exp_a_ready")
        adt_ready = sem("adt_ready")
        decay_sums = sem("decay_sums")
        decays_ready = sem("decays_ready")
        q_mm = sem("q_mm")
        q_roped = sem("q_roped")
        k_roped = sem("k_roped")
        v_ready = sem("v_ready")
        q_turned = sem("q_turned")
        k_turned = sem("k_turned")
        q_t_ready = sem("q_t_ready")
        k_t_ready = sem("k_t_ready")
        xbc_mm = sem("xbc_mm")
        conv_begun = sem("conv_begun")
        conv_ready = sem("conv_ready")
        conv_tanh = sem("conv_tanh")
        tanh_plus = sem("tanh_plus")
        xbc_ready = sem("xbc_ready")
        z_mm = sem("z_mm")
        z_tanhed = sem("z_tanhed")
        z_ready = sem("z_ready")
        scores = sem("scores")
        row_max = sem("row_max")
        exps = sem("exps")
        sink_exp = sem("sink_exp")
        probs_ready = sem("probs_ready")
        probs_turned = sem("probs_turned")
        probs_t_ready = sem("probs_t_ready")
        att_mm = sem("att_mm")
        att_ready = sem("att_ready")
        att_hi = sem("att_hi")
        att_lo = sem("att_lo")
        seg_in_ready = sem("seg_in_ready")
        seg_mm = sem("seg_mm")
        seg_exp = sem("seg_exp")
        xs_turned = sem("xs_turned")
        xs_ready = sem("xs_ready")
        xs_dt_ready = sem("xs_dt_ready")
        xs_dec_ready = sem("xs_dec_ready")
        b_turned = sem("b_turned")
        b_ready = sem("b_ready")
        gram_mm = sem("gram_mm")
        gram_ready = sem("gram_ready")
        mix_ready = sem("mix_ready")
        skip_ready = sem("skip_ready")
        state_mm = sem("state_mm")
        state_ready = sem("state_ready")
        diag_mm = sem("diag_mm")
        off_mm = sem("off_mm")
        gated = sem("gated")
        g_squared = sem("g_squared")
        g_rstd = sem("g_rstd")
        ssd_ready = sem("ssd_ready")
        ssd_turned = sem("ssd_turned")
        ssd_full = sem("ssd_full")
        ssd_hi = sem("ssd_hi")
        ssd_lo = sem("ssd_lo")

        block = ctx.enter_context(nc.Block())

        def turned_bank(site, t, e):
            return 2 * t + e + (0 if site == 1 else 2)

        def skip_of(t):
            return nrm[:, t, 4:8, :].rearrange("p k c -> p (k c)")

        def at(l, per_layer, k):
            return l * per_layer + k

        def piece_done(l, q, i=None):
            return at(l, PIECES, STAGES + number(q) + 1) + (0 if i is None else i * RING)

        def wait_y(eng, l, site, t):
            if t == 0:
                eng.wait_ge(y_done, at(l, SITES, site + 1))
            else:
                eng.wait_ge(stage_used, piece_done(l, LAST_PIECE[site]))

        FIRST_USE = ADA_AHEAD // FIRST_RING + 1

        def ada_use(l, p):
            return l * (ADA_PIECES // ADA_RING) + (FIRST_USE + p // ADA_RING)

        def wait_apart(eng, signal, value):
            value = value if isinstance(value, int) else eng.to_reg(value)
            eng.wait_ge(kt_zeroed, 1)
            eng.wait_ge(signal, value)

        def wait_block(eng, signal, l, t, q):
            if t == 0:
                eng.wait_ge(signal, at(l, 1, 1))
            else:
                eng.wait_ge(stage_used, piece_done(l, q))

        FFNS = [("ffn1", 0, 0), ("ffn2", 1, Q_FFN2)]
        LAST_PIECE = [Q_MIX - 1, MIX[-1], PLACES - 1]
        ODD, EVEN = slice(64, 128), slice(0, 64)
        WINDOWS = [[(0, 64)], [(0, 128)], [(128, 64), (64, 64)], [(128, 128)]]
        KEYS = [sum(n for _, n in w) for w in WINDOWS]
        V_OF = [0, 0, 2, 1]
        DT_AT, DECAY_AT = 64, 128

        @block.sync
        def _(sp):
            def load(l, q, i, parts):
                n = before(q, RING) if i is None else number(q) - RING
                wait_apart(sp, lo_ready, at(l, PIECES, RING + n + 1) + (0 if i is None else i * RING))
                for dst, src in parts:
                    sp.dma_start(dst, src).then_inc(raw_landed[q % RING], 16)

            def slot(q, pattern, **sizes):
                return raw[:, q % RING, :].rearrange(pattern, **sizes)

            def load_gu(f, l, q, j, half, i=None):
                dst = slot(q, "p (g k n) -> p g k n", g=2, k=4)
                load(l, q, i, [(dst[:, g], a[f + w].rearrange("l (k p) n -> l p k n", p=P)
                                [l, :, 4 * half:4 * half + 4, bass.ds(j * FB, FB)])
                               for g, w in enumerate(("_w_gate", "_w_up"))])

            def load_down(f, l, q, j, i=None):
                dst = slot(q, "p (c n) -> p c n", c=2)
                src = a[f + "_w_down"].rearrange("l (j p) n -> l p j n", p=P)
                load(l, q, i, [(dst[:, c], src[l, :, bass.ds(j * 2 + c, 1), :].rearrange("p j n -> p (j n)"))
                               for c in range(2)])

            def load_ada(use, slot_no, layer, r):
                wait_apart(sp, ada_step[slot_no], use * KC)
                sp.dma_start(ada_raw[:, slot_no],
                             a["ada_w"].rearrange("l (k p) n -> l p k n", p=P)
                             [layer, :, :, bass.ds(r * ADA_W, ADA_W)]).then_inc(ada_landed[slot_no], 16)

            def load_first(r):
                if r >= FIRST_RING:
                    sp.wait_ge(first_summed, r - FIRST_RING + 1)
                sp.dma_start(first_raw[r % FIRST_RING], a["ada_w"].rearrange("l (k p) n -> l p k n", p=P)
                             [0, :, :, r * ADA_W:(r + 1) * ADA_W]).then_inc(first_landed[r % FIRST_RING], 16)

            sp.dma_start(c_row[:, :], a["c"].rearrange("b (k p) -> (b k) p", p=P)).then_inc(c_landed, 16)
            sp.dma_start(const[:, :], a["const"]).then_inc(const_landed, 16)
            for r in range(FIRST_RING):
                load_first(r)
            for l in range(DEPTH):
                def rows(name, tile, r0):
                    src = a[name][l]
                    src = src.rearrange("w (k p) -> (w k) p", p=P) if name == "conv_w" else \
                        src.rearrange("(k p) -> k p", p=P)
                    sp.dma_start(tile[r0:r0 + src.shape[0], l, :], src).then_inc(rows_landed, 16)
                rows("ada_b", prow_a, ROW_ADA)
                for s, name in enumerate(("ffn1", "mix", "ffn2")):
                    rows(name + "_norm_pre", prow_a, ROW_PRE[s])
                    rows(name + "_norm_post", prow_a, ROW_POST[s])
                rows("ssd_norm", prow_a, ROW_SSDN)
                rows("conv_b", prow_b, ROW_CONVB)
                rows("conv_w", prow_b, ROW_CONVW)
            for t in range(TB):
                sp.dma_start(x_sb[:, t, :], a["x"][0, t * P:(t + 1) * P, :]).then_inc(x_landed, 16)
            for n, name in enumerate(("dt_bias", "a_log", "d_skip", "attn_sinks")):
                for l in range(DEPTH):
                    sp.dma_start(small[:, l, n, :], a[name][l:l + 1, :].broadcast_to([P, 8])).then_inc(small_landed, 16)
            for r in range(FIRST_RING, ADA_AHEAD):
                load_first(r)

            with sp.Fori(0, DEPTH) as l:
                for f, ff, q0 in FFNS:
                    load_gu(f, l, q0, 0, 0)
                    load_gu(f, l, q0 + 1, 0, 1)
                    if ff:
                        for u in range(ADA_PRO):
                            load_ada(ada_use(l, ADA_LOOP1 + ADA_EPI + u), u, l, ADA_AHEAD + ADA_LOOP1 + ADA_EPI + u)
                    if ff == 0:
                        sp.wait_ge(first_summed, ADA_AHEAD)
                    if ff:
                        wait_apart(sp, lo_ready, at(l, PIECES, RING + number(MIX[-1]) + 1))
                    with sp.Fori(0, 5) as i:
                        for u in range(2):
                            q, j = q0 + 2 + 3 * u, i * 2 + (1 + u)
                            load_gu(f, l, q, j, 0, i)
                            load_gu(f, l, q + 1, j, 1, i)
                            if ff == 0:
                                load_ada(i * 2 + ada_use(l, 2 * u), 0, l, i * 4 + (ADA_AHEAD + 2 * u))
                            load_down(f, l, q + 2, i * 2 + u, i)
                            if ff == 0:
                                load_ada(i * 2 + ada_use(l, 2 * u), 1, l, i * 4 + (ADA_AHEAD + 2 * u + 1))
                            else:
                                g = i * 2 + (ADA_AHEAD + ADA_LOOP2 + u)
                                load_ada(i + ada_use(l, ADA_LOOP2), u, (l + g // ADA_PIECES) % DEPTH, g % ADA_PIECES)
                    load_down(f, l, q0 + 32, FSTEPS - 1)
                    if ff == 0:
                        w_in = a["w_in"].rearrange("l (k p) n -> l p k n", p=P)
                        w_out = a["w_out"].rearrange("l (k p) n -> l p k n", p=P)
                        sp.dma_start(w_dt[:, :, :], w_in[l, :, :, COL_DT:COL_DT + SSM_H]).then_inc(dtw_landed, 16)

                        def load_wide(m, col, kh):
                            dst = slot(MIX[m], "p (k n) -> p k n", k=4)
                            load(l, MIX[m], None, [(dst[:, 2 * e:2 * e + 2],
                                 w_in[l, :, 4 * kh + 2 * e:4 * kh + 2 * e + 2, col:col + 512]) for e in range(2)])

                        def load_tall(m, col):
                            dst = slot(MIX[m], "p (k n) -> p k n", k=8)
                            load(l, MIX[m], None, [(dst[:, 4 * e:4 * e + 4],
                                 w_in[l, :, 4 * e:4 * e + 4, col:col + 256]) for e in range(2)])

                        load_wide(0, COL_Q, 0)
                        load_wide(1, COL_Q, 1)
                        load_tall(2, COL_KV)
                        for m in range(4):
                            load_ada(ada_use(l, ADA_LOOP1 + m), m % ADA_RING, l, ADA_AHEAD + ADA_LOOP1 + m)
                            load_tall(3 + m, COL_XBC + 256 * m)
                        load_wide(7, COL_Z, 0)
                        load_wide(8, COL_Z, 1)
                        for n, k2 in enumerate((2, 3, 0, 1)):
                            dst = slot(MIX[9 + n], "p (c n) -> p c n", c=2)
                            load(l, MIX[9 + n], None, [(dst[:, c], w_out[l, :, 2 * k2 + c, :]) for c in range(2)])
            for t in range(TB):
                sp.wait_ge(x_ready, DEPTH * SITES * TB + t + 1)
                sp.dma_start(out[0, t * P:(t + 1) * P, :], x_sb[:, t, :]).then_inc(out_landed, 16)
            sp.wait_ge(out_landed, 16 * TB)

        @block.gpsimd
        def _(pool):
            pool.memset(minus_half[:, :], -0.5).then_inc(half_ready, 1)
            pool.memset(k_t[:, :, :, :], 0.0).then_inc(kt_zeroed, 1)
            pool.wait_ge(half_ready, 1)
            pool.wait_ge(x_landed, 16 * TB)
            pool.sem_inc(x_ready, TB)
            args = Steps(pow_arg, 4 * SITES + TB)

            def power(l, site, which):
                for t in range(TB):
                    k = at(l, SITES * TB, site * TB + t + 1)
                    wait_apart(pool, x_squared if which else y_squared, k)
                    if which:
                        ins = pool.tensor_scalar(pow_in[:, 1, t:t + 1], sq_x[:, t:t + 1], EPS, None, ALU.add)
                    else:
                        ins = pool.tensor_scalar(pow_in[:, 0, t:t + 1], sq_y[:, t, 0:1], sq_y[:, t, 1:2], EPS,
                                                 ALU.add, ALU.add)
                    args.link(pool, ins)
                    pool.tensor_tensor(rstd[:, which, t:t + 1], pow_in[:, which, t:t + 1], minus_half[:, 0:1],
                                       ALU.pow).then_inc(x_rstd if which else y_rstd, 1)

            def ada_reduce(pos, s, use):
                rows = ada_raw[:, s]
                pool.wait_ge(mod_ready, pos + (1 - ADA_RING))
                pool.wait_ge(ada_landed[s], use * 16)
                pool.tensor_tensor(rows, rows, c_col[:, :].unsqueeze(2).broadcast_to([P, KC, ADA_W]), ALU.mult)\
                    .then_inc(ada_step[s], 2)
                for n, (dst, a_half, b_half) in enumerate(((rows[:, 0:4], rows[:, 0:4], rows[:, 4:8]),
                                                           (rows[:, 0:2], rows[:, 0:2], rows[:, 2:4]),
                                                           (ada_acc[:, s, :], rows[:, 0], rows[:, 1]))):
                    pool.wait_ge(ada_step[s], use * KC + 2 * (n + 1))
                    pool.tensor_tensor(dst, a_half, b_half, ALU.add).then_inc(ada_step[s], 2)

            def ada_apart(l, p):
                ada_reduce(l * ADA_PIECES + (ADA_AHEAD + p), p % ADA_RING, ada_use(l, p))

            with pool.Fori(0, DEPTH) as l:
                args.begin(l)
                power(l, 0, 1)
                with pool.Fori(0, 5) as i:
                    for u in range(2):
                        ada_reduce(i * 4 + (l * ADA_PIECES + (ADA_AHEAD + 2 * u + 1)), 1, i * 2 + ada_use(l, 2 * u))
                power(l, 0, 0)
                power(l, 1, 1)
                for u in range(ADA_EPI):
                    ada_apart(l, ADA_LOOP1 + u)
                for ct in range(8):
                    wait_apart(pool, conv_tanh, at(l, 8, ct + 1))
                    pool.tensor_scalar(tanh_sb[:, ct % 2, :], tanh_sb[:, ct % 2, :], 1.0, None, ALU.add)\
                        .then_inc(tanh_plus, 1)
                    pool.wait_ge(tanh_plus, at(l, 8, ct + 1))
                    pool.tensor_tensor(conv[:, ct, :], tanh_sb[:, ct % 2, :], conv[:, ct, :], ALU.mult)\
                        .then_inc(xbc_ready, 1)
                def heads_of(ap):
                    return ap.rearrange("p (h d) -> p h d", d=HEAD)

                def by_head(col):
                    return col.unsqueeze(2).broadcast_to([P, SSM_H, HEAD])

                for t in range(TB):
                    pool.wait_ge(xs_ready, at(l, TB, t + 1))
                    pool.tensor_tensor(heads_of(xs_dt[:, t, :]), heads_of(xs_nat[:, t, :]), by_head(dt_sb[:, t, :]),
                                       ALU.mult).then_inc(xs_dt_ready, 1)
                    pool.wait_ge(xs_dt_ready, at(l, TB, t + 1))
                    pool.tensor_tensor(heads_of(xs_dec[:, t, :]), heads_of(xs_dt[:, t, :]),
                                       by_head(decays[:, t, 0, :]), ALU.mult).then_inc(xs_dec_ready, 1)
                for t in range(TB):
                    pool.wait_ge(seg_exp, at(l, 2 * TB, 2 * t + 2))
                    pool.tensor_tensor(heads_of(skip_of(t)), heads_of(xs_nat[:, t, :]), by_head(cur_small[:, 2, :]),
                                       ALU.mult).then_inc(skip_ready, 1)
                for t in range(TB):
                    wait_apart(pool, g_squared, at(l, TB * GROUPS, GROUPS * (t + 1)))
                    args.link(pool, pool.tensor_scalar(gpow[:, t, :], gsq[:, t, :], EPS, None, ALU.add))
                    pool.tensor_tensor(grstd[:, t, :], gpow[:, t, :], minus_half[:, 0:GROUPS],
                                       ALU.pow).then_inc(g_rstd, 1)
                power(l, 1, 0)
                power(l, 2, 1)
                for u in range(ADA_PRO):
                    ada_apart(l, ADA_LOOP1 + ADA_EPI + u)
                power(l, 2, 0)
                args.end()

        @block.scalar
        def _(act):
            def hi(l, q, i=None):
                n = before(q, STAGES) if i is None else number(q) - STAGES
                act.wait_ge(raw_landed[q % RING], (l * USES[q % RING] + (uses(q) if i is None else i + uses(q))) * 32)
                act.wait_ge(stage_used, at(l, PIECES, STAGES + n + 1) + (0 if i is None else i * RING))
                nc.scalar.activation(w_hi[:, q % STAGES], raw[:, q % RING], ACT.Copy).then_inc(hi_ready, 1)

            def x_squares(l, site, t):
                act.wait_ge(x_ready, at(l, SITES * TB, site * TB + t + 1))
                nc.scalar.activation(nrm[:, t, :, :].rearrange("p k c -> p (k c)"), x_sb[:, t, :], ACT.Square,
                                     scale=D ** -0.5, accum_out=sq_x[:, t:t + 1]).then_inc(x_squared, 1)

            def y_squares(l, site, t):
                k = at(l, SITES * TB, site * TB + t + 1)
                wait_y(act, l, site, t)
                if t:
                    act.wait_ge(y_squared, k - 1)
                else:
                    act.wait_ge(gate_ready, at(l, SITES, site + 1))
                nc.scalar.activation(bank[:, 6, :], bank[:, 2 + 2 * t, :], ACT.Square,
                                     scale=D ** -0.5, accum_out=sq_y[:, t, 0:1]).then_inc(y_first_squared, 1)
                act.wait_ge(y_second_gated, k)
                act.wait_ge(y_first_squared, k)
                nc.scalar.activation(bank[:, 6, :], bank[:, 3 + 2 * t, :], ACT.Square,
                                     scale=D ** -0.5, accum_out=sq_y[:, t, 1:2]).then_inc(y_squared, 1)

            def h_whole(l, site, t, e):
                act.wait_ge(xn_turned, at(l, 2 * TB * SITES, 2 * TB * site + 2 * t + e + 1))
                for k in range(4 * e, 4 * e + 4):
                    c0 = KC * (3 * site + SHIFT) + k
                    nc.scalar.activation(nrm[:, t, k, :], bank[:, turned_bank(site, t, e), (k % 4) * P:(k % 4 + 1) * P],
                                         ACT.Identity, bias=mod[:, c0:c0 + 1], scale=a_col[:, k:k + 1])\
                       .then_inc(h_full, 1)

            def h_high(l, site, t, e):
                act.wait_ge(h_full, at(l, 16 * SITES, 16 * site + 4 * (2 * e + t + 1)))
                nc.scalar.activation(h_hi[:, 4 * e:4 * e + 4, t * P:(t + 1) * P],
                                     nrm[:, t, 4 * e:4 * e + 4, :], ACT.Copy).then_inc(h_hi_ready, 1)

            def operand(l, site, first=None, second=None, middle=None):
                x_squares(l, site, 0)
                if middle is not None:
                    hi(l, middle)
                x_squares(l, site, 1)
                if first is not None:
                    hi(l, first)
                act.wait_ge(a_ready, at(l, SITES, site + 1))
                for e in range(2):
                    for t in range(TB):
                        h_whole(l, site, t, e)
                        h_high(l, site, t, e)
                    if e == 0 and second is not None:
                        hi(l, second)

            def gate(l, site, b):
                act.wait_ge(gate_spread, at(l, SITES, site + 1))
                nc.scalar.activation(gate_rows[:, :], pair(b), ACT.Copy).then_inc(gate_ready, 1)

            def silu(l, ff, j, t):
                act.wait_ge(gu_done, at(l, 4 * FSTEPS, 2 * FSTEPS * ff + t + 1) + j * 2)
                nc.scalar.activation(silu_sb[:, t], bank[:, t, 0:FB], ACT.Silu).then_inc(silu_done, 1)

            def hid(l, ff, j, q, i=None):
                act.wait_ge(prod_done, at(l, 4 * FSTEPS, 2 * FSTEPS * ff + 2) + j * 2)
                act.wait_ge(stage_used, piece_done(l, q, i))
                nc.scalar.activation(hid_hi[:, :, :], prod[:, :, :], ACT.Copy).then_inc(hid_hi_ready, 1)

            def mixer(l):
                def dt_part():
                    act.wait_ge(dt_heads, at(l, 1, 1))
                    nc.scalar.activation(dt_row[:, :], bank[0:SSM_H, 7, T:2 * T], ACT.Copy).then_inc(dt_row_ready, 1)
                    act.wait_ge(cur_ready, at(l, 5, 5))
                    nc.scalar.activation(exp_a[:, :], cur_small[:, 1, :], ACT.Exp).then_inc(exp_a_ready, 1)
                    hi(l, MIX[4])
                    act.wait_ge(dt_abs, at(l, 1, 1))
                    nc.scalar.activation(soft[:, 3, :], soft[:, 2, :], ACT.Exp, scale=-1.0).then_inc(dt_exp, 1)
                    act.wait_ge(dt_one, at(l, 1, 1))
                    nc.scalar.activation(soft[:, 5, :], soft[:, 4, :], ACT.Ln).then_inc(dt_ln, 1)

                def decay_part():
                    act.wait_ge(decay_sums, at(l, 1, 1))
                    nc.scalar.activation(decays[:, :, :, :], bank[:, 7, DECAY_AT:DECAY_AT + 8 * SSM_H].rearrange(
                        "p (t a h) -> p t a h", t=TB, a=4), ACT.Exp).then_inc(decays_ready, 1)

                def conv_first(ct):
                    w, b = (cur[:, c0 + ct:c0 + ct + 1] for c0 in
                            (ROWS_A + ROW_CONVW + 8 * (CONV_W - 1), ROWS_A + ROW_CONVB))
                    if ct % 2 == 0:
                        act.wait_ge(xbc_mm, at(l, 4, ct // 2 + 1))
                    else:
                        act.wait_ge(stage_used, piece_done(l, MIX[3 + ct // 2]))
                    nc.scalar.activation(conv[:, ct, :], bank[:, ct % 4, 0:T], ACT.Identity, bias=b, scale=w)\
                       .then_inc(conv_begun, 1)

                def tanh(ct):
                    act.wait_ge(conv_ready, at(l, 8, ct + 1))
                    if ct >= 2:
                        act.wait_ge(xbc_ready, at(l, 8, ct - 1))
                    nc.scalar.activation(tanh_sb[:, ct % 2, :], conv[:, ct, :], ACT.Tanh).then_inc(conv_tanh, 1)

                def exp_scores(c):
                    act.wait_ge(row_max, at(l, 4, c + 1))
                    for i in range(4):
                        nc.scalar.activation(probs[:, c % 2, i, 0:KEYS[c]], bank[:, 4 + c % 2, i * P:i * P + KEYS[c]],
                                             ACT.Exp, bias=sm[:, c, 2, i:i + 1], scale=ATT_SCALE,
                                             accum_out=sm[:, c, 3, i:i + 1]).then_inc(exps, 1)
                    nc.scalar.activation(sm[:, c, 4, :], sm[:, c, 1, :], ACT.Exp).then_inc(sink_exp, 1)

                def probs_part(c):
                    act.wait_ge(probs_turned, at(l, 4, c + 1))
                    nc.scalar.activation(probs_t[0:KEYS[c], c % 2, :, :], bank[0:KEYS[c], 6 + c % 2, :].rearrange(
                        "p (i q) -> p i q", i=4), ACT.Copy).then_inc(probs_t_ready, 1)

                def att_part(c):
                    act.wait_ge(att_mm, at(l, 4, c + 1))
                    nc.scalar.activation(att[:, :, 64 * c:64 * c + 64], bank[:, 4 + c % 2, 0:256].rearrange(
                        "p (i q) -> p i q", i=4), ACT.Copy).then_inc(att_ready, 1)

                hi(l, MIX[2])
                hi(l, MIX[3])
                dt_part()
                for t in range(TB):
                    act.wait_ge(stage_used, piece_done(l, MIX[2]))
                    nc.scalar.activation(v_sb[:, t, :], bank[:, 6, 256 * t + 128:256 * t + 256], ACT.Copy)\
                       .then_inc(v_ready, 1)
                for t, half in ((1, EVEN), (0, ODD)):
                    act.wait_ge(v_ready, at(l, TB + 2, TB))
                    nc.scalar.activation(v_sb[half, 2, :], v_sb[half, t, :], ACT.Copy).then_inc(v_ready, 1)
                conv_first(0)
                conv_first(1)
                hi(l, MIX[5])
                decay_part()
                for t in range(TB):
                    act.wait_ge(q_turned, at(l, TB, t + 1))
                    nc.scalar.activation(q_t[:, :, t * P:(t + 1) * P], bank[:, 4 + t, :].rearrange(
                        "p (i q) -> p i q", i=4), ACT.Copy).then_inc(q_t_ready, 1)
                act.wait_ge(k_turned, at(l, 1, 1))
                for e, half in enumerate((EVEN, ODD)):
                    nc.scalar.activation(k_t[half, :, e, :], bank[half, 6, :].rearrange("p (g q) -> p g q", g=2),
                                         ACT.Copy).then_inc(k_t_ready, 1)
                hi(l, MIX[6])
                tanh(0)
                tanh(1)
                conv_first(2)
                conv_first(3)
                exp_scores(0)
                exp_scores(1)
                tanh(2)
                tanh(3)
                conv_first(4)
                conv_first(5)
                probs_part(0)
                probs_part(1)
                hi(l, MIX[7])
                att_part(0)
                att_part(1)
                tanh(4)
                tanh(5)
                conv_first(6)
                conv_first(7)
                exp_scores(2)
                exp_scores(3)
                hi(l, MIX[8])
                tanh(6)
                tanh(7)
                probs_part(2)
                probs_part(3)
                att_part(2)
                att_part(3)
                hi(l, MIX[9])
                for t in range(TB):
                    act.wait_ge(xs_turned, at(l, TB, t + 1))
                    nc.scalar.activation(xs_nat[:, t, :], bank[:, 2 + t, :], ACT.Copy).then_inc(xs_ready, 1)
                for t in range(TB):
                    if t:
                        act.wait_ge(b_turned, at(l, 1, 1))
                        nc.scalar.activation(b_nat[:, :, :], bank[:, 4, :].rearrange("p (t n) -> p t n", t=TB),
                                             ACT.Copy).then_inc(b_ready, 1)
                    for hh in range(2):
                        act.wait_ge(seg_mm, at(l, 2 * TB, 2 * t + hh + 1))
                        nc.scalar.activation(decay_l[:, t, 4 * hh:4 * hh + 4, :], bank[:, 6 + hh, :].rearrange(
                            "p (h s) -> p h s", h=4), ACT.Exp).then_inc(seg_exp, 1)
                for t in range(TB):
                    wait_block(act, z_mm, l, t, MIX[8])
                    if t:
                        act.wait_ge(z_ready, at(l, TB, t))
                    nc.scalar.activation(z_tanh, bank[:, t, :], ACT.Tanh, scale=0.5).then_inc(z_tanhed, 1)
                act.wait_ge(att_ready, at(l, 4, 4))
                nc.scalar.activation(h_hi[:, 4:8, :], att[:, :, :], ACT.Copy).then_inc(att_hi, 1)
                hi(l, MIX[10])
                hi(l, MIX[11])
                for t in range(TB):
                    act.wait_ge(gated, at(l, TB, t + 1))
                    for g in range(GROUPS):
                        nc.scalar.activation(nrm[:, t, 4 + 2 * g:6 + 2 * g, :].rearrange("p k c -> p (k c)"),
                                             xs_dec[:, t, 256 * g:256 * g + 256], ACT.Square,
                                             scale=(D_SSM // GROUPS) ** -0.5,
                                             accum_out=gsq[:, t, g:g + 1]).then_inc(g_squared, 1)
                hi(l, MIX[12])
                for t in range(TB):
                    act.wait_ge(ssd_turned, at(l, TB, t + 1))
                    for k in range(4):
                        nc.scalar.activation(nrm[:, t, k, :], bank[:, t, k * P:(k + 1) * P], ACT.Copy,
                                             scale=cur[:, ROW_SSDN + k:ROW_SSDN + k + 1]).then_inc(ssd_full, 1)
                    act.wait_ge(ssd_full, at(l, 4 * TB, 4 * t + 4))
                    nc.scalar.activation(h_hi[:, 0:4, t * P:(t + 1) * P], nrm[:, t, 0:4, :], ACT.Copy)\
                       .then_inc(ssd_hi, 1)

            act.wait_ge(kt_zeroed, 1)
            nc.scalar.activation(zeros_r[:, :], k_t[:, :, :, :].rearrange("p g e q -> p (g e q)")[:, 0:512],
                                 ACT.Copy).then_inc(zeros_ready, 1)
            act.wait_ge(c_turned, 1)
            nc.scalar.activation(c_col[:, :], bank[:, 0, 0:KC], ACT.Silu).then_inc(c_ready, 1)

            with act.Fori(0, DEPTH) as l:
                for f, ff, q0 in FFNS:
                    site = 2 * ff
                    operand(l, site, q0, q0 + 1) if ff == 0 else operand(l, site, middle=q0 + 1)
                    with act.Fori(0, 5) as i:
                        for u in range(2):
                            q, j = q0 + 2 + 3 * u, i * 2 + u
                            hi(l, q, i)
                            silu(l, ff, j, 0)
                            silu(l, ff, j, 1)
                            hi(l, q + 1, i)
                            hid(l, ff, j, q - 1, i)
                            hi(l, q + 2, i)
                    hi(l, q0 + 32)
                    silu(l, ff, FSTEPS - 1, 0)
                    silu(l, ff, FSTEPS - 1, 1)
                    if ff == 0:
                        hi(l, MIX[0])
                    hid(l, ff, FSTEPS - 1, q0 + FFN_PIECES - 2)
                    if ff == 0:
                        hi(l, MIX[1])
                        act.wait_ge(dtw_landed, at(l, 1, 1) * 16)
                        nc.scalar.activation(w_dt_hi[:, :, :], w_dt[:, :, :], ACT.Copy).then_inc(dtw_hi, 1)
                    gate(l, site, 0)
                    y_squares(l, site, 0)
                    y_squares(l, site, 1)
                    if ff == 0:
                        operand(l, 1)
                        mixer(l)
                        hi(l, Q_FFN2)
                        gate(l, 1, 6)
                        y_squares(l, 1, 0)
                        y_squares(l, 1, 1)

        @block.vector
        def _(dve):
            V = nc.vector
            steps = Steps(vec_step, VEC_STEPS)

            def lo(l, q, i=None):
                n = number(q) + 1
                dve.wait_ge(hi_ready, at(l, PIECES, n) + (0 if i is None else i * RING))
                V.tensor_tensor(w_lo[:, q % STAGES], raw[:, q % RING], w_hi[:, q % STAGES], ALU.subtract)\
                 .then_inc(lo_ready, 1)

            def ada_reduce(s, use):
                dve.wait_ge(ada_landed[s], use * 16)
                V.tensor_scalar(ada_acc[:, s, :], ada_raw[:, s, 0, :], c_col[:, 0:1], None, ALU.mult)\
                 .then_inc(ada_step[s], 1)
                for k in range(1, KC):
                    dve.wait_ge(ada_step[s], use * KC + k)
                    V.scalar_tensor_tensor(out=ada_acc[:, s, :], in0=ada_raw[:, s, k, :], scalar=c_col[:, k:k + 1],
                                           in1=ada_acc[:, s, :], op0=ALU.mult, op1=ALU.add).then_inc(ada_step[s], 1)

            def ada_store(pos, r, turned=True):
                wait_apart(dve, ada_summed, pos + (1 - ADA_AHEAD))
                dst = mod[:, bass.ds(r * 2, 2)]
                if turned:
                    ins = V.tensor_reduce(dst, bank[:, 7, 0:ADA_W].rearrange("p (e n) -> p e n", e=2), AX_X, ALU.add)
                else:
                    ins = V.tensor_copy(dst, bank[:, 7, 0:2])
                ins.then_inc(mod_ready, 1)

            def add_bias(l, site, c0, width, k):
                m = mod[:, c0:c0 + width]
                V.tensor_tensor(m, m, cur[:, ROW_ADA + c0:ROW_ADA + c0 + width], ALU.add).then_inc(mod_biased, 1)
                dve.wait_ge(mod_biased, at(l, 2 * SITES, k))

            def scale_col(l, site, mods):
                dve.wait_ge(mod_ready, mods)
                add_bias(l, site, KC * (3 * site + SHIFT), 2 * KC, 2 * site + 1)
                c0 = KC * (3 * site + SCALE)
                V.scalar_tensor_tensor(out=a_col[:, :], in0=mod[:, c0:c0 + KC], scalar=1.0,
                                       in1=cur[:, ROW_PRE[site]:ROW_PRE[site] + KC], op0=ALU.add, op1=ALU.mult)\
                 .then_inc(a_ready, 1)

            def gate_diag(l, site, mods, weight):
                dve.wait_ge(mod_ready, mods)
                c0 = KC * (3 * site + GATE)
                add_bias(l, site, c0, KC, 2 * site + 2)
                V.scalar_tensor_tensor(out=g_col[:, :], in0=mod[:, c0:c0 + KC], scalar=weight,
                                       in1=cur[:, ROW_POST[site]:ROW_POST[site] + KC], op0=ALU.mult, op1=ALU.mult)\
                 .then_inc(gcol_ready, 1)
                dve.wait_ge(gcol_ready, at(l, SITES, site + 1))
                V.tensor_tensor(nrm[:, 0, :, :], ident.unsqueeze(1).broadcast_to([P, KC, P]),
                                g_col[:, :].unsqueeze(2).broadcast_to([P, KC, P]), ALU.mult).then_inc(diag_ready, 1)

            def post(l, site):
                def gated(t):
                    return nrm[:, t, :, :].rearrange("p k c -> p (k c)")

                def times_gate(t, half, signal):
                    n = slice(512 * half, 512 * half + 512)
                    V.tensor_tensor(gated(t)[:, n], bank[:, 2 + 2 * t + half, :], gate_rows[:, n], ALU.mult)\
                     .then_inc(signal, 1)

                def second(t):
                    wait_y(dve, l, site, t)
                    times_gate(t, 1, y_second_gated)

                def first(t):
                    dve.wait_ge(y_first_squared, at(l, SITES * TB, site * TB + t + 1))
                    times_gate(t, 0, y_gated)

                def add(t):
                    k = at(l, SITES * TB, site * TB + t + 1)
                    dve.wait_ge(y_second_gated, k)
                    dve.wait_ge(y_gated, k)
                    dve.wait_ge(y_rstd, k)
                    V.scalar_tensor_tensor(out=x_sb[:, t, :], in0=gated(t), scalar=rstd[:, 0, t:t + 1],
                                           in1=x_sb[:, t, :], op0=ALU.mult, op1=ALU.add).then_inc(x_ready, 1)

                dve.wait_ge(gate_ready, at(l, SITES, site + 1))
                second(0)
                first(0)
                second(1)
                add(0)
                first(1)
                add(1)

            def normalise(l, site, t):
                dve.wait_ge(x_rstd, at(l, SITES * TB, site * TB + t + 1))
                V.tensor_scalar(nrm[:, t, :, :].rearrange("p k c -> p (k c)"), x_sb[:, t, :],
                                rstd[:, 1, t:t + 1], None, ALU.mult).then_inc(xn_ready, 1)

            def h_low(l, site, t, e):
                dve.wait_ge(h_hi_ready, at(l, 4 * SITES, 4 * site + 2 * e + t + 1))
                part = h_hi[:, 4 * e:4 * e + 4, t * P:(t + 1) * P]
                V.tensor_tensor(h_lo[:, 4 * e:4 * e + 4, t * P:(t + 1) * P], nrm[:, t, 4 * e:4 * e + 4, :],
                                part, ALU.subtract).then_inc(h_lo_ready, 1)

            def operand(l, site, first=None, second=None):
                normalise(l, site, 0)
                normalise(l, site, 1)
                if first is not None:
                    lo(l, first)
                for e in range(2):
                    for t in range(TB):
                        h_low(l, site, t, e)
                    if e == 0 and second is not None:
                        lo(l, second)

            def product(l, ff, j):
                for t in range(TB):
                    dve.wait_ge(silu_done, at(l, 4 * FSTEPS, 2 * FSTEPS * ff + t + 1) + j * 2)
                    V.tensor_tensor(prod[:, t], silu_sb[:, t], bank[:, t, FB:2 * FB], ALU.mult).then_inc(prod_done, 1)

            def hid_low(l, ff, j):
                dve.wait_ge(hid_hi_ready, at(l, 2 * FSTEPS, FSTEPS * ff + 1) + j)
                V.tensor_tensor(hid_lo[:, :, :], prod[:, :, :], hid_hi[:, :, :], ALU.subtract).then_inc(hid_lo_ready, 1)
                dve.wait_ge(hid_lo_ready, at(l, 2 * FSTEPS, FSTEPS * ff + 1) + j)

            def take_columns(l):
                V.tensor_copy(cur[:, :], pcol[:, bass.ds(l, 1), :].rearrange("p a n -> p (a n)")).then_inc(cur_ready, 1)
                V.tensor_copy(cur_small[:, :, :], small[:, bass.ds(l, 1), :, :].rearrange("p a b n -> p (a b) n"))\
                 .then_inc(cur_ready, 1)
                dve.wait_ge(cur_ready, at(l, 5, 2))
                sinks = cur_small[:, 3, :].rearrange("p (i e) -> p e i", e=2)
                for e, half in enumerate((EVEN, ODD)):
                    V.tensor_copy(cur_sink[half, :], sinks[half, e, :]).then_inc(cur_ready, 1)
                cb = cur[:, ROWS_A:PCOLS]
                V.tensor_scalar(cb, cb, 0.5, None, ALU.mult).then_inc(cur_ready, 1)
                dve.wait_ge(cur_ready, at(l, 5, 5))

            def mixer(l):
                steps.begin(l)

                def link(ins):
                    steps.link(dve, ins)

                def dt_part():
                    bias = cur_small[:, 0, :].unsqueeze(1).broadcast_to([P, TB, SSM_H])
                    v, mx, ab, ex, one, ln, t6, t7 = (soft[:, n, :] for n in range(8))
                    dve.wait_ge(dt_mm, at(l, 1, 1))
                    V.tensor_tensor(v.rearrange("p (t h) -> p t h", t=TB),
                                    bank[:, 7, DT_AT:DT_AT + TB * SSM_H].rearrange("p (t h) -> p t h", t=TB), bias, ALU.add)\
                     .then_inc(dt_x, 1)
                    dve.wait_ge(dt_x, at(l, 1, 1))
                    V.scalar_tensor_tensor(out=ab, in0=v, scalar=-1.0, in1=v, op0=ALU.mult, op1=ALU.max)\
                     .then_inc(dt_abs, 1)
                    link(V.tensor_scalar(mx, v, 0.0, None, ALU.max))
                    dve.wait_ge(dt_exp, at(l, 1, 1))
                    V.tensor_scalar(one, ex, 1.0, None, ALU.add).then_inc(dt_one, 1)
                    dve.wait_ge(dt_one, at(l, 1, 1))
                    link(V.tensor_scalar(t6, one, -1.0, None, ALU.add))
                    link(V.tensor_tensor(t6, ex, t6, ALU.subtract))
                    link(V.reciprocal(t7, one))
                    link(V.tensor_tensor(t6, t6, t7, ALU.mult))
                    link(V.tensor_tensor(t6, t6, mx, ALU.add))
                    dve.wait_ge(dt_ln, at(l, 1, 1))
                    link(V.tensor_tensor(dt_sb[:, :, :].rearrange("p t h -> p (t h)"), ln, t6, ALU.add))
                    dve.wait_ge(exp_a_ready, at(l, 1, 1))
                    V.scalar_tensor_tensor(out=adt[:, :, :], in0=dt_sb[:, :, :], scalar=-1.0,
                                           in1=exp_a[:, :].unsqueeze(1).broadcast_to([P, TB, SSM_H]),
                                           op0=ALU.mult, op1=ALU.mult).then_inc(adt_ready, 1)

                def rope(src, t, heads, outs, signal):
                    v = src.rearrange("p (h d) -> p h d", d=HEAD)
                    cos = const[:, C_COS + t * HEAD:C_COS + (t + 1) * HEAD].unsqueeze(1)
                    sin = const[:, C_SIN + t * HEAD:C_SIN + (t + 1) * HEAD].unsqueeze(1)
                    c_part, s_part = rope_t[:, 0, 0:heads, :], rope_t[:, 1, 0:heads, :]
                    steps.mark(V.tensor_tensor(c_part, v, cos.broadcast_to([P, heads, HEAD]), ALU.mult))
                    for lo_, hi_ in ((0, 32), (32, 0)):
                        steps.mark(V.tensor_tensor(s_part[:, :, lo_:lo_ + 32], v[:, :, hi_:hi_ + 32],
                                                   sin[:, :, lo_:lo_ + 32].broadcast_to([P, heads, 32]), ALU.mult))
                    steps.settle(dve)
                    for dst in outs:
                        ins = V.tensor_tensor(dst, c_part, s_part, ALU.add)
                        ins.then_inc(signal, 1)
                    return ins

                def conv_part(ct):
                    src = bank[:, ct % 4, 0:T]
                    w = [cur[:, ROWS_A + ROW_CONVW + 8 * tap + ct:ROWS_A + ROW_CONVW + 8 * tap + ct + 1]
                         for tap in range(CONV_W)]
                    dve.wait_ge(conv_begun, at(l, 8, ct + 1))
                    for back in range(1, CONV_W):
                        ins = V.scalar_tensor_tensor(out=conv[:, ct, back:T], in0=src[:, 0:T - back],
                                                     scalar=w[CONV_W - 1 - back], in1=conv[:, ct, back:T],
                                                     op0=ALU.mult, op1=ALU.add)
                        if back < CONV_W - 1:
                            link(ins)
                        else:
                            ins.then_inc(conv_ready, 1)

                def soft_max(c):
                    dve.wait_ge(scores, at(l, 4, c + 1))
                    link(V.tensor_reduce(sm[:, c, 0, :], bank[:, 4 + c % 2, :].rearrange("p (i k) -> p i k", i=4)
                                         [:, :, 0:KEYS[c]], AX_X, ALU.max))
                    link(V.scalar_tensor_tensor(out=sm[:, c, 0, :], in0=sm[:, c, 0, :], scalar=ATT_SCALE,
                                                in1=cur_sink[:, :], op0=ALU.mult, op1=ALU.max))
                    link(V.tensor_tensor(sm[:, c, 1, :], cur_sink[:, :], sm[:, c, 0, :], ALU.subtract))
                    V.tensor_scalar(sm[:, c, 2, :], sm[:, c, 0, :], -1.0, None, ALU.mult).then_inc(row_max, 1)

                def soft_divide(c):
                    dve.wait_ge(exps, at(l, 16, 4 * c + 4))
                    dve.wait_ge(sink_exp, at(l, 4, c + 1))
                    link(V.tensor_tensor(sm[:, c, 5, :], sm[:, c, 3, :], sm[:, c, 4, :], ALU.add))
                    link(V.reciprocal(sm[:, c, 5, :], sm[:, c, 5, :]))
                    p = probs[:, c % 2, :, 0:KEYS[c]]
                    V.tensor_tensor(p, p, sm[:, c, 5, :].unsqueeze(2).broadcast_to([P, 4, KEYS[c]]), ALU.mult)\
                     .then_inc(probs_ready, 1)

                def by_head(col):
                    return col.unsqueeze(2).broadcast_to([col.shape[0], SSM_H, HEAD])

                def heads_of(ap):
                    return ap.rearrange("p (h d) -> p h d", d=HEAD)

                def conditioning_store(u):
                    p = ADA_AHEAD + ADA_LOOP1 + u
                    ada_store(l * ADA_PIECES + p, p, turned=False)

                conditioning_store(0)
                lo(l, MIX[2])
                lo(l, MIX[3])
                for t in range(TB):
                    wait_block(dve, q_mm, l, t, MIX[1])
                    if t:
                        dve.wait_ge(q_roped, at(l, TB, t))
                    rope(bank[:, 4 + t, :], t, ATT_H, [q_rot[:, t]], q_roped)
                dt_part()
                lo(l, MIX[4])
                for t in range(TB):
                    dve.wait_ge(v_ready, at(l, TB + 2, TB))
                    if t == 0:
                        dve.wait_ge(q_roped, at(l, TB, TB))
                    else:
                        dve.wait_ge(k_roped, at(l, 2 * TB, 2 * t))
                    rope(bank[:, 6, 256 * t:256 * t + 128], t, KV_H, [k_rot[:, t, :, n, :] for n in range(2)], k_roped)
                conditioning_store(1)
                conditioning_store(2)
                conv_part(0)
                conv_part(1)
                conditioning_store(3)
                lo(l, MIX[5])
                lo(l, MIX[6])
                soft_max(0)
                soft_max(1)
                conv_part(2)
                conv_part(3)
                soft_divide(0)
                soft_divide(1)
                conv_part(4)
                conv_part(5)
                lo(l, MIX[7])
                soft_max(2)
                soft_max(3)
                conv_part(6)
                conv_part(7)
                soft_divide(2)
                soft_divide(3)
                lo(l, MIX[8])
                for t in range(TB):
                    V.tensor_tensor(nrm[:, t, :, :], upto.unsqueeze(1).broadcast_to([P, SSM_H, P]),
                                    adt[:, t, :].unsqueeze(2).broadcast_to([P, SSM_H, P]), ALU.mult)\
                     .then_inc(seg_in_ready, 1)
                lo(l, MIX[9])

                def z_part(t):
                    dve.wait_ge(z_tanhed, at(l, TB, t + 1))
                    V.scalar_tensor_tensor(out=z_silu[:, t, :], in0=z_tanh, scalar=1.0, in1=bank[:, t, :],
                                           op0=ALU.add, op1=ALU.mult).then_inc(z_ready, 1)

                def mix_part(t):
                    dve.wait_ge(seg_exp, at(l, 2 * TB, 2 * t + 2))
                    for g in range(GROUPS):
                        m = decay_l[:, t, 4 * g:4 * g + 4, :]
                        V.tensor_tensor(m, m, gram[:, 2 * t + g, :].unsqueeze(1).broadcast_to([P, 4, P]), ALU.mult)\
                         .then_inc(mix_ready, 1)

                dve.wait_ge(gram_mm, at(l, 1, 1))
                V.tensor_tensor(gram[:, :, :], bank[:, 5, :].rearrange("p (b l) -> p b l", b=4),
                                upto.unsqueeze(1).broadcast_to([P, 4, P]), ALU.mult).then_inc(gram_ready, 1)
                dve.wait_ge(gram_ready, at(l, 1, 1))
                mix_part(0)
                mix_part(1)
                z_part(0)
                dve.wait_ge(state_mm, at(l, 3, 1))
                V.tensor_copy(state[:, 0, :], bank[:, 2, :]).then_inc(state_ready, 1)
                z_part(1)
                for c in (1, 2):
                    dve.wait_ge(state_ready, at(l, 3, c))
                    link(V.tensor_tensor(heads_of(state[:, c, :]), heads_of(state[:, c - 1, :]),
                                         by_head(decays[:, c // 2, 2 + c % 2, :]), ALU.mult))
                    dve.wait_ge(state_mm, at(l, 3, c + 1))
                    V.tensor_tensor(state[:, c, :], state[:, c, :], bank[:, 2 + c, :], ALU.add)\
                     .then_inc(state_ready, 1)
                dve.wait_ge(att_hi, at(l, 1, 1))
                V.tensor_tensor(h_lo[:, 4:8, :], att[:, :, :], h_hi[:, 4:8, :], ALU.subtract).then_inc(att_lo, 1)
                lo(l, MIX[10])
                for t in range(TB):
                    y = xs_dec[:, t, :]
                    tmp = nrm[:, t, 0:4, :].rearrange("p k c -> p (k c)")
                    r = ODD if t == 0 else slice(0, P)
                    dve.wait_ge(skip_ready, at(l, TB, t + 1))
                    dve.wait_ge(diag_mm, at(l, TB, t + 1))
                    link(V.tensor_tensor(y, skip_of(t), bank[:, t, :], ALU.add))
                    dve.wait_ge(off_mm, at(l, TB, t + 1))
                    link(V.tensor_tensor(heads_of(tmp[r]), heads_of(bank[r, 6 + t, :]), by_head(decays[r, t, 1, :]),
                                         ALU.mult))
                    link(V.tensor_tensor(y[r], y[r], tmp[r], ALU.add))
                    V.scalar_tensor_tensor(out=y, in0=y, scalar=0.5, in1=z_silu[:, t, :], op0=ALU.mult,
                                           op1=ALU.mult).then_inc(gated, 1)
                for t in range(TB):
                    dve.wait_ge(g_rstd, at(l, TB, t + 1))
                    for g in range(GROUPS):
                        y = xs_dec[:, t, 256 * g:256 * g + 256]
                        V.tensor_scalar(y, y, grstd[:, t, g:g + 1], None, ALU.mult).then_inc(ssd_ready, 1)
                lo(l, MIX[11])
                for t in range(TB):
                    dve.wait_ge(ssd_hi, at(l, TB, t + 1))
                    V.tensor_tensor(h_lo[:, 0:4, t * P:(t + 1) * P], nrm[:, t, 0:4, :],
                                    h_hi[:, 0:4, t * P:(t + 1) * P], ALU.subtract).then_inc(ssd_lo, 1)
                lo(l, MIX[12])
                steps.end()

            dve.sem_inc(lo_ready, RING)
            for s in range(ADA_RING):
                dve.sem_inc(ada_step[s], KC * FIRST_USE)
            dve.wait_ge(const_landed, 16)
            dve.wait_ge(c_ready, 1)
            for r in range(ADA_AHEAD):
                src, acc = first_raw[r % FIRST_RING], ada_acc[:, r % ADA_RING, :]
                dve.wait_ge(first_landed[r % FIRST_RING], 16 * (r // FIRST_RING + 1))
                if r >= ADA_RING:
                    dve.wait_ge(first_summed, r - ADA_RING + 1)
                V.tensor_scalar(acc, src[:, 0, :], c_col[:, 0:1], None, ALU.mult).then_inc(first_step, 1)
                for k in range(1, FIRST_VEC):
                    dve.wait_ge(first_step, r * FIRST_VEC + k)
                    V.scalar_tensor_tensor(out=acc, in0=src[:, k, :], scalar=c_col[:, k:k + 1], in1=acc,
                                           op0=ALU.mult, op1=ALU.add).then_inc(first_step, 1)
            dve.wait_ge(params_turned, 1)
            V.tensor_copy(pcol[:, :, 0:ROWS_A], bank[:, 1, 0:DEPTH * ROWS_A].rearrange("p (l n) -> p l n", l=DEPTH))\
             .then_inc(pcol_ready, 1)
            V.tensor_copy(pcol[:, :, ROWS_A:PCOLS], bank[:, 2, 0:DEPTH * ROWS_B].rearrange("p (l n) -> p l n", l=DEPTH))\
             .then_inc(pcol_ready, 1)
            dve.wait_ge(pcol_ready, 2)
            dve.wait_ge(first_summed, ADA_AHEAD)
            n = 2 * ADA_AHEAD
            V.tensor_copy(mod[:, 0:n], bank[:, 7, 0:n]).then_inc(mod_ready, ADA_AHEAD)
            dve.wait_ge(small_landed, 16 * 4 * DEPTH)

            with dve.Fori(0, DEPTH) as l:
                ada0 = l * ADA_PIECES + ADA_AHEAD
                take_columns(l)
                for f, ff, q0 in FFNS:
                    site = 2 * ff
                    scale_col(l, site, ada0 if ff == 0 else ada0 + (ADA_LOOP1 + ADA_EPI))
                    operand(l, site, None if ff else q0, q0 + 1)
                    lo(l, q0 + 2)
                    if ff:
                        for u in range(ADA_PRO):
                            p = ADA_LOOP1 + ADA_EPI + u
                            ada_store(ada0 + p, ADA_AHEAD + p)
                    with dve.Fori(0, 5) as i:
                        for u in range(2):
                            q, j = q0 + 2 + 3 * u, i * 2 + u
                            product(l, ff, j)
                            if ff == 0:
                                p, r = i * 4 + (ada0 + 2 * u), i * 4 + (ADA_AHEAD + 2 * u)
                                use = i * 2 + ada_use(l, 2 * u)
                                if u:
                                    ada_store(p - 1, r - 1)
                                lo(l, q + 1, i)
                                ada_reduce(0, use)
                                hid_low(l, ff, j)
                                lo(l, q + 2, i)
                                ada_store(p, r)
                                if u:
                                    ada_store(p + 1, r + 1)
                                lo(l, q + 3, i)
                            else:
                                p, use = i * 2 + (ada0 + (ADA_LOOP2 + u)), i + ada_use(l, ADA_LOOP2)
                                r = (i * 2 + (ADA_AHEAD + ADA_LOOP2 + u)) % ADA_PIECES
                                lo(l, q + 1, i)
                                ada_reduce(u, use)
                                hid_low(l, ff, j)
                                lo(l, q + 2, i)
                                ada_store(p, r)
                                lo(l, q + 3, i)
                    gate_diag(l, site, ada0 + (ADA_LOOP1 if ff == 0 else ADA_PIECES - ADA_AHEAD), 0.5)
                    product(l, ff, FSTEPS - 1)
                    if ff == 0:
                        lo(l, MIX[0])
                    hid_low(l, ff, FSTEPS - 1)
                    if ff == 0:
                        lo(l, MIX[1])
                        dve.wait_ge(dtw_hi, at(l, 1, 1))
                        V.tensor_tensor(w_dt_lo[:, :, :], w_dt[:, :, :], w_dt_hi[:, :, :], ALU.subtract)\
                         .then_inc(dtw_lo, 1)
                    if ff == 0:
                        scale_col(l, 1, ada0 + ADA_LOOP1)
                    post(l, site)
                    if ff == 0:
                        operand(l, 1)
                        mixer(l)
                        gate_diag(l, 1, ada0 + (ADA_LOOP1 + ADA_EPI), 1.0)
                        lo(l, Q_FFN2)
                        post(l, 1)

        @block.tensor
        def _(pe):
            MM = nc.tensor.matmul

            def split(dst, xs, ys, start=False, stop=False):
                first = MM(dst, xs[0], ys[0], start=start, stop=False)
                MM(dst, xs[0], ys[1], start=False, stop=False)
                return first, MM(dst, xs[1], ys[0], start=False, stop=stop)

            def weights(l, q, i=None):
                pe.wait_ge(lo_ready, at(l, PIECES, RING + number(q) + 1) + (0 if i is None else i * RING))

            def stage(q, pattern, **sizes):
                return [w[:, q % STAGES, :].rearrange(pattern, **sizes) for w in (w_hi, w_lo)]

            def h_cols(k, t):
                return h_hi[:, k, t * P:(t + 1) * P], h_lo[:, k, t * P:(t + 1) * P]

            def hid_cols(c, t):
                return hid_hi[:, c, t * P:(t + 1) * P], hid_lo[:, c, t * P:(t + 1) * P]

            def h_parts(l, site, t, e):
                pe.wait_ge(h_lo_ready, at(l, 4 * SITES, 4 * site + 2 * e + t + 1))

            def gu_piece(l, ff, q, half, j=None, i=None, between=None):
                weights(l, q, i)
                wh, wl = stage(q, "p (g k n) -> p g k n", g=2, k=4)
                if i is None:
                    for t in range(TB):
                        h_parts(l, 2 * ff, t, half)
                for e in range(2):
                    if i is not None and half == 0:
                        pe.wait_ge(prod_done, at(l, 4 * FSTEPS, 2 * FSTEPS * ff + e - 1) + j * 2)
                    cols = slice(e * P, (e + 1) * P)
                    for g in range(2):
                        for k in range(4):
                            _, mm = split(bank[:, e, g * T:(g + 1) * T], (wh[:, g, k, cols], wl[:, g, k, cols]),
                                          (h_hi[:, 4 * half + k, :], h_lo[:, 4 * half + k, :]),
                                          start=(half == 0 and (g, k) == (0, 0)), stop=(half == 1 and (g, k) == (1, 3)))
                    if half == 1:
                        mm.then_inc(gu_done, 1)
                    if e == 0 and between is not None:
                        between()
                if half == 0:
                    mm.then_inc(stage_used, 1)

            def rows_piece(q, cols, start=False, stop=False, frees=False, done=None, parts=None):
                wh, wl = stage(q, "p (c n) -> p c n", c=2)
                for t in range(TB):
                    if parts is not None:
                        parts(t)
                    for half in range(2):
                        n = slice(512 * half, 512 * half + 512)
                        for c in range(2):
                            first, mm = split(bank[:, 2 + 2 * t + half, :], cols(c, t), (wh[:, c, n], wl[:, c, n]),
                                              start=(start and c == 0), stop=(stop and c == 1))
                            if frees and (t, half, c) == (0, 0, 0):
                                first.then_inc(stage_used, 1)
                    if done is not None and t == 0:
                        mm.then_inc(done, 1)
                mm.then_inc(stage_used, 1)

            def open_y():
                for b in range(2, 6):
                    mm = MM(bank[:, b, :], zeros_r[:, 0:P], zeros_r[:, :], start=True, stop=False)
                    if b == 2:
                        mm.then_inc(stage_used, 1)

            def ada(pos, s, use, turned=True):
                pe.wait_ge(ada_step[s], (use + 1) * KC)
                pe.wait_ge(mod_ready, pos)
                for e in range(2):
                    cols = ada_acc[:, s, e * P:(e + 1) * P]
                    if turned:
                        mm = nc.tensor.transpose(bank[:, 7, e * P:(e + 1) * P], cols, ident)
                    else:
                        mm = MM(bank[:, 7, e:e + 1], cols, ones[:, 0:1], start=True, stop=True)
                mm.then_inc(ada_summed, 1)

            def turn_rows(l, site):
                for t in range(TB):
                    pe.wait_ge(xn_ready, at(l, SITES * TB, site * TB + t + 1))
                    for e in range(2):
                        for k in range(4):
                            mm = nc.tensor.transpose(bank[:, turned_bank(site, t, e), k * P:(k + 1) * P], nrm[:, t, 4 * e + k, :],
                                                     ident)
                        mm.then_inc(xn_turned, 1)

            def spread_gate(l, site, b):
                pe.wait_ge(diag_ready, at(l, SITES, site + 1))
                for e in range(2):
                    mm = MM(bank[:, b + e, :], ones, nrm[:, 0, 4 * e:4 * e + 4, :], start=True, stop=True)
                mm.then_inc(gate_spread, 1)

            def mixer(l):

                def wide(m, kh, b, signal):
                    weights(l, MIX[m])
                    wh, wl = stage(MIX[m], "p (k n) -> p k n", k=4)
                    for t in range(TB):
                        if m < 2:
                            h_parts(l, 1, t, kh)
                        for k in range(4):
                            _, mm = split(bank[:, b + t, :], h_cols(4 * kh + k, t), (wh[:, k, :], wl[:, k, :]),
                                          start=(kh == 0 and k == 0), stop=(kh == 1 and k == 3))
                        if kh == 1 and t == 0:
                            mm.then_inc(signal, 1)
                    mm.then_inc(stage_used, 1)

                def xbc(m):
                    weights(l, MIX[3 + m])
                    wh, wl = stage(MIX[3 + m], "p (k n) -> p k n", k=KC)
                    for e in range(2):
                        for k in range(KC):
                            cols = slice(e * P, (e + 1) * P)
                            _, mm = split(bank[:, (2 * m + e) % 4, 0:T], (wh[:, k, cols], wl[:, k, cols]),
                                          (h_hi[:, k, :], h_lo[:, k, :]), start=(k == 0), stop=(k == KC - 1))
                        mm.then_inc(stage_used if e else xbc_mm, 1)

                def score(c):
                    for i in range(4):
                        for e in range(2):
                            o = i * P
                            for k0, n in WINDOWS[c]:
                                mm = MM(bank[64 * e:64 * e + 64, 4 + c % 2, o:o + n], q_t[:, i, 64 * c:64 * c + 64],
                                        k_t[:, i // 2, e, k0:k0 + n], start=True, stop=True)
                                o += n
                    mm.then_inc(scores, 1)

                def turn_probs(c):
                    wait_apart(pe, probs_ready, at(l, 4, c + 1))
                    for i in range(4):
                        mm = nc.tensor.transpose(bank[0:KEYS[c], 6 + c % 2, i * P:(i + 1) * P],
                                                 probs[:, c % 2, i, 0:KEYS[c]], ident)
                    mm.then_inc(probs_turned, 1)

                def attend(c):
                    wait_apart(pe, probs_t_ready, at(l, 4, c + 1))
                    n = KEYS[c]
                    for i in range(4):
                        for e in range(2):
                            mm = MM(bank[64 * e:64 * e + 64, 4 + c % 2, 64 * i:64 * i + 64],
                                    v_sb[0:n, V_OF[c], 64 * (i // 2):64 * (i // 2) + 64],
                                    probs_t[0:n, c % 2, i, 64 * e:64 * e + 64], start=True, stop=True)
                    mm.then_inc(att_mm, 1)

                def conditioning(u):
                    ada(l * ADA_PIECES + (ADA_AHEAD + ADA_LOOP1 + u), u % ADA_RING, ada_use(l, ADA_LOOP1 + u),
                        turned=False)

                wide(0, 0, 4, None)
                conditioning(0)
                for e in range(2):
                    for t in range(TB):
                        h_parts(l, 1, t, e)
                pe.wait_ge(dtw_lo, at(l, 1, 1))
                pe.wait_ge(mod_ready, l * ADA_PIECES + (ADA_AHEAD + ADA_LOOP1 + 1))
                for k in range(KC):
                    _, mm = split(bank[0:SSM_H, 7, T:2 * T], (w_dt_hi[:, k, :], w_dt_lo[:, k, :]),
                                  (h_hi[:, k, :], h_lo[:, k, :]), start=(k == 0), stop=(k == KC - 1))
                mm.then_inc(dt_heads, 1)
                wide(1, 1, 4, q_mm)
                wait_apart(pe, dt_row_ready, at(l, 1, 1))
                for t in range(TB):
                    o = DT_AT + t * SSM_H
                    mm = nc.tensor.transpose(bank[:, 7, o:o + SSM_H], dt_row[:, t * P:(t + 1) * P],
                                             ident[0:SSM_H, 0:SSM_H])
                mm.then_inc(dt_mm, 1)
                weights(l, MIX[2])
                wh, wl = stage(MIX[2], "p (k n) -> p k n", k=KC)
                for t in range(TB):
                    for k in range(KC):
                        _, mm = split(bank[:, 6, 256 * t:256 * t + 256], h_cols(k, t), (wh[:, k, :], wl[:, k, :]),
                                      start=(k == 0), stop=(k == KC - 1))
                mm.then_inc(stage_used, 1)
                pe.wait_ge(dt_x, at(l, 1, 1))
                conditioning(1)
                xbc(0)
                pe.wait_ge(mod_ready, l * ADA_PIECES + (ADA_AHEAD + ADA_LOOP1 + 2))
                pe.wait_ge(adt_ready, at(l, 1, 1))
                for t in range(TB):
                    for n, c0 in enumerate((C_AFTER, C_UPTO, C_FIRST, C_SECOND)):
                        o = DECAY_AT + (4 * t + n) * SSM_H
                        mm = MM(bank[:, 7, o:o + SSM_H], const[:, c0:c0 + P], adt[:, t, :], start=True, stop=True)
                mm.then_inc(decay_sums, 1)
                for t in range(TB):
                    pe.wait_ge(q_roped, at(l, TB, t + 1))
                    for i in range(4):
                        mm = nc.tensor.transpose(bank[:, 4 + t, i * P:(i + 1) * P],
                                                 q_rot[:, t, 2 * i:2 * i + 2, :].rearrange("p h d -> p (h d)"), ident)
                    mm.then_inc(q_turned, 1)
                pe.wait_ge(k_roped, at(l, 2 * TB, 2 * TB))
                for g in range(KV_H):
                    for t in range(TB):
                        mm = nc.tensor.transpose(bank[:, 6, g * T + t * P:g * T + (t + 1) * P],
                                                 k_rot[:, t, g, :, :].rearrange("p a d -> p (a d)"), ident)
                mm.then_inc(k_turned, 1)
                pe.wait_ge(decays_ready, at(l, 1, 1))
                conditioning(2)
                xbc(1)
                conditioning(3)
                pe.wait_ge(mod_ready, l * ADA_PIECES + (ADA_AHEAD + ADA_LOOP1 + ADA_EPI))
                pe.wait_ge(q_t_ready, at(l, TB, TB))
                pe.wait_ge(k_t_ready, at(l, 2, 2))
                score(0)
                score(1)
                pe.wait_ge(conv_ready, at(l, 8, 2))
                xbc(2)
                pe.wait_ge(conv_ready, at(l, 8, 4))
                xbc(3)
                for c in (0, 1):
                    turn_probs(c)
                attend(0)
                attend(1)
                for c in (2, 3):
                    pe.wait_ge(att_ready, at(l, 4, c - 1))
                    score(c)
                pe.wait_ge(conv_ready, at(l, 8, 6))
                wide(7, 0, 0, None)
                for c in (2, 3):
                    turn_probs(c)
                attend(2)
                attend(3)
                pe.wait_ge(xbc_ready, at(l, 8, 8))
                pe.wait_ge(conv_ready, at(l, 8, 8))
                for t in range(TB):
                    for k in range(4):
                        mm = nc.tensor.transpose(bank[:, 2 + t, k * P:(k + 1) * P], conv[:, k, t * P:(t + 1) * P],
                                                 ident)
                    mm.then_inc(xs_turned, 1)
                def log_decays(t):
                    pe.wait_ge(seg_in_ready, at(l, TB, t + 1))
                    for hh in range(2):
                        if t:
                            pe.wait_ge(seg_exp, at(l, 2 * TB, hh + 1))
                        MM(bank[:, 6 + hh, :], after, nrm[:, t, 4 * hh:4 * hh + 4, :], start=True, stop=True)\
                            .then_inc(seg_mm, 1)

                pe.wait_ge(probs_t_ready, at(l, 4, 4))
                log_decays(0)
                pe.wait_ge(att_ready, at(l, 4, 4))
                for t in range(TB):
                    for g in range(GROUPS):
                        o = (t * GROUPS + g) * P
                        mm = nc.tensor.transpose(bank[:, 4, o:o + P], conv[:, 4 + g, t * P:(t + 1) * P], ident)
                mm.then_inc(b_turned, 1)
                for t in range(TB):
                    for g in range(GROUPS):
                        o = (t * GROUPS + g) * P
                        rows = slice(t * P, (t + 1) * P)
                        mm = MM(bank[:, 5, o:o + P], conv[:, 4 + g, rows], conv[:, 6 + g, rows], start=True, stop=True)
                mm.then_inc(gram_mm, 1)
                log_decays(1)

                wide(8, 1, 0, z_mm)
                pe.wait_ge(xs_ready, at(l, TB, TB))
                pe.wait_ge(b_ready, at(l, 1, 1))
                for c in range(3):
                    pe.wait_ge(xs_dec_ready, at(l, TB, c // 2 + 1))
                    half = ODD if c % 2 else EVEN
                    for g in range(GROUPS):
                        mm = MM(bank[:, 2 + c, 256 * g:256 * g + 256], b_nat[half, c // 2, P * g:P * g + P],
                                xs_dec[half, c // 2, 256 * g:256 * g + 256], start=True, stop=True)
                    mm.then_inc(state_mm, 1)
                for t in range(TB):
                    pe.wait_ge(mix_ready, at(l, 2 * TB, 2 * t + 2))
                    pe.wait_ge(z_ready, at(l, TB, t + 1))
                    for h in range(SSM_H):
                        mm = MM(bank[:, t, 64 * h:64 * h + 64], decay_l[:, t, h, :], xs_dt[:, t, 64 * h:64 * h + 64],
                                start=True, stop=True)
                    mm.then_inc(diag_mm, 1)
                pe.wait_ge(seg_exp, at(l, 2 * TB, 2 * TB))
                for c in range(1, 4):
                    pe.wait_ge(state_ready, at(l, 3, c))
                    for g in range(GROUPS):
                        mm = MM(bank[ODD if c % 2 else EVEN, 6 + c // 2, 256 * g:256 * g + 256],
                                conv[:, 6 + g, 64 * c:64 * c + 64], state[:, c - 1, 256 * g:256 * g + 256],
                                start=True, stop=True)
                    if c != 2:
                        mm.then_inc(off_mm, 1)
                def out_piece(n, k0, **flags):
                    weights(l, MIX[9 + n])
                    rows_piece(MIX[9 + n], lambda c, t: h_cols(k0 + c, t), **flags)

                pe.wait_ge(att_lo, at(l, 1, 1))
                pe.wait_ge(gram_ready, at(l, 1, 1))
                out_piece(0, 4, start=True)
                out_piece(1, 6)
                for t in range(TB):
                    pe.wait_ge(ssd_ready, at(l, 2 * TB, 2 * t + 2))
                    for k in range(4):
                        mm = nc.tensor.transpose(bank[:, t, k * P:(k + 1) * P], xs_dec[:, t, k * P:(k + 1) * P], ident)
                    mm.then_inc(ssd_turned, 1)
                out_piece(2, 0, parts=lambda t: pe.wait_ge(ssd_lo, at(l, TB, t + 1)))
                spread_gate(l, 1, 6)
                out_piece(3, 2, stop=True, done=y_done)

            pe.sem_inc(stage_used, STAGES)
            pe.wait_ge(const_landed, 16)
            pe.wait_ge(c_landed, 16)
            nc.tensor.transpose(bank[:, 0, 0:KC], c_row[:, :], ident[0:KC, 0:KC]).then_inc(c_turned, 1)
            pe.wait_ge(c_ready, 1)
            for r in range(ADA_AHEAD):
                pe.wait_ge(first_landed[r % FIRST_RING], 16 * (r // FIRST_RING + 1))
                for e in range(2):
                    dst, cols = bank[:, 7, 2 * r + e:2 * r + e + 1], slice(e * P, (e + 1) * P)
                    for k in range(FIRST_VEC, KC):
                        MM(dst, first_raw[r % FIRST_RING][:, k, cols], c_col[:, k:k + 1], start=(k == FIRST_VEC),
                           stop=False)
                    if e == 0:
                        pe.wait_ge(first_step, FIRST_VEC * (r + 1))
                    mm = MM(dst, ada_acc[:, r % ADA_RING, cols], ones[:, 0:1], start=False, stop=True)
                mm.then_inc(first_summed, 1)
            pe.wait_ge(rows_landed, 16 * (10 * DEPTH))
            for l in range(DEPTH):
                nc.tensor.transpose(bank[:, 1, l * ROWS_A:(l + 1) * ROWS_A], prow_a[:, l, :], ident[0:ROWS_A, 0:ROWS_A])
                mm = nc.tensor.transpose(bank[:, 2, l * ROWS_B:(l + 1) * ROWS_B], prow_b[:, l, :],
                                         ident[0:ROWS_B, 0:ROWS_B])
            mm.then_inc(params_turned, 1)
            pe.wait_ge(zeros_ready, 1)
            pe.wait_ge(kt_zeroed, 1)

            with pe.Fori(0, DEPTH) as l:
                ada0 = l * ADA_PIECES + ADA_AHEAD
                for f, ff, q0 in FFNS:
                    site = 2 * ff
                    turn_rows(l, site)
                    gu_piece(l, ff, q0, 0)
                    gu_piece(l, ff, q0 + 1, 1)
                    open_y()
                    if ff:
                        for u in range(ADA_PRO):
                            ada(ada0 + (ADA_LOOP1 + ADA_EPI + u), u, ada_use(l, ADA_LOOP1 + ADA_EPI + u))
                    with pe.Fori(0, 5) as i:
                        for u in range(2):
                            q, j = q0 + 2 + 3 * u, i * 2 + (u + 1)
                            if ff == 0:
                                between = lambda: ada(i * 4 + (ada0 + 2 * u), 0, i * 2 + ada_use(l, 2 * u))
                            else:
                                between = lambda: ada(i * 2 + (ada0 + (ADA_LOOP2 + u)), u, i + ada_use(l, ADA_LOOP2))
                            gu_piece(l, ff, q, 0, j, i)
                            gu_piece(l, ff, q + 1, 1, j, i, between)
                            if ff == 0:
                                ada(i * 4 + (ada0 + (2 * u + 1)), 1, i * 2 + ada_use(l, 2 * u))
                            weights(l, q + 2, i)
                            pe.wait_ge(hid_lo_ready, at(l, 2 * FSTEPS, FSTEPS * ff) + j)
                            rows_piece(q + 2, hid_cols, frees=True)
                    pe.wait_ge(prod_done, at(l, 4 * FSTEPS, 2 * FSTEPS * (ff + 1)))
                    spread_gate(l, site, 0)
                    weights(l, q0 + 32)
                    pe.wait_ge(hid_lo_ready, at(l, 2 * FSTEPS, FSTEPS * (ff + 1)))
                    rows_piece(q0 + 32, hid_cols, stop=True, done=y_done)
                    if ff == 0:
                        turn_rows(l, 1)
                        mixer(l)


INPUTS = ["x", "c", "ada_w", "ada_b", "ffn1_norm_pre", "ffn1_w_gate", "ffn1_w_up", "ffn1_w_down", "ffn1_norm_post",
          "mix_norm_pre", "w_in", "conv_w", "conv_b", "dt_bias", "a_log", "d_skip", "ssd_norm", "attn_sinks", "w_out",
          "mix_norm_post", "ffn2_norm_pre", "ffn2_w_gate", "ffn2_w_up", "ffn2_w_down", "ffn2_norm_post"]


def kernel(**inputs):
    import concourse.bacc as bacc
    from concourse.bass_utils import run_bass_kernel_spmd

    nc = bacc.Bacc("TRN2", target_bir_lowering=False, num_devices=1, dynamic_dma_scratch_size=1024)
    arrays, aps = {}, {}
    for name in INPUTS:
        arrays[name] = np.ascontiguousarray(inputs[name])
    arrays["const"] = constants()
    for name, v in arrays.items():
        aps[name] = nc.dram_tensor("in_" + name, v.shape, mybir.dt.from_np(v.dtype), kind="ExternalInput").ap()
    out = nc.dram_tensor("out_x", (1, T, D), F32, kind="ExternalOutput").ap()
    trunk(nc, aps, out)
    r = run_bass_kernel_spmd(nc, [{"in_" + name: v for name, v in arrays.items()}], core_ids=[0])
    return r.results[0]["out_x"]
```
